# Optimizing a Trainium2 kernel written in Bass

```python
import math
import jax, jax.numpy as jnp
from jax import lax
import numpy as np

D_MODEL = 1024
BATCH = 1
SEQ = 2048
DEPTH = 1

N_MEM = 256
EPS = 1e-6
NEG = -1e30
F_MIN = 1e-12
ATT_HEADS = 8
ATT_HEAD_DIM = 64
ATT_W = ATT_HEADS * ATT_HEAD_DIM
DILATED_PATTERNS = ((128, 1), (512, 4), (2048, 16))
BLK = 128
HG_HEADS = 4
HG_HEAD_DIM = 128
HG_W = HG_HEADS * HG_HEAD_DIM
HG_CHUNK = 32
MIX_W = ATT_W + HG_W
IN_W = 3 * ATT_W + 4 * HG_W
MEM_HEADS = 4
MEM_HEAD_DIM = D_MODEL // MEM_HEADS
D_FF = 4 * D_MODEL

kernel_name = "hybrid_dilated_attn_hgrn2_block"

def rms_norm(x, g):
    xf = x.astype(jnp.float32)
    y = xf * lax.rsqrt(jnp.mean(xf * xf, axis=-1, keepdims=True) + EPS)
    return (y * g.astype(jnp.float32)).astype(x.dtype)

def dilated_branch(q, k, v, window, dilation, slopes):
    B_, S_, H_, E_ = q.shape
    steps = window // dilation
    L = S_ // dilation
    nb = -(-L // BLK)
    Lp = nb * BLK

    def split(t):
        t = t.reshape(B_, L, dilation, H_, E_).transpose(0, 2, 3, 1, 4)
        t = jnp.pad(t, ((0, 0), (0, 0), (0, 0), (0, Lp - L), (0, 0)))
        return t.reshape(B_, dilation, H_, nb, BLK, E_)

    def with_prev(t):
        prev = jnp.pad(t, ((0, 0), (0, 0), (0, 0), (1, 0), (0, 0), (0, 0)))[:, :, :, :-1]
        return jnp.concatenate([prev, t], axis=-2)

    qb = split(q)
    kx = with_prev(split(k))
    vx = with_prev(split(v))
    s = jnp.einsum('bdhnqe,bdhnke->bdhnqk', qb, kx) * (1.0 / math.sqrt(E_))
    qi = jnp.arange(BLK)[:, None]
    kj = jnp.arange(2 * BLK)[None, :]
    step = qi + BLK - kj
    blk = jnp.arange(nb)[:, None, None]
    valid = (step >= 0) & (step <= steps) & (blk * BLK + kj - BLK >= 0)
    bias = -slopes[:, None, None, None] * (step * dilation).astype(jnp.float32)[None, None]
    s = jnp.where(valid, s + bias, NEG)
    lse = jax.nn.logsumexp(s, axis=-1)
    p = jnp.where(valid, jnp.exp(s - lse[..., None]), 0.0)
    o = jnp.einsum('bdhnqk,bdhnke->bdhnqe', p, vx)
    o = o.reshape(B_, dilation, H_, Lp, E_)[:, :, :, :L].transpose(0, 3, 1, 2, 4).reshape(B_, S_, H_, E_)
    lse = lse.reshape(B_, dilation, H_, Lp)[..., :L].transpose(0, 3, 1, 2).reshape(B_, S_, H_)
    return o, lse

def hgrn2_recurrence(q, f_logit, i, lb):
    B_, S_, H_, K_ = q.shape
    q = jax.nn.silu(q.astype(jnp.float32))
    i = i.astype(jnp.float32)
    fl = f_logit.astype(jnp.float32)
    f = lb + (1.0 - lb) * jax.nn.sigmoid(fl)
    log_f = jnp.log(jnp.maximum(f, F_MIN))
    k = (1.0 - lb) * jax.nn.sigmoid(-fl)
    n = S_ // HG_CHUNK

    def chunks(t):
        return t.reshape(B_, n, HG_CHUNK, H_, K_).transpose(1, 0, 3, 2, 4)

    qc, kc, vc, gc = chunks(q), chunks(k), chunks(i), chunks(log_f)
    bc = jnp.cumsum(gc, axis=-2)
    causal = jnp.tril(jnp.ones((HG_CHUNK, HG_CHUNK), dtype=bool))[:, :, None]

    def step(state, inp):
        qt, kt, vt, bt = inp
        diff = bt[..., :, None, :] - bt[..., None, :, :]
        decay = jnp.where(causal, jnp.exp(jnp.where(causal, diff, 0.0)), 0.0)
        scores = jnp.einsum('bhtk,bhsk,bhtsk->bhts', qt, kt, decay)
        o = jnp.einsum('bhts,bhsv->bhtv', scores, vt) + jnp.einsum('bhtk,bhkv->bhtv', qt * jnp.exp(bt), state)
        b_last = bt[..., -1:, :]
        state = jnp.exp(b_last[..., 0, :])[..., None] * state + jnp.einsum('bhsk,bhsv->bhkv', kt * jnp.exp(b_last - bt), vt)
        return state, o

    state0 = jnp.zeros((B_, H_, K_, K_), jnp.float32)
    _, o = lax.scan(step, state0, (qc, kc, vc, bc))
    return o.transpose(1, 0, 3, 2, 4).reshape(B_, S_, H_, K_)

def setup_inputs(seed: int = 0) -> dict:
    key = jax.random.key(seed)
    ks = jax.random.split(key, 20)
    f32 = jnp.float32

    def w(k, shape, fan_in):
        return jax.random.normal(k, shape, f32) * fan_in ** -0.5

    def gain(k, shape):
        return 1.0 + 0.02 * jax.random.normal(k, shape, f32)

    return {
        "x": jax.random.normal(ks[0], (BATCH, SEQ, D_MODEL), f32),
        "mem": jax.random.normal(ks[1], (BATCH, N_MEM, D_MODEL), f32),
        "norm1_g": gain(ks[2], (DEPTH, D_MODEL)),
        "w_in": w(ks[3], (DEPTH, D_MODEL, IN_W), D_MODEL),
        "attn_qn_g": gain(ks[4], (DEPTH, ATT_HEAD_DIM)),
        "attn_kn_g": gain(ks[5], (DEPTH, ATT_HEAD_DIM)),
        "hg_lb": 0.1 * jax.random.normal(ks[6], (DEPTH, HG_W), f32),
        "hg_onorm_g": gain(ks[7], (DEPTH, HG_W)),
        "w_out": w(ks[8], (DEPTH, MIX_W, D_MODEL), MIX_W),
        "norm2_g": gain(ks[9], (DEPTH, D_MODEL)),
        "mem_norm_g": gain(ks[10], (DEPTH, D_MODEL)),
        "w_mq": w(ks[11], (DEPTH, D_MODEL, D_MODEL), D_MODEL),
        "w_mkv": w(ks[12], (DEPTH, D_MODEL, 2 * D_MODEL), D_MODEL),
        "mq_norm_g": gain(ks[13], (DEPTH, MEM_HEAD_DIM)),
        "mk_norm_g": gain(ks[14], (DEPTH, MEM_HEAD_DIM)),
        "w_mo": w(ks[15], (DEPTH, D_MODEL, D_MODEL), D_MODEL),
        "norm3_g": gain(ks[16], (DEPTH, D_MODEL)),
        "w_ff1": w(ks[17], (DEPTH, D_MODEL, D_FF), D_MODEL),
        "w_ff2": w(ks[18], (DEPTH, D_FF, D_MODEL), D_FF),
    }

def reference(x, mem, norm1_g, w_in, attn_qn_g, attn_kn_g, hg_lb, hg_onorm_g, w_out,
              norm2_g, mem_norm_g, w_mq, w_mkv, mq_norm_g, mk_norm_g, w_mo,
              norm3_g, w_ff1, w_ff2):
    B_, S_, _ = x.shape
    f32 = jnp.float32
    slopes = jnp.exp2(-8.0 / ATT_HEADS * jnp.arange(1, ATT_HEADS + 1, dtype=f32))
    p_lb = jax.nn.softmax(hg_lb.astype(f32), axis=0)
    lower_bounds = jnp.cumsum(p_lb, axis=0) - p_lb[0:1]
    cuts = np.cumsum([ATT_W, ATT_W, ATT_W, HG_W, HG_W, HG_W]).tolist()

    for l in range(DEPTH):
        h = rms_norm(x, norm1_g[l])
        z = h @ w_in[l]
        qa, ka, va, qh, fh, ih, gh = jnp.split(z, cuts, axis=-1)
        qa = rms_norm(qa.reshape(B_, S_, ATT_HEADS, ATT_HEAD_DIM), attn_qn_g[l]).astype(f32)
        ka = rms_norm(ka.reshape(B_, S_, ATT_HEADS, ATT_HEAD_DIM), attn_kn_g[l]).astype(f32)
        va = va.reshape(B_, S_, ATT_HEADS, ATT_HEAD_DIM).astype(f32)
        outs, lses = [], []
        for window, dilation in DILATED_PATTERNS:
            o_b, lse_b = dilated_branch(qa, ka, va, window, dilation, slopes)
            outs.append(o_b)
            lses.append(lse_b)
        wts = jax.nn.softmax(jnp.stack(lses, axis=0), axis=0)
        ya = jnp.sum(wts[..., None] * jnp.stack(outs, axis=0), axis=0).reshape(B_, S_, ATT_W)

        hs = (B_, S_, HG_HEADS, HG_HEAD_DIM)
        oh = hgrn2_recurrence(qh.reshape(hs), fh.reshape(hs), ih.reshape(hs),
                              lower_bounds[l].reshape(HG_HEADS, HG_HEAD_DIM))
        oh = rms_norm(oh, hg_onorm_g[l].reshape(HG_HEADS, HG_HEAD_DIM)).reshape(B_, S_, HG_W)
        yh = oh * jax.nn.silu(gh.astype(f32))

        y = jnp.concatenate([ya, yh], axis=-1).astype(x.dtype) @ w_out[l]
        x = x + y

        h = rms_norm(x, norm2_g[l])
        mn = rms_norm(mem, mem_norm_g[l])
        qm = rms_norm((h @ w_mq[l]).reshape(B_, S_, MEM_HEADS, MEM_HEAD_DIM), mq_norm_g[l]).astype(f32)
        km, vm = jnp.split(mn @ w_mkv[l], 2, axis=-1)
        km = rms_norm(km.reshape(B_, -1, MEM_HEADS, MEM_HEAD_DIM), mk_norm_g[l]).astype(f32)
        vm = vm.reshape(B_, -1, MEM_HEADS, MEM_HEAD_DIM).astype(f32)
        sm = jnp.einsum('bshe,bmhe->bhsm', qm, km) * (1.0 / math.sqrt(MEM_HEAD_DIM))
        pm = jax.nn.softmax(sm, axis=-1)
        om = jnp.einsum('bhsm,bmhe->bshe', pm, vm).reshape(B_, S_, D_MODEL)
        x = x + om.astype(x.dtype) @ w_mo[l]

        h = rms_norm(x, norm3_g[l])
        u = jnp.square(jax.nn.relu(h @ w_ff1[l]))
        x = x + u @ w_ff2[l]
    return x


_drawn_inputs = setup_inputs


def setup_inputs(seed=0):
    import zlib

    import numpy as np

    out = dict(_drawn_inputs(seed))
    spreads = {}
    factors = {'norm1_g': 4.036,
     'attn_qn_g': 8.0,
     'attn_kn_g': 8.0,
     'hg_onorm_g': 7.012,
     'norm2_g': 8.0,
     'mem_norm_g': 8.0,
     'mq_norm_g': 8.0,
     'mk_norm_g': 8.0,
     'norm3_g': 12.807}
    for name, (base, spread) in spreads.items():
        noise = np.random.default_rng([zlib.crc32(name.encode()), seed]).standard_normal(out[name].shape)
        drawn = base * np.exp(spread * noise) if base else spread * noise
        out[name] = __import__('jax').numpy.asarray(drawn.astype(out[name].dtype))
    for name, factor in factors.items():
        out[name] = (out[name] * factor).astype(out[name].dtype)
    return out
```

```python
import math

import concourse.bass as bass
from concourse import mybir
from contextlib import ExitStack

F32 = mybir.dt.float32
F32R = mybir.dt.float32r
ALU = mybir.AluOpType
ACT = mybir.ActivationFunctionType
AX = mybir.AxisListType

P = 128
BANK = 512
D = 1024
KT = D // P
HK = KT // 2
EPS = 1e-6
F_MIN = 1e-12


def newton(dve, chain, at, r, v, t):
    dve.tensor_tensor(t, r, r, ALU.mult).then_inc(chain, 1)
    dve.wait_ge(chain, at + 1)
    dve.tensor_tensor(t, t, v, ALU.mult).then_inc(chain, 1)
    dve.wait_ge(chain, at + 2)
    dve.tensor_scalar(t, t, -0.5, 1.5, ALU.mult, ALU.add).then_inc(chain, 1)
    dve.wait_ge(chain, at + 3)
    dve.tensor_tensor(r, r, t, ALU.mult).then_inc(chain, 1)
    dve.wait_ge(chain, at + 4)


def project(nc, name, src, gain, weight, plan, groups, tiles, ident, residual=None, lower=None):
    T = tiles * P
    chunks = sum(p[2] for p in plan)
    kinds = {p[0].split()[0]: sum(q[2] for q in plan if q[0].split()[0] == p[0].split()[0]) for p in plan}
    head_width = next((int(p[0].split()[1]) for p in plan if p[0].startswith("heads")), BANK)
    NH = BANK // head_width
    with nc.cleanup_on_exit(), ExitStack() as ctx:
        def sb(what, shape, dt=F32):
            return ctx.enter_context(nc.sbuf_tensor(f"{name}_{what}", shape, dt))

        def ps(what, shape):
            return ctx.enter_context(nc.psum_tensor(f"{name}_{what}", shape, F32))

        def sem(what):
            return nc.alloc_semaphore(f"{name}_{what}")

        x_in = sb("x_in", [P, 2, D])
        junk = sb("junk", [P, D])
        sumsq = sb("sumsq", [P, 2])
        root = sb("root", [P, 2])
        scratch = sb("scratch", [P, 2])
        eps = sb("eps", [P, 1])
        rstd = sb("rstd", [P, 2])
        h = sb("h", [P, 2, D]) if gain is not None else x_in
        g_rep = sb("g_rep", [P, D])
        a_hi = [sb(f"a_hi{s}", [P, KT, T], F32R) for s in range(2)]
        a_lo = [sb(f"a_lo{s}", [P, KT, T], F32R) for s in range(2)]
        raw = sb("raw", [P, 2, HK, BANK])
        w_hi = sb("w_hi", [P, 2, HK, BANK], F32R)
        w_lo = sb("w_lo", [P, 2, HK, BANK], F32R)
        out_sb = sb("out", [P, tiles, BANK])
        res = sb("res", [P, tiles, BANK]) if residual is not None else None
        side = sb("side", [P, 2, BANK])
        keys = sb("keys", [P, tiles, BANK]) if "gates" in kinds else None
        head_sum = sb("head_sum", [P, 2, NH])
        head_rstd = sb("head_rstd", [P, 2, NH])
        head_scratch = sb("head_scratch", [P, 2, NH])
        acc = ps("acc", [P, 4, BANK])
        turn = ps("turn", [P, 2, BANK])

        gain_landed = sem("gain_landed")
        gain_ready = sem("gain_ready")
        x_landed = [sem(f"x_landed{s}") for s in range(2)]
        sumsq_ready = sem("sumsq_ready")
        eps_ready = sem("eps_ready")
        root_ready = sem("root_ready")
        rstd_chain = sem("rstd_chain")
        side_ready = {k: [sem(f"{k}_side{s}") for s in range(2)] for k in kinds}
        side_used = {k: [sem(f"{k}_used{s}") for s in range(2)] for k in kinds}
        side_free = [sem(f"side_free{s}") for s in range(2)]
        keys_stored = [sem(f"keys_stored{t}") for t in range(tiles)]
        head_summed = sem("head_summed")
        head_rooted = sem("head_rooted")
        head_chain = sem("head_chain")
        rstd_ready = sem("rstd_ready")
        h_ready = sem("h_ready")
        turned = sem("turned")
        a_hi_ready = sem("a_hi_ready")
        a_ready = sem("a_ready")
        raw_landed = [sem(f"raw_landed{s}") for s in range(2)]
        w_hi_ready = [sem(f"w_hi_ready{s}") for s in range(2)]
        w_ready = [sem(f"w_ready{s}") for s in range(2)]
        first_half_used = sem("first_half_used")
        acc_full = [sem(f"acc_full{t}") for t in range(tiles)]
        acc_read = [sem(f"acc_read{t}") for t in range(tiles)]
        out_stored = [sem(f"out_stored{t}") for t in range(tiles)]
        res_landed = [sem(f"res_landed{t}") for t in range(tiles)]
        block = ctx.enter_context(nc.Block())

        src_tiles = src.rearrange("(n p) d -> n p d", p=P)
        w_rows = weight.rearrange("(h k p) c -> h p k c", k=HK, p=P)

        def destination(kind, dst, j, g, t):
            if by_rows(kind):
                return dst[g * T + t * P:g * T + (t + 1) * P, bass.ds(j * BANK, BANK)]
            return dst[bass.ds(j * BANK + t * P, P), g * T:(g + 1) * T]

        def each_chunk(eng, g, body):
            n0 = g * chunks
            seen = {k: g * v for k, v in kinds.items()}
            for i, (what, c0, count, dst, d0) in enumerate(plan):
                final = i == len(plan) - 1
                looped = count - 1 if final else count
                m0 = seen[what.split()[0]]
                if looped > 1:
                    with eng.Fori(0, looped) as r:
                        body(what, r + c0, dst, r + d0, r + n0, r + m0, False)
                elif looped == 1:
                    body(what, c0, dst, d0, n0, m0, False)
                n0 += count
                seen[what.split()[0]] += count
                if final:
                    body(what, c0 + count - 1, dst, d0 + count - 1, n0 - 1, m0 + count - 1, True)

        def by_rows(kind):
            return kind.startswith("heads") or kind.endswith("rows")

        def prepares(g, last):
            return last and g + 1 < groups

        @block.sync
        def _(sp):
            if gain is not None:
                sp.dma_start(g_rep[:], gain.broadcast_to([P, D])).then_inc(gain_landed, 16)

            def load_rows(n):
                if n >= 2 and gain is not None:
                    sp.wait_ge(h_ready, n - 1)
                if n >= 2 and gain is None:
                    sp.wait_ge(turned, 2 * (n - 1))
                sp.dma_start(x_in[:, n % 2, :], src_tiles[n]).then_inc(x_landed[n % 2], 16)

            def chunk(g):
                def body(kind, c, dst, j, n, m, last):
                    for half in range(2):
                        sp.wait_ge(w_ready[half], n)
                        sp.dma_start(raw[:, half], w_rows[half, :, :, bass.ds(c * BANK, BANK)]
                                     ).then_inc(raw_landed[half], 16)
                    if residual is not None:
                        for t in range(tiles):
                            sp.wait_ge(acc_read[t], n)
                            sp.dma_start(res[:, t], destination("rows", residual, j, g, t)
                                         ).then_inc(res_landed[t], 16)
                    if prepares(g, last):
                        for t in range(tiles):
                            load_rows((g + 1) * tiles + t)
                return body

            for t in range(tiles):
                load_rows(t)
            for g in range(groups):
                each_chunk(sp, g, chunk(g))
            for t in range(tiles):
                sp.wait_ge(out_stored[t], 16 * groups * chunks)
                if "gates" in kinds:
                    sp.wait_ge(keys_stored[t], 16 * groups * kinds["gates"])

        @block.gpsimd
        def _(pool):
            def chunk(kind, c, dst, j, n, m, last):
                for half in range(2):
                    pool.wait_ge(w_hi_ready[half], n + 1)
                    pool.tensor_tensor(w_lo[:, half], raw[:, half], w_hi[:, half].bitcast(F32), ALU.subtract
                                       ).then_inc(w_ready[half], 1)
            for g in range(groups):
                each_chunk(pool, g, chunk)

        @block.scalar
        def _(act):
            def square(n):
                act.wait_ge(x_landed[n % 2], 16 * (n // 2 + 1))
                if n >= 1:
                    act.wait_ge(sumsq_ready, n)
                if n >= 2:
                    act.wait_ge(rstd_ready, n - 1)
                act.activation(junk[:], x_in[:, n % 2, :], ACT.Square,
                               accum_out=sumsq[:, n % 2:n % 2 + 1]).then_inc(sumsq_ready, 1)
                act.wait_ge(sumsq_ready, n + 1)
                act.activation(root[:, n % 2:n % 2 + 1], sumsq[:, n % 2:n % 2 + 1], ACT.Sqrt,
                               bias=eps[:]).then_inc(root_ready, 1)

            def high_part(n, b):
                act.wait_ge(turned, 2 * n + b + 1)
                g, t = divmod(n, tiles)
                act.activation(a_hi[g % 2][:, b * HK:(b + 1) * HK, t * P:(t + 1) * P],
                               turn[:, b].rearrange("p (k c) -> p k c", k=HK), ACT.Copy
                               ).then_inc(a_hi_ready, 1)

            def finish(kind, t, n, m):
                s, w = t % 2, m * (tiles // 2) + t // 2
                if residual is not None:
                    return
                if kind in ("rows", "columns"):
                    act.wait_ge(out_stored[t], n * 16)
                    act.activation(out_sb[:, t], acc[:, t], ACT.Copy).then_inc(acc_read[t], 1)
                elif kind == "silu":
                    act.activation(side[:, s], acc[:, t], ACT.Sigmoid).then_inc(side_ready[kind][s], 1)
                elif kind == "gates":
                    act.wait_ge(keys_stored[t], m * 16)
                    act.activation(keys[:, t], acc[:, t], ACT.Sigmoid, scale=-1.0)
                    act.activation(side[:, s], acc[:, t], ACT.Sigmoid).then_inc(side_ready[kind][s], 1)
                elif kind == "heads":
                    act.activation(side[:, s], acc[:, t], ACT.Square).then_inc(side_ready[kind][s], 1)
                    act.wait_ge(head_summed, m * tiles + t + 1)
                    act.activation(head_rstd[:, s], head_sum[:, s], ACT.Sqrt).then_inc(head_rooted, 1)

            def chunk(g):
                def body(kind, c, dst, j, n, m, last):
                    for step in range(2 * tiles):
                        if prepares(g, last):
                            at = (g + 1) * tiles + step // 2
                            if gain is not None and step == 0:
                                square(at)
                            if gain is not None and step % 2 == 0 and step < 2 * tiles - 2:
                                square(at + 1)
                            high_part(at, step % 2)
                        t = step - tiles
                        if t < 0:
                            continue
                        act.wait_ge(acc_full[t], n + 1)
                        finish(kind.split()[0], t, n, m)
                        act.wait_ge(acc_read[t], n + 1)
                        first = dst[0] if kind == "gates" else dst
                        act.dma_start(destination(kind, first, j, g, t), out_sb[:, t]).then_inc(out_stored[t], 16)
                        if kind == "gates":
                            act.dma_start(destination(kind, dst[1], j, g, t), keys[:, t]).then_inc(keys_stored[t], 16)
                return body

            act.wait_ge(eps_ready, 1)
            for n in range(tiles):
                if gain is not None:
                    square(n)
                high_part(n, 0)
                high_part(n, 1)
            for g in range(groups):
                each_chunk(act, g, chunk(g))

        @block.vector
        def _(dve):
            dve.memset(eps[:], D * EPS).then_inc(eps_ready, 1)
            if gain is not None:
                dve.wait_ge(gain_landed, 16)
                dve.tensor_scalar(g_rep[:], g_rep[:], math.sqrt(D), None, ALU.mult
                                  ).then_inc(gain_ready, 1)
                dve.wait_ge(gain_ready, 1)

            def normalise(n):
                if n >= 2:
                    dve.wait_ge(turned, 2 * (n - 1))
                s = slice(n % 2, n % 2 + 1)
                dve.wait_ge(root_ready, n + 1)
                dve.tensor_scalar(sumsq[:, s], sumsq[:, s], D * EPS, None, ALU.add).then_inc(rstd_chain, 1)
                dve.reciprocal(rstd[:, s], root[:, s]).then_inc(rstd_chain, 1)
                dve.wait_ge(rstd_chain, n * 6 + 2)
                newton(dve, rstd_chain, n * 6 + 2, rstd[:, s], sumsq[:, s], scratch[:, s])
                dve.engine_nop().then_inc(rstd_ready, 1)
                dve.wait_ge(rstd_ready, n + 1)
                dve.scalar_tensor_tensor(h[:, n % 2], x_in[:, n % 2], rstd[:, s], g_rep[:],
                                         ALU.mult, ALU.mult).then_inc(h_ready, 1)

            def low_part(n, b):
                dve.wait_ge(a_hi_ready, 2 * n + b + 1)
                g, t = divmod(n, tiles)
                at = (slice(None), slice(b * HK, (b + 1) * HK), slice(t * P, (t + 1) * P))
                dve.tensor_tensor(a_lo[g % 2][at], turn[:, b].rearrange("p (k c) -> p k c", k=HK),
                                  a_hi[g % 2].bitcast(F32)[at], ALU.subtract).then_inc(a_ready, 1)

            def split_weights(n, half):
                dve.wait_ge(raw_landed[half], n * 16 + 16)
                dve.wait_ge(acc_full[tiles - 1] if half else first_half_used, n)
                dve.tensor_copy(w_hi[:, half], raw[:, half]).then_inc(w_hi_ready[half], 1)

            def finish(kind, t, n, m):
                s, w = t % 2, m * (tiles // 2) + t // 2
                if kind in ("rows", "columns"):
                    return
                dve.wait_ge(side_ready[kind][s], w + 1)
                dve.wait_ge(out_stored[t], n * 16)
                if kind == "silu":
                    dve.tensor_tensor(out_sb[:, t], acc[:, t], side[:, s], ALU.mult).then_inc(acc_read[t], 1)
                elif kind == "gates":
                    dve.tensor_scalar(keys[:, t], keys[:, t], lower[1][:, t:t + 1], None, ALU.mult)
                    dve.tensor_scalar(out_sb[:, t], side[:, s], lower[1][:, t:t + 1], lower[0][:, t:t + 1],
                                      ALU.mult, ALU.add).then_inc(side_used[kind][s], 1)
                    dve.wait_ge(side_used[kind][s], w + 1)
                    dve.tensor_scalar(out_sb[:, t], out_sb[:, t], F_MIN, None, ALU.max).then_inc(acc_read[t], 1)
                elif kind == "heads":
                    at = (m * tiles + t) * 6
                    dve.tensor_reduce(head_sum[:, s], side[:, s].rearrange("p (h e) -> p h e", h=NH), AX.X, ALU.add
                                      ).then_inc(head_chain, 1)
                    dve.wait_ge(head_chain, at + 1)
                    dve.tensor_scalar(head_sum[:, s], head_sum[:, s], head_width * EPS, None, ALU.add
                                      ).then_inc(head_summed, 1)
                    dve.wait_ge(head_rooted, m * tiles + t + 1)
                    dve.reciprocal(head_rstd[:, s], head_rstd[:, s]).then_inc(head_chain, 1)
                    dve.wait_ge(head_chain, at + 2)
                    newton(dve, head_chain, at + 2, head_rstd[:, s], head_sum[:, s], head_scratch[:, s])
                    dve.scalar_tensor_tensor(out_sb[:, t].rearrange("p (h e) -> p h e", h=NH),
                                             acc[:, t].rearrange("p (h e) -> p h e", h=NH), math.sqrt(head_width),
                                             head_rstd[:, s].unsqueeze(2).broadcast_to([P, NH, head_width]),
                                             ALU.mult, ALU.mult).then_inc(acc_read[t], 1)

            def chunk(g):
                def body(kind, c, dst, j, n, m, last):
                    for step in range(2 * tiles):
                        if step % tiles == 0:
                            if step == 0:
                                split_weights(n, 1)
                            elif not (last and g + 1 == groups):
                                split_weights(n + 1, 0)
                        if prepares(g, last):
                            at = (g + 1) * tiles + step // 2
                            if step % 2 == 0 and gain is not None:
                                normalise(at)
                            low_part(at, step % 2)
                        t = step - tiles
                        if t >= 0 and residual is not None:
                            dve.wait_ge(acc_full[t], n + 1)
                            dve.wait_ge(res_landed[t], n * 16 + 16)
                            dve.wait_ge(out_stored[t], n * 16)
                            dve.tensor_tensor(out_sb[:, t], acc[:, t], res[:, t], ALU.add
                                              ).then_inc(acc_read[t], 1)
                        elif t >= 0:
                            finish(kind.split()[0], t, n, m)
                return body

            for n in range(tiles):
                if gain is not None:
                    normalise(n)
                low_part(n, 0)
                low_part(n, 1)
            split_weights(0, 0)
            for g in range(groups):
                each_chunk(dve, g, chunk(g))

        @block.tensor
        def _(pe):
            def turn_rows(n, b):
                if gain is not None:
                    pe.wait_ge(h_ready, n + 1)
                else:
                    pe.wait_ge(x_landed[n % 2], 16 * (n // 2 + 1))
                if n >= 1:
                    pe.wait_ge(a_ready, 2 * (n - 1) + b + 1)
                for k in range(HK):
                    at = (b * HK + k) * P
                    mm = pe.transpose(turn[:, b, k * P:(k + 1) * P], h[:, n % 2, at:at + P], ident[:])
                mm.then_inc(turned, 1)

            def products(kind, s, half, t, first, final):
                for k in range(HK):
                    a = half * HK + k
                    cut = slice(t * P, (t + 1) * P)
                    if by_rows(kind):
                        terms = [(a_hi[s][:, a, cut], w_hi[:, half, k]), (a_hi[s][:, a, cut], w_lo[:, half, k]),
                                 (a_lo[s][:, a, cut], w_hi[:, half, k])]
                    else:
                        terms = [(w_hi[:, half, k, cut], a_hi[s][:, a]), (w_hi[:, half, k, cut], a_lo[s][:, a]),
                                 (w_lo[:, half, k, cut], a_hi[s][:, a])]
                    for i, (left, right) in enumerate(terms):
                        mm = pe.matmul(acc[:, t], left, right, start=(first and k == 0 and i == 0),
                                       stop=(final and k == HK - 1 and i == 2))
                return mm

            def chunk(g):
                def body(kind, c, dst, j, n, m, last):
                    for half in range(2):
                        pe.wait_ge(w_ready[half], n + 1)
                        for t in range(tiles):
                            if half == 0:
                                pe.wait_ge(acc_read[t], n)
                            mm = products(kind, g % 2, half, t, half == 0, half == 1)
                            if half == 1:
                                mm.then_inc(acc_full[t], 1)
                            elif t == tiles - 1:
                                mm.then_inc(first_half_used, 1)
                            if prepares(g, last):
                                step = half * tiles + t
                                turn_rows((g + 1) * tiles + step // 2, step % 2)
                return body

            for n in range(tiles):
                turn_rows(n, 0)
                turn_rows(n, 1)
            for g in range(groups):
                pe.wait_ge(a_ready, 2 * (g + 1) * tiles)
                each_chunk(pe, g, chunk(g))


HEADS, HD = 8, 64
AW = HEADS * HD
SEQ = 2048
DILATIONS = (16, 4, 1)
NEG = -1e30
OW = AW + 2 * HEADS


def attend(nc, zt, branch_rows, q_gain, k_gain, ident):
    name = "att"
    with nc.cleanup_on_exit(), ExitStack() as ctx:
        def sb(what, shape, dt=F32):
            return ctx.enter_context(nc.sbuf_tensor(f"{name}_{what}", shape, dt))

        def ps(what, shape):
            return ctx.enter_context(nc.psum_tensor(f"{name}_{what}", shape, F32))

        def sem(what):
            return nc.alloc_semaphore(f"{name}_{what}")

        gains = sb("gains", [P, 2])
        gain = sb("gain", [P, 1])
        step = sb("step", [P, 2 * P])
        hidden = sb("hidden", [P, 2 * P])
        bias = sb("bias", [P, len(DILATIONS) * HEADS, 2 * P])
        qk_in = sb("qk_in", [P, 2, 2 * AW])
        v_in = sb("v_in", [P, 2, AW])
        gate = sb("gate", [1, 2])
        q_t = sb("q_t", [P, 2, 4, P])
        k_t = sb("k_t", [P, 2, 4, P])
        p_sb = sb("p", [P, 2, 2 * P])
        pt_sb = sb("pt_sb", [P, 2, 2, P])
        o_sb = sb("o", [P, 2, OW])
        score = ps("score", [P, 2, BANK])
        pt = ps("pt", [P, 2, BANK])
        o_acc = ps("o_acc", [P, 2, BANK])
        turn = ps("turn", [P, 2, BANK])

        gains_landed = sem("gains_landed")
        gain_ready = sem("gain_ready")
        step_ready = sem("step_ready")
        hidden_set = sem("hidden_set")
        hidden_ready = sem("hidden_ready")
        bias_ready = sem("bias_ready")
        qk_landed = [sem(f"qk_landed{s}") for s in range(2)]
        v_landed = [sem(f"v_landed{s}") for s in range(2)]
        turned = [sem(f"turned{s}") for s in range(2)]
        q_staged = [sem(f"q_staged{s}") for s in range(2)]
        k_staged = [sem(f"k_staged{s}") for s in range(2)]
        s_full = [sem(f"s_full{p}") for p in range(2)]
        masked = [sem(f"masked{p}") for p in range(2)]
        exped = [sem(f"exped{p}") for p in range(2)]
        pt_full = [sem(f"pt_full{p}") for p in range(2)]
        pt_read = [sem(f"pt_read{p}") for p in range(2)]
        pv_done = [sem(f"pv_done{p}") for p in range(2)]
        o_read = [sem(f"o_read{s}") for s in range(2)]
        o_stored = [sem(f"o_stored{s}") for s in range(2)]
        block = ctx.enter_context(nc.Block())

        def rows(t, d, r, n, cols):
            if d == 1:
                return t[bass.ds(n * P, P), cols]
            v = t.rearrange("(j d) c -> j d c", d=d)
            return v[n * P:(n + 1) * P, bass.ds(r, 1), cols].rearrange("j o c -> j (o c)")

        def each_block(eng, body):
            def one(u, c, s, b, r, n, prev, nxt):
                body(u, c, s, (b, DILATIONS[b], r, n), prev, nxt)

            with eng.Fori(0, 8) as m:
                one(m * 2, m, 0, 0, m * 2, 0, False, False)
                one(m * 2 + 1, m, 1, 0, m * 2 + 1, 0, False, False)
            with eng.Fori(0, 4) as r:
                for n in range(4):
                    one(r * 4 + 16 + n, r * 2 + 8 + n // 2, n % 2, 1, r, n, n > 0, n < 3)
            one(32, 16, 0, 2, 0, 0, False, True)
            one(33, 16, 1, 2, 0, 1, True, True)
            with eng.Fori(1, 7) as m:
                for s in range(2):
                    one(m * 2 + 32 + s, m + 16, s, 2, 0, m * 2 + s, True, True)
            one(46, 23, 0, 2, 0, 14, True, True)
            one(47, 23, 1, 2, 0, 15, True, None)

        @block.sync
        def _(sp):
            for i, g in enumerate((q_gain, k_gain)):
                for half in range(2):
                    sp.dma_start(gains[half * HD:(half + 1) * HD, i:i + 1], g).then_inc(gains_landed, 16)

            def load(u, c, s, at, prev, nxt):
                b, d, r, n = at
                sp.wait_ge(turned[s], c)
                sp.dma_start(qk_in[:, s], rows(zt, d, r, n, slice(0, 2 * AW))).then_inc(qk_landed[s], 16)
                if s == 0:
                    sp.wait_ge(o_read[1], c)
                else:
                    sp.wait_ge(o_read[0], c + 1)
                sp.dma_start(v_in[:, s], rows(zt, d, r, n, slice(2 * AW, 3 * AW))
                             ).then_inc(v_landed[s], 16)

            each_block(sp, load)
            for s in range(2):
                sp.wait_ge(o_stored[s], 16 * 24)

        @block.gpsimd
        def _(pool):
            pool.iota(step[:], pattern=[[-1, 2 * P]], base=P, channel_multiplier=1,
                      allow_small_or_imprecise_dtypes=True).then_inc(step_ready, 1)
            pool.memset(hidden[:], 0.0).then_inc(hidden_set, 1)
            pool.wait_ge(hidden_set, 1)
            pool.affine_select(out=hidden[:], in_=hidden[:], compare_op=ALU.is_ge, fill=NEG, base=P,
                               pattern=[[-1, 2 * P]], channel_multiplier=1).then_inc(hidden_set, 1)
            pool.wait_ge(hidden_set, 2)
            pool.affine_select(out=hidden[:], in_=hidden[:], compare_op=ALU.is_ge, fill=NEG, base=0,
                               pattern=[[1, 2 * P]], channel_multiplier=-1).then_inc(hidden_ready, 1)

        @block.vector
        def _(dve):
            dve.wait_ge(gains_landed, 64)
            dve.scalar_tensor_tensor(gain[:], gains[:, 0:1], 1 / math.sqrt(HD), gains[:, 1:2],
                                     ALU.mult, ALU.mult).then_inc(gain_ready, 1)
            dve.wait_ge(step_ready, 1)
            dve.wait_ge(hidden_ready, 1)
            for b, d in enumerate(DILATIONS):
                for e in range(HEADS):
                    slope = 2.0 ** (-8.0 / HEADS * (e + 1))
                    dve.scalar_tensor_tensor(bias[:, b * HEADS + e], step[:], -slope * d, hidden[:],
                                             ALU.mult, ALU.add).then_inc(bias_ready, 1)
            dve.wait_ge(bias_ready, len(DILATIONS) * HEADS)
            dve.wait_ge(gain_ready, 1)

            def stage_q(s, c):
                dve.wait_ge(turned[s], c + 1)
                dve.tensor_scalar(q_t[:, s], turn[:, 0].rearrange("p (k c) -> p k c", k=4), gain[:], None,
                                  ALU.mult).then_inc(q_staged[s], 1)

            def read_pt(u, e):
                p, w = e % 2, u * 4 + e // 2
                dve.wait_ge(pt_full[p], w + 1)
                dve.wait_ge(pv_done[p], w)
                return p

            def body(u, c, s, at, prev, nxt):
                b = at[0]
                for e in range(HEADS):
                    p, w = e % 2, u * 4 + e // 2
                    lo = 0 if prev else P
                    if e == 0:
                        dve.wait_ge(o_stored[s], c * 16)
                    dve.wait_ge(s_full[p], w + 1)
                    dve.wait_ge(pt_full[p], w)
                    dve.memset(gate[:, p:p + 1], 0.0)
                    dve.tensor_tensor_reduce(p_sb[:, p, lo:], score[:, p, lo:2 * P],
                                             bias[:, b * HEADS + e, lo:], -1.0, 3e38, ALU.add,
                                             ALU.min, o_sb[:, s, AW + e:AW + e + 1]
                                             ).then_inc(masked[p], 1)
                    if e == 6 and nxt is not None:
                        stage_q(1 - s, c + s)
                    if e % 2 == 1:
                        q = read_pt(u, e - 1)
                        dve.tensor_copy(pt_sb[:, q, lo // P:], pt[:, q, lo:2 * P].rearrange("p (k c) -> p k c", c=P)
                                        ).then_inc(pt_read[q], 1)

            stage_q(0, 0)
            each_block(dve, body)

        @block.scalar
        def _(act):
            def stage_k(s, c):
                act.wait_ge(turned[s], c + 1)
                act.activation(k_t[:, s], turn[:, 1].rearrange("p (k c) -> p k c", k=4), ACT.Copy
                               ).then_inc(k_staged[s], 1)

            def body(u, c, s, at, prev, nxt):
                lo = 0 if prev else P
                b, d, r, n = at
                for e in range(HEADS):
                    p, w = e % 2, u * 4 + e // 2
                    act.wait_ge(masked[p], w + 1)
                    act.activation(p_sb[:, p, lo:], p_sb[:, p, lo:], ACT.Exp, scale=-1.0,
                                   bias=o_sb[:, s, AW + e:AW + e + 1],
                                   accum_out=o_sb[:, s, AW + HEADS + e:AW + HEADS + e + 1]
                                   ).then_inc(exped[p], 1)
                    if e == 6 and nxt is not None:
                        stage_k(1 - s, c + s)
                    for o in ((e - 1,) if e % 2 == 0 and e else (e,) if e == HEADS - 1 else ()):
                        q, v = o % 2, u * 4 + o // 2
                        act.wait_ge(pt_full[q], v + 1)
                        act.wait_ge(pv_done[q], v)
                        act.activation(pt_sb[:, q, lo // P:], pt[:, q, lo:2 * P].rearrange("p (k c) -> p k c", c=P), ACT.Copy
                                       ).then_inc(pt_read[q], 1)
                act.wait_ge(pv_done[1], u * 4 + 4)
                act.activation(o_sb[:, s, 0:AW], o_acc[:, s, :], ACT.Copy).then_inc(o_read[s], 1)
                act.wait_ge(o_read[s], c + 1)
                act.dma_start(rows(branch_rows[b], d, r, n, slice(0, OW)), o_sb[:, s]).then_inc(o_stored[s], 16)

            stage_k(0, 0)
            each_block(act, body)

        @block.tensor
        def _(pe):
            def turn_qk(s, c):
                pe.wait_ge(qk_landed[s], c * 16 + 16)
                for j in range(8):
                    mm = pe.transpose(turn[:, j // 4, (j % 4) * P:(j % 4 + 1) * P],
                                      qk_in[:, s, j * P:(j + 1) * P], ident[:])
                mm.then_inc(turned[s], 1)

            def scores(u, s, e, prev):
                p, w = e % 2, u * 4 + e // 2
                pe.wait_ge(masked[p], w)
                pair, base = e // 2, (e % 2) * HD
                at = slice(base, base + HD)
                for side in ((0, 1) if prev else (1,)):
                    k_slot = s if side else 1 - s
                    mm = pe.matmul(score[:, p, side * P:(side + 1) * P], q_t[at, s, pair], k_t[at, k_slot, pair],
                                   start=True, stop=True)
                mm.then_inc(s_full[p], 1)

            def transposes(u, e, prev):
                p, w = e % 2, u * 4 + e // 2
                pe.wait_ge(exped[p], w + 1)
                pe.wait_ge(pt_read[p], w)
                for side in ((0, 1) if prev else (1,)):
                    cols = slice(side * P, (side + 1) * P)
                    mm = pe.transpose(pt[:, p, cols], p_sb[:, p, cols], ident[:])
                mm.then_inc(pt_full[p], 1)

            def sums(u, c, s, e, prev):
                p, w = e % 2, u * 4 + e // 2
                if e == 0:
                    pe.wait_ge(v_landed[s], c * 16 + 16)
                    pe.wait_ge(o_read[s], c)
                pe.wait_ge(pt_read[p], w + 1)
                cols = slice(e * HD, (e + 1) * HD)
                for side in ((0, 1) if prev else (1,)):
                    mm = pe.matmul(o_acc[:, s, cols], pt_sb[:, p, side], v_in[:, s if side else 1 - s, cols],
                                   start=(side == 0 or not prev), stop=(side == 1))
                mm.then_inc(pv_done[p], 1)

            def body(u, c, s, at, prev, nxt):
                for e in range(HEADS):
                    transposes(u, e, prev)
                    if e < HEADS - 2:
                        scores(u, s, e + 2, prev)
                    elif nxt is not None:
                        if e == HEADS - 2:
                            pe.wait_ge(q_staged[1 - s], c + s + 1)
                            pe.wait_ge(k_staged[1 - s], c + s + 1)
                        scores(u + 1, 1 - s, e + 2 - HEADS, nxt)
                    if e == HEADS - 3 and nxt is not None:
                        turn_qk(1 - s, c + s)
                    if e:
                        sums(u, c, s, e - 1, prev)
                sums(u, c, s, HEADS - 1, prev)

            turn_qk(0, 0)
            pe.wait_ge(q_staged[0], 1)
            pe.wait_ge(k_staged[0], 1)
            scores(0, 0, 0, False)
            scores(0, 0, 1, False)
            each_block(pe, body)


HH, HK_ = 4, 128
HGW = HH * HK_
SEQ = 2048
LEVELS = 7
C = P


def recur(nc, zf, zt, y, onorm_g, ident):
    name = "hg"
    with nc.cleanup_on_exit(), ExitStack() as ctx:
        def sb(what, shape, dt=F32):
            return ctx.enter_context(nc.sbuf_tensor(f"{name}_{what}", shape, dt))

        def ps(what, shape):
            return ctx.enter_context(nc.psum_tensor(f"{name}_{what}", shape, F32))

        def sem(what):
            return nc.alloc_semaphore(f"{name}_{what}")

        I32 = mybir.dt.int32
        row_i = sb("row_i", [P, C], I32)
        col_i = sb("col_i", [P, C], I32)
        after = sb("after", [P, C], I32)
        differ = sb("differ", [P, C], I32)
        later = sb("later", [P, C], I32)
        gate = sb("gate", [1, LEVELS + 1])
        top = sb("top", [P, C], I32)
        mask = sb("mask", [P, LEVELS + 1, C], I32)
        restart = sb("restart", [P, HH, C])
        og = sb("og", [P, HGW])
        eps = sb("eps", [P, 1])
        q_in = sb("q_in", [P, 2, HH, C])
        k_in = sb("k_in", [P, 2, HH, C])
        f_in = sb("f_in", [P, 2, HH, C])
        ig_in = sb("ig_in", [P, 2, 2 * HGW])
        b = sb("b", [P, 2, HH, C])
        diff = sb("diff", [P, 2, HH, C])
        decay = sb("decay", [P, 2, HH, C])
        q_dec = sb("q_dec", [P, LEVELS + 1, HH, C])
        k_dec = sb("k_dec", [P, LEVELS + 1, HH, C])
        b_exp = sb("b_exp", [P, HH, C])
        last_exp = sb("last_exp", [P, HH])
        k_rows = sb("k_rows", [P, HH, C])
        s_sb = sb("s_sb", [P, 2, HH, C])
        state = sb("state", [P, HH, C])
        squares = sb("squares", [P, HH, C])
        ms = sb("ms", [P, 4, HH])
        gated = sb("gated", [P, 2, HGW])
        out = sb("out", [P, 2, HGW])
        s_ps = ps("s_ps", [P, 4, BANK])
        o_ps = ps("o_ps", [P, 2, BANK])
        kt_ps = ps("kt_ps", [P, BANK])
        st_ps = ps("st_ps", [P, BANK])

        consts = sem("consts")
        og_landed = sem("og_landed")
        iotas = sem("iotas")
        masks = sem("masks")
        cleared = sem("cleared")
        in_landed = [sem(f"in_landed{s}") for s in range(2)]
        ig_landed = [sem(f"ig_landed{s}") for s in range(2)]
        logged = sem("logged")
        summed = sem("summed")
        diffed = [sem(f"diffed{p}") for p in range(2)]
        exped = [sem(f"exped{p}") for p in range(2)]
        b_exped = sem("b_exped")
        last_exped = sem("last_exped")
        q_scaled = sem("q_scaled")
        k_scaled = sem("k_scaled")
        s_full = [sem(f"s_full{p}") for p in range(4)]
        s_read = [sem(f"s_read{p}") for p in range(4)]
        k_turned = sem("k_turned")
        k_rows_ready = sem("k_rows_ready")
        st_full = sem("st_full")
        st_ready = sem("st_ready")
        o_full = [sem(f"o_full{s}") for s in range(2)]
        squared = sem("squared")
        mean_ready = sem("mean_ready")
        ln_ready = sem("ln_ready")
        rstd0 = sem("rstd0")
        chain = sem("chain")
        gated_ready = sem("gated_ready")
        out_ready = [sem(f"out_ready{s}") for s in range(2)]
        out_stored = [sem(f"out_stored{s}") for s in range(2)]
        block = ctx.enter_context(nc.Block())

        def each_chunk(eng, body):
            with eng.Fori(0, SEQ // C // 2) as c:
                for s in range(2):
                    body(c * 2 + s, c, s)

        def blocks_of(t, lev):
            half = C >> (lev + 1)
            return t.rearrange("p h (n two c) -> p (h n) two c", two=2, c=half)

        @block.sync
        def _(sp):
            sp.dma_start(og[:], onorm_g.broadcast_to([P, HGW])).then_inc(og_landed, 16)

            def body(u, c, s):
                sp.wait_ge(st_ready, u)
                sp.wait_ge(out_ready[s], c)
                for t, r0 in ((q_in, 0), (f_in, HGW), (k_in, 2 * HGW)):
                    sp.dma_start(t[:, s], zf[r0:r0 + HGW, bass.ds(u * C, C)].rearrange("(h p) c -> p h c", p=P)
                                 ).then_inc(in_landed[s], 16)
                sp.dma_start(ig_in[:, s], zt[bass.ds(u * C, C), 1536:1536 + 2 * HGW]).then_inc(ig_landed[s], 16)

            each_chunk(sp, body)
            for s in range(2):
                sp.wait_ge(out_stored[s], 16 * 8)

        @block.gpsimd
        def _(pool):
            pool.iota(row_i[:], pattern=[[0, C]], base=0, channel_multiplier=1).then_inc(iotas, 1)
            pool.iota(col_i[:], pattern=[[1, C]], base=0, channel_multiplier=0).then_inc(iotas, 1)
            pool.iota(later[:], pattern=[[1, C]], base=0, channel_multiplier=-1).then_inc(iotas, 1)
            for t in (q_dec, k_dec, s_sb, state):
                pool.memset(t[:], 0.0).then_inc(cleared, 1)
            pool.memset(restart[:], 1.0).then_inc(consts, 1)
            pool.wait_ge(consts, 1)
            pool.memset(restart[:, :, 0:1], 0.0).then_inc(consts, 1)
            pool.memset(eps[:], EPS).then_inc(consts, 1)
            pool.wait_ge(cleared, 4)

            def body(u, c, s):
                pool.wait_ge(in_landed[s], c * 48 + 48)
                for lev in range(LEVELS + 1):
                    p, w = lev % 2, u * 4 + lev // 2
                    pool.wait_ge(exped[p], w + 1)
                    if lev < LEVELS:
                        pool.wait_ge(s_full[(lev + 1) % 4], u * 2)
                        o, i, e = (blocks_of(t, lev)[:, :, 0] for t in (k_dec[:, lev], k_in[:, s], decay[:, p]))
                        pool.tensor_tensor(o, i, e, ALU.mult).then_inc(k_scaled, 1)
                    else:
                        pool.wait_ge(k_turned, u)
                        pool.tensor_tensor(k_dec[:, lev], k_in[:, s], decay[:, p], ALU.mult).then_inc(k_scaled, 1)
                pool.wait_ge(ig_landed[s], c * 16 + 16)
                pool.wait_ge(og_landed, 16)
                pool.wait_ge(out_ready[s], c)
                pool.tensor_tensor(gated[:, s], ig_in[:, s, HGW:], og[:], ALU.mult).then_inc(gated_ready, 1)

            each_chunk(pool, body)

        @block.scalar
        def _(act):
            nc.scalar.preload_act_table_set("natural_log_exp_and_others")
            act.wait_ge(consts, 3)

            def body(u, c, s):
                act.wait_ge(in_landed[s], c * 48 + 48)
                act.activation(f_in[:, s], f_in[:, s], ACT.Ln).then_inc(logged, 1)
                act.wait_ge(summed, u + 1)
                act.wait_ge(q_scaled, u * 8)
                act.activation(b_exp[:], b[:, s], ACT.Exp).then_inc(b_exped, 1)
                act.wait_ge(st_ready, u + 1)
                act.activation(last_exp[:], b[:, s, :, C - 1], ACT.Exp).then_inc(last_exped, 1)
                for lev in range(LEVELS + 1):
                    p, w = lev % 2, u * 4 + lev // 2
                    act.wait_ge(diffed[p], w + 1)
                    act.wait_ge(q_scaled, u * 8 + max(lev - 1, 0))
                    act.wait_ge(k_scaled, u * 8 + max(lev - 1, 0))
                    act.activation(decay[:, p], diff[:, p], ACT.Exp).then_inc(exped[p], 1)
                act.wait_ge(k_turned, u + 1)
                act.wait_ge(st_full, u)
                act.activation(k_rows[:], kt_ps[:].rearrange("p (h c) -> p h c", h=HH), ACT.Copy
                               ).then_inc(k_rows_ready, 1)
                act.wait_ge(o_full[s], c + 1)
                act.activation(squares[:], o_ps[:, s].rearrange("p (h c) -> p h c", h=HH), ACT.Square
                               ).then_inc(squared, 1)
                act.wait_ge(mean_ready, u + 1)
                act.activation(ms[:, 1], ms[:, 0], ACT.Ln).then_inc(ln_ready, 1)
                act.wait_ge(ln_ready, u + 1)
                act.activation(ms[:, 2], ms[:, 1], ACT.Exp, scale=-0.5).then_inc(rstd0, 1)
                act.wait_ge(out_ready[s], c + 1)
                act.dma_start(y[bass.ds(u * C, C), 512:1024], out[:, s]).then_inc(out_stored[s], 16)

            each_chunk(act, body)

        @block.vector
        def _(dve):
            dve.wait_ge(iotas, 3)
            dve.tensor_tensor(differ[:], row_i[:], col_i[:], ALU.bitwise_xor).then_inc(masks, 1)
            dve.tensor_scalar(after[:], later[:], 0, None, ALU.is_gt).then_inc(masks, 1)
            dve.wait_ge(masks, 2)
            dve.tensor_scalar(mask[:, 0], differ[:], 0, None, ALU.is_equal).then_inc(masks, 1)
            for lev in range(LEVELS):
                dve.wait_ge(masks, 3 + 2 * lev)
                dve.tensor_scalar(top[:], differ[:], LEVELS - 1 - lev, None, ALU.logical_shift_right).then_inc(masks, 1)
                dve.wait_ge(masks, 4 + 2 * lev)
                dve.scalar_tensor_tensor(mask[:, lev + 1], top[:], 1, after[:], ALU.is_equal, ALU.mult
                                         ).then_inc(masks, 1)
            dve.wait_ge(masks, 3 + 2 * LEVELS)
            dve.wait_ge(consts, 3)
            dve.wait_ge(cleared, 4)
            dve.engine_nop().then_inc(st_ready, 1)

            def differences(u, s, lev):
                p, w = lev % 2, u * 4 + lev // 2
                dve.wait_ge(exped[p], w)
                if lev == LEVELS:
                    edge = b[:, s, :, C - 1:C].broadcast_to([P, HH, C])
                    dve.tensor_tensor(diff[:, p], edge, b[:, s], ALU.subtract).then_inc(diffed[p], 1)
                    return
                half = C >> (lev + 1)
                bb, dd = blocks_of(b[:, s], lev), blocks_of(diff[:, p], lev)
                edge = bb[:, :, 0, half - 1:half].broadcast_to([P, HH * C // half // 2, half])
                dve.tensor_tensor(dd[:, :, 0], edge, bb[:, :, 0], ALU.subtract)
                dve.tensor_tensor(dd[:, :, 1], bb[:, :, 1], edge, ALU.subtract).then_inc(diffed[p], 1)

            def scale_q(u, c, s, lev):
                p, w = lev % 2, u * 4 + lev // 2
                if lev == LEVELS:
                    dve.wait_ge(b_exped, u + 1)
                    dve.wait_ge(o_full[1 - s], c + s)
                    dve.tensor_tensor(q_dec[:, lev], q_in[:, s], b_exp[:], ALU.mult).then_inc(q_scaled, 1)
                    return
                dve.wait_ge(exped[p], w + 1)
                dve.wait_ge(s_full[(lev + 1) % 4], u * 2)
                o, i, e = (blocks_of(t, lev)[:, :, 1] for t in (q_dec[:, lev], q_in[:, s], decay[:, p]))
                dve.tensor_tensor(o, i, e, ALU.mult).then_inc(q_scaled, 1)

            def pick(u, s, j):
                dve.wait_ge(s_full[j % 4], u * 2 + j // 4 + 1)
                if j:
                    dve.wait_ge(s_read[(j - 1) % 4], u * 2 + (j - 1) // 4 + 1)
                dve.memset(gate[:, j:j + 1], 0.0)
                m = mask[:, j:j + 1].broadcast_to([P, HH, C])
                dve.copy_predicated(s_sb[:, s], m, s_ps[:, j % 4].rearrange("p (h c) -> p h c", h=HH)
                                    ).then_inc(s_read[j % 4], 1)

            def body(u, c, s):
                dve.wait_ge(logged, u + 1)
                dve.tensor_tensor_scan(b[:, s].rearrange("p h c -> p (h c)"), restart[:].rearrange("p h c -> p (h c)"),
                                       f_in[:, s].rearrange("p h c -> p (h c)"), 0.0, ALU.mult, ALU.add
                                       ).then_inc(summed, 1)
                dve.wait_ge(summed, u + 1)
                differences(u, s, 0)
                dve.wait_ge(o_full[s], c)
                for lev in range(LEVELS + 1):
                    if lev < LEVELS:
                        differences(u, s, lev + 1)
                    scale_q(u, c, s, lev)
                    pick(u, s, lev)
                dve.wait_ge(st_full, u + 1)
                dve.wait_ge(o_full[s], c + 1)
                dve.wait_ge(last_exped, u + 1)
                for h in range(HH):
                    i = dve.scalar_tensor_tensor(state[:, h], state[:, h], last_exp[:, h:h + 1], st_ps[:, h * C:(h + 1) * C],
                                                 ALU.mult, ALU.add)
                i.then_inc(st_ready, 1)
                dve.wait_ge(squared, u + 1)
                dve.tensor_reduce(ms[:, 0], squares[:], AX.X, ALU.add).then_inc(chain, 1)
                dve.wait_ge(chain, u * 5 + 1)
                dve.tensor_scalar(ms[:, 0], ms[:, 0], 1 / C, EPS, ALU.mult, ALU.add).then_inc(mean_ready, 1)
                dve.wait_ge(rstd0, u + 1)
                dve.tensor_tensor(ms[:, 3], ms[:, 2], ms[:, 2], ALU.mult).then_inc(chain, 1)
                dve.wait_ge(chain, u * 5 + 2)
                dve.tensor_tensor(ms[:, 3], ms[:, 3], ms[:, 0], ALU.mult).then_inc(chain, 1)
                dve.wait_ge(chain, u * 5 + 3)
                dve.tensor_scalar(ms[:, 3], ms[:, 3], -0.5, 1.5, ALU.mult, ALU.add).then_inc(chain, 1)
                dve.wait_ge(chain, u * 5 + 4)
                dve.tensor_tensor(ms[:, 3], ms[:, 3], ms[:, 2], ALU.mult).then_inc(chain, 1)
                dve.wait_ge(chain, u * 5 + 5)
                dve.wait_ge(gated_ready, u + 1)
                dve.wait_ge(out_stored[s], c * 16)
                for h in range(HH):
                    cols = slice(h * C, (h + 1) * C)
                    i = dve.scalar_tensor_tensor(out[:, s, cols], o_ps[:, s, cols], ms[:, 3, h:h + 1], gated[:, s, cols],
                                                 ALU.mult, ALU.mult)
                i.then_inc(out_ready[s], 1)

            each_chunk(dve, body)

        @block.tensor
        def _(pe):
            pe.wait_ge(cleared, 4)

            def body(u, c, s):
                for j in range(LEVELS + 1):
                    pe.wait_ge(s_read[j % 4], u * 2 + j // 4)
                    if j == 0:
                        pe.wait_ge(in_landed[s], c * 48 + 48)
                        kk, qq = k_in[:, s], q_in[:, s]
                    else:
                        pe.wait_ge(q_scaled, u * 8 + j)
                        pe.wait_ge(k_scaled, u * 8 + j)
                        kk, qq = k_dec[:, j - 1], q_dec[:, j - 1]
                    for h in range(HH):
                        mm = pe.matmul(s_ps[:, j % 4, h * C:(h + 1) * C], kk[:, h], qq[:, h], start=True, stop=True)
                    mm.then_inc(s_full[j % 4], 1)
                pe.wait_ge(k_scaled, u * 8 + 8)
                pe.wait_ge(k_rows_ready, u)
                for h in range(HH):
                    mm = pe.transpose(kt_ps[:, h * C:(h + 1) * C], k_dec[:, LEVELS, h], ident[:])
                mm.then_inc(k_turned, 1)
                pe.wait_ge(q_scaled, u * 8 + 8)
                pe.wait_ge(s_read[3], u * 2 + 2)
                pe.wait_ge(ig_landed[s], c * 16 + 16)
                pe.wait_ge(st_ready, u + 1)
                pe.wait_ge(out_ready[s], c)
                for h in range(HH):
                    cols = slice(h * C, (h + 1) * C)
                    pe.matmul(o_ps[:, s, cols], s_sb[:, s, h], ig_in[:, s, cols], start=True, stop=False)
                    mm = pe.matmul(o_ps[:, s, cols], q_dec[:, LEVELS, h], state[:, h], start=False, stop=True)
                mm.then_inc(o_full[s], 1)
                pe.wait_ge(k_rows_ready, u + 1)
                for h in range(HH):
                    cols = slice(h * C, (h + 1) * C)
                    mm = pe.matmul(st_ps[:, cols], k_rows[:, h], ig_in[:, s, cols], start=True, stop=True)
                mm.then_inc(st_full, 1)

            each_chunk(pe, body)


def merge(nc, branch_rows, y):
    name = "mg"
    B = 3
    with nc.cleanup_on_exit(), ExitStack() as ctx:
        def sb(what, shape, dt=F32):
            return ctx.enter_context(nc.sbuf_tensor(f"{name}_{what}", shape, dt))

        def sem(what):
            return nc.alloc_semaphore(f"{name}_{what}")

        o_in = sb("o_in", [P, 2, B, OW])
        least = sb("least", [P, 2, HEADS])
        gap = sb("gap", [P, 2, B, HEADS])
        total = sb("total", [P, 2, B, HEADS])
        norm = sb("norm", [P, 2, HEADS])
        scaled = sb("scaled", [P, 2, B, AW])
        pair = sb("pair", [P, 2, AW])
        out = sb("out", [P, 2, AW])

        landed = [sem(f"landed{s}") for s in range(2)]
        chain = sem("chain")
        gap_ready = sem("gap_ready")
        exped = sem("exped")
        scaled_ready = sem("scaled_ready")
        paired = sem("paired")
        out_ready = [sem(f"out_ready{s}") for s in range(2)]
        out_stored = [sem(f"out_stored{s}") for s in range(2)]
        block = ctx.enter_context(nc.Block())

        def each_tile(eng, body):
            with eng.Fori(0, SEQ // P // 2) as c:
                for s in range(2):
                    body(c * 2 + s, c, s)

        @block.sync
        def _(sp):
            def body(u, c, s):
                sp.wait_ge(out_ready[s], c)
                for b in range(B):
                    sp.dma_start(o_in[:, s, b], branch_rows[b][bass.ds(u * P, P), :]).then_inc(landed[s], 16)
            each_tile(sp, body)
            for s in range(2):
                sp.wait_ge(out_stored[s], 16 * 8)

        @block.vector
        def _(dve):
            def body(u, c, s):
                n = u * 6
                dve.wait_ge(landed[s], c * 48 + 48)
                minus_max, weights = o_in[:, s, :, AW:AW + HEADS], o_in[:, s, :, AW + HEADS:OW]
                dve.tensor_tensor(least[:, s], minus_max[:, 0], minus_max[:, 1], ALU.min).then_inc(chain, 1)
                dve.wait_ge(chain, n + 1)
                dve.tensor_tensor(least[:, s], least[:, s], minus_max[:, 2], ALU.min).then_inc(chain, 1)
                dve.wait_ge(chain, n + 2)
                dve.tensor_tensor(gap[:, s], least[:, s:s + 1].broadcast_to([P, B, HEADS]), minus_max,
                                  ALU.subtract).then_inc(gap_ready, 1)
                dve.wait_ge(exped, u + 1)
                dve.tensor_tensor(total[:, s], gap[:, s], weights, ALU.mult).then_inc(chain, 1)
                dve.wait_ge(chain, n + 3)
                dve.tensor_reduce(norm[:, s], total[:, s].rearrange("p b h -> p h b"), AX.X, ALU.add).then_inc(chain, 1)
                dve.wait_ge(chain, n + 4)
                dve.reciprocal(norm[:, s], norm[:, s]).then_inc(chain, 1)
                dve.wait_ge(chain, n + 5)
                dve.tensor_tensor(gap[:, s], gap[:, s], norm[:, s:s + 1].broadcast_to([P, B, HEADS]), ALU.mult
                                  ).then_inc(chain, 1)
                dve.wait_ge(chain, n + 6)
                dve.wait_ge(out_ready[s], c)
                for b in range(B):
                    i = dve.tensor_tensor(scaled[:, s, b].rearrange("p (h e) -> p h e", e=HD),
                                          o_in[:, s, b, 0:AW].rearrange("p (h e) -> p h e", e=HD),
                                          gap[:, s, b].unsqueeze(2).broadcast_to([P, HEADS, HD]), ALU.mult)
                i.then_inc(scaled_ready, 1)

            each_tile(dve, body)

        @block.gpsimd
        def _(pool):
            def body(u, c, s):
                pool.wait_ge(scaled_ready, u + 1)
                pool.tensor_tensor(pair[:, s], scaled[:, s, 0], scaled[:, s, 1], ALU.add).then_inc(paired, 1)
                pool.wait_ge(paired, u + 1)
                pool.wait_ge(out_stored[s], c * 16)
                pool.tensor_tensor(out[:, s], pair[:, s], scaled[:, s, 2], ALU.add).then_inc(out_ready[s], 1)
            each_tile(pool, body)

        @block.scalar
        def _(act):
            def body(u, c, s):
                act.wait_ge(gap_ready, u + 1)
                act.activation(gap[:, s], gap[:, s], ACT.Exp).then_inc(exped, 1)
                act.wait_ge(out_ready[s], c + 1)
                act.dma_start(y[bass.ds(u * P, P), 0:AW], out[:, s]).then_inc(out_stored[s], 16)
            each_tile(act, body)


MEM, MH, MD = 256, 4, 256


def attend_memory(nc, qm, kvm, om, q_gain, k_gain, ident):
    name = "ma"
    M2 = MEM // P
    with nc.cleanup_on_exit(), ExitStack() as ctx:
        def sb(what, shape, dt=F32):
            return ctx.enter_context(nc.sbuf_tensor(f"{name}_{what}", shape, dt))

        def ps(what, shape):
            return ctx.enter_context(nc.psum_tensor(f"{name}_{what}", shape, F32))

        def sem(what):
            return nc.alloc_semaphore(f"{name}_{what}")

        gains = sb("gains", [P, 2, MD // P])
        gain = sb("gain", [P, MD // P])
        k_in = sb("k_in", [P, M2, D])
        v_in = sb("v_in", [P, M2, D])
        k_t = sb("k_t", [P, KT, MEM])
        q_in = sb("q_in", [P, 2, D])
        q_t = sb("q_t", [P, 2, KT, P])
        top = sb("top", [P, 2, MH])
        minus = sb("minus", [P, 2, MH])
        weight = sb("weight", [P, 2, MH])
        inverse = sb("inverse", [P, 2, MH])
        p_sb = sb("p", [P, 2, MEM])
        pt_sb = sb("pt_sb", [P, 2, M2, P])
        o_sb = sb("o", [P, 2, D])
        turn = ps("turn", [P, 2, BANK])
        score = ps("score", [P, 2, BANK])
        pt = ps("pt", [P, 2, BANK])
        o_ps = ps("o_ps", [P, 2, BANK])

        const_landed = sem("const_landed")
        gain_ready = sem("gain_ready")
        k_turned = sem("k_turned")
        k_ready = sem("k_ready")
        q_landed = [sem(f"q_landed{s}") for s in range(2)]
        q_turned = [sem(f"q_turned{i}") for i in range(2)]
        q_ready = [sem(f"q_ready{i}") for i in range(2)]
        s_full = [sem(f"s_full{p}") for p in range(2)]
        topped = [sem(f"topped{p}") for p in range(2)]
        minus_ready = [sem(f"minus_ready{p}") for p in range(2)]
        exped = [sem(f"exped{p}") for p in range(2)]
        inverted = [sem(f"inverted{p}") for p in range(2)]
        pt_full = [sem(f"pt_full{p}") for p in range(2)]
        pt_read = [sem(f"pt_read{p}") for p in range(2)]
        o_full = [sem(f"o_full{p}") for p in range(2)]
        o_read = [sem(f"o_read{p}") for p in range(2)]
        o_stored = [sem(f"o_stored{s}") for s in range(2)]
        block = ctx.enter_context(nc.Block())

        def each_tile(eng, body):
            with eng.Fori(0, SEQ // P // 2) as c:
                for s in range(2):
                    body(c * 2 + s, c, s)

        @block.sync
        def _(sp):
            for i, g in enumerate((q_gain, k_gain)):
                for t in range(MD // P):
                    sp.dma_start(gains[:, i, t:t + 1], g[t * P:(t + 1) * P, :]).then_inc(const_landed, 16)
            for m in range(M2):
                sp.dma_start(k_in[:, m], kvm[m * P:(m + 1) * P, 0:D]).then_inc(const_landed, 16)
                sp.dma_start(v_in[:, m], kvm[m * P:(m + 1) * P, D:2 * D]).then_inc(const_landed, 16)

            def body(u, c, s):
                sp.wait_ge(q_ready[1], u)
                sp.dma_start(q_in[:, s], qm[bass.ds(u * P, P), :]).then_inc(q_landed[s], 16)
            each_tile(sp, body)
            for s in range(2):
                sp.wait_ge(o_stored[s], 16 * 8)

        @block.vector
        def _(dve):
            dve.wait_ge(const_landed, 16 * (4 + 2 * M2))
            dve.scalar_tensor_tensor(gain[:], gains[:, 0], 1 / math.sqrt(MD), gains[:, 1], ALU.mult, ALU.mult
                                     ).then_inc(gain_ready, 1)
            dve.wait_ge(gain_ready, 1)
            for i in range(2 * M2):
                m, b = divmod(i, 2)
                dve.wait_ge(k_turned, i + 1)
                for j in range(4):
                    at = 4 * b + j
                    x = dve.tensor_scalar(k_t[:, at, m * P:(m + 1) * P], turn[:, b, j * P:(j + 1) * P],
                                          gain[:, at % 2:at % 2 + 1], None, ALU.mult)
                x.then_inc(k_ready, 1)

            def body(u, c, s):
                for e in range(MH):
                    p, w = e % 2, u * 2 + e // 2
                    if e == 0:
                        dve.wait_ge(o_stored[s], c * 16)
                    dve.wait_ge(s_full[p], w + 1)
                    dve.tensor_reduce(top[:, s, e:e + 1], score[:, p, 0:MEM], AX.X, ALU.max).then_inc(topped[p], 1)
                    dve.wait_ge(topped[p], w + 1)
                    dve.tensor_scalar(minus[:, s, e:e + 1], top[:, s, e:e + 1], -1.0, None, ALU.mult
                                      ).then_inc(minus_ready[p], 1)
                    if e:
                        finish(u, s, e - 1)
                finish(u, s, MH - 1)

            def finish(u, s, e):
                p, w = e % 2, u * 2 + e // 2
                dve.wait_ge(exped[p], w + 1)
                dve.reciprocal(inverse[:, s, e:e + 1], weight[:, s, e:e + 1]).then_inc(inverted[p], 1)
                dve.wait_ge(pt_full[p], w + 1)
                dve.wait_ge(o_full[p], w)
                dve.tensor_copy(pt_sb[:, p], pt[:, p, 0:MEM].rearrange("p (k c) -> p k c", c=P)).then_inc(pt_read[p], 1)

            each_tile(dve, body)

        @block.scalar
        def _(act):
            def body(u, c, s):
                for i in range(2):
                    act.wait_ge(q_turned[i], u + 1)
                    act.activation(q_t[:, s, 4 * i:4 * i + 4], turn[:, i].rearrange("p (k c) -> p k c", k=4), ACT.Copy
                                   ).then_inc(q_ready[i], 1)
                for e in range(MH):
                    p, w = e % 2, u * 2 + e // 2
                    act.wait_ge(minus_ready[p], w + 1)
                    act.wait_ge(pt_full[p], w)
                    act.activation(p_sb[:, p], score[:, p, 0:MEM], ACT.Exp, bias=minus[:, s, e:e + 1],
                                   accum_out=weight[:, s, e:e + 1]).then_inc(exped[p], 1)
                    if e:
                        finish(u, c, s, e - 1)
                finish(u, c, s, MH - 1)
                for p in range(2):
                    act.wait_ge(o_read[p], u * 2 + 2)
                act.dma_start(om[bass.ds(u * P, P), :], o_sb[:, s]).then_inc(o_stored[s], 16)

            def finish(u, c, s, e):
                p, w = e % 2, u * 2 + e // 2
                act.wait_ge(o_full[p], w + 1)
                act.wait_ge(inverted[p], w + 1)
                act.wait_ge(o_stored[s], c * 16)
                act.activation(o_sb[:, s, e * MD:(e + 1) * MD], o_ps[:, p, 0:MD], ACT.Copy,
                               scale=inverse[:, s, e:e + 1]).then_inc(o_read[p], 1)

            each_tile(act, body)

        @block.tensor
        def _(pe):
            pe.wait_ge(const_landed, 16 * (4 + 2 * M2))
            for i in range(2 * M2):
                m, b = divmod(i, 2)
                if i >= 2:
                    pe.wait_ge(k_ready, i - 1)
                for j in range(4):
                    at = (4 * b + j) * P
                    mm = pe.transpose(turn[:, b, j * P:(j + 1) * P], k_in[:, m, at:at + P], ident[:])
                mm.then_inc(k_turned, 1)
            pe.wait_ge(k_ready, 2 * M2)

            def body(u, c, s):
                pe.wait_ge(q_landed[s], c * 16 + 16)
                for i in range(2):
                    pe.wait_ge(q_ready[i], u)
                    for j in range(4):
                        at = (4 * i + j) * P
                        mm = pe.transpose(turn[:, i, j * P:(j + 1) * P], q_in[:, s, at:at + P], ident[:])
                    mm.then_inc(q_turned[i], 1)
                scores(u, s, 0)
                for e in range(MH):
                    if e + 1 < MH:
                        scores(u, s, e + 1)
                    p, w = e % 2, u * 2 + e // 2
                    pe.wait_ge(exped[p], w + 1)
                    pe.wait_ge(pt_read[p], w)
                    for m in range(M2):
                        mm = pe.transpose(pt[:, p, m * P:(m + 1) * P], p_sb[:, p, m * P:(m + 1) * P], ident[:])
                    mm.then_inc(pt_full[p], 1)
                    pe.wait_ge(pt_read[p], w + 1)
                    pe.wait_ge(o_read[p], w)
                    for m in range(M2):
                        mm = pe.matmul(o_ps[:, p, 0:MD], pt_sb[:, p, m], v_in[:, m, e * MD:(e + 1) * MD],
                                       start=(m == 0), stop=(m == M2 - 1))
                    mm.then_inc(o_full[p], 1)

            def scores(u, s, e):
                p, w = e % 2, u * 2 + e // 2
                pe.wait_ge(q_ready[e // 2], u + 1)
                pe.wait_ge(exped[p], w)
                for i in range(MD // P):
                    at = e * (MD // P) + i
                    mm = pe.matmul(score[:, p, 0:MEM], q_t[:, s, at], k_t[:, at], start=(i == 0), stop=(i == 1))
                mm.then_inc(s_full[p], 1)

            each_tile(pe, body)


def feed_forward(nc, src, gain, w1, w2, dst, ident):
    name = "ff"
    S = src.shape[0]
    T = BANK
    groups, tiles = S // T, T // P
    QUARTERS = w1.shape[1] // D
    PER = 4
    with nc.cleanup_on_exit(), ExitStack() as ctx:
        def sb(what, shape, dt=F32):
            return ctx.enter_context(nc.sbuf_tensor(f"{name}_{what}", shape, dt))

        def ps(what, shape):
            return ctx.enter_context(nc.psum_tensor(f"{name}_{what}", shape, F32))

        def sem(what):
            return nc.alloc_semaphore(f"{name}_{what}")

        x_in = sb("x_in", [P, 2, D])
        junk = sb("junk", [P, D])
        sumsq = sb("sumsq", [P, 2])
        root = sb("root", [P, 2])
        scratch = sb("scratch", [P, 2])
        eps = sb("eps", [P, 1])
        rstd = sb("rstd", [P, 2])
        h = sb("h", [P, 2, D])
        g_rep = sb("g_rep", [P, D])
        a_hi = [sb(f"a_hi{s}", [P, KT, T], F32R) for s in range(2)]
        a_lo = [sb(f"a_lo{s}", [P, KT, T], F32R) for s in range(2)]
        raw = sb("raw", [P, 2, HK, BANK])
        w_hi = sb("w_hi", [P, 2, HK, BANK], F32R)
        w_lo = sb("w_lo", [P, 2, HK, BANK], F32R)
        relu = sb("relu", [P, 2, BANK])
        square_sb = sb("square", [P, 2, BANK])
        u_hi = sb("u_hi", [P, KT, T], F32R)
        u_lo = sb("u_lo", [P, KT, T], F32R)
        total = sb("total", [P, tiles, D])
        acc = ps("acc", [P, 4, BANK])
        turn = ps("turn", [P, 2, BANK])

        eps_ready = sem("eps_ready")
        gain_landed = sem("gain_landed")
        gain_ready = sem("gain_ready")
        x_landed = [sem(f"x_landed{s}") for s in range(2)]
        sumsq_ready = sem("sumsq_ready")
        root_ready = sem("root_ready")
        rstd_chain = sem("rstd_chain")
        rstd_ready = sem("rstd_ready")
        h_ready = sem("h_ready")
        turned = sem("turned")
        a_hi_ready = sem("a_hi_ready")
        a_ready = sem("a_ready")
        raw_landed = [sem(f"raw_landed{s}") for s in range(2)]
        w_hi_ready = [sem(f"w_hi_ready{s}") for s in range(2)]
        w_ready = [sem(f"w_ready{s}") for s in range(2)]
        first_half_used = sem("first_half_used")
        acc_full = [sem(f"acc_full{t}") for t in range(tiles)]
        acc_read = [sem(f"acc_read{t}") for t in range(tiles)]
        squared = [sem(f"squared{s}") for s in range(2)]
        u_hi_ready = [sem(f"u_hi_ready{s}") for s in range(2)]
        u_ready = sem("u_ready")
        total_landed = sem("total_landed")
        stored = sem("stored")
        block = ctx.enter_context(nc.Block())

        src_tiles = src.rearrange("(n p) d -> n p d", p=P)
        w1_rows = w1.rearrange("(h k p) c -> h p k c", k=HK, p=P)

        def each_quarter(eng, g, body):
            with eng.Fori(0, QUARTERS - 1) as q:
                body(q, q + g * QUARTERS, False)
            body(QUARTERS - 1, (g + 1) * QUARTERS - 1, True)

        def prepares(g, last, i):
            return last and g + 1 < groups and i == 0

        @block.sync
        def _(sp):
            sp.dma_start(g_rep[:], gain.broadcast_to([P, D])).then_inc(gain_landed, 16)

            def load_rows(n):
                if n >= 2:
                    sp.wait_ge(h_ready, n - 1)
                sp.dma_start(x_in[:, n % 2, :], src_tiles[n]).then_inc(x_landed[n % 2], 16)

            def quarter(g):
                def body(q, n, last):
                    for i in range(PER):
                        for half in range(2):
                            sp.wait_ge(w_ready[half], n * PER + i)
                            if i < 2:
                                w = w1_rows[half, :, :, bass.ds(q * D + i * BANK, BANK)]
                            else:
                                w = w2[bass.ds(q * D + half * BANK, BANK), (i - 2) * BANK:(i - 1) * BANK
                                       ].rearrange("(k p) c -> p k c", p=P)
                            sp.dma_start(raw[:, half], w).then_inc(raw_landed[half], 16)
                        if prepares(g, last, i):
                            for t in range(tiles):
                                load_rows((g + 1) * tiles + t)
                return body

            for t in range(tiles):
                load_rows(t)
            for g in range(groups):
                each_quarter(sp, g, quarter(g))
            sp.wait_ge(stored, groups * tiles * 16)

        @block.gpsimd
        def _(pool):
            def body(q, n, last):
                for i in range(PER):
                    for half in range(2):
                        m = n * PER + i
                        pool.wait_ge(w_hi_ready[half], m + 1)
                        pool.tensor_tensor(w_lo[:, half], raw[:, half], w_hi[:, half].bitcast(F32), ALU.subtract
                                           ).then_inc(w_ready[half], 1)
            for g in range(groups):
                each_quarter(pool, g, body)

        @block.scalar
        def _(act):
            def square(n):
                act.wait_ge(x_landed[n % 2], 16 * (n // 2 + 1))
                if n >= 1:
                    act.wait_ge(sumsq_ready, n)
                if n >= 2:
                    act.wait_ge(rstd_ready, n - 1)
                at = slice(n % 2, n % 2 + 1)
                act.activation(junk[:], x_in[:, n % 2, :], ACT.Square, accum_out=sumsq[:, at]
                               ).then_inc(sumsq_ready, 1)
                act.wait_ge(sumsq_ready, n + 1)
                act.activation(root[:, at], sumsq[:, at], ACT.Sqrt, bias=eps[:]).then_inc(root_ready, 1)

            def high_part(n, b):
                act.wait_ge(turned, 2 * n + b + 1)
                g, t = divmod(n, tiles)
                act.activation(a_hi[g % 2][:, b * HK:(b + 1) * HK, t * P:(t + 1) * P],
                               turn[:, b].rearrange("p (k c) -> p k c", k=HK), ACT.Copy
                               ).then_inc(a_hi_ready, 1)

            def high_square(n, i, t):
                s, m = t % 2, n * 4 + i * 2 + t // 2
                act.wait_ge(squared[s], m + 1)
                act.activation(u_hi[:, i * tiles + t], square_sb[:, s], ACT.Copy).then_inc(u_hi_ready[s], 1)

            def quarter(g):
                def body(q, n, last):
                    for i in range(PER):
                        for step in range(2 * tiles):
                            if prepares(g, last, i):
                                at = (g + 1) * tiles + step // 2
                                if step == 0:
                                    square(at)
                                if step % 2 == 0 and step < 2 * tiles - 2:
                                    square(at + 1)
                                high_part(at, step % 2)
                            t = step - tiles
                            if t < 0 or i >= 2:
                                continue
                            m = n * 4 + i * 2 + t // 2
                            act.wait_ge(acc_full[t], n * PER + i + 1)
                            act.wait_ge(squared[t % 2], m)
                            act.activation(relu[:, t % 2], acc[:, t], ACT.Relu).then_inc(acc_read[t], 1)
                            if t:
                                high_square(n, i, t - 1)
                        if i < 2:
                            high_square(n, i, tiles - 1)
                    if last:
                        for t in range(tiles):
                            act.wait_ge(acc_read[t], (n + 1) * PER)
                            act.dma_start(dst[(g * tiles + t) * P:(g * tiles + t + 1) * P, :], total[:, t]
                                          ).then_inc(stored, 16)
                return body

            act.wait_ge(eps_ready, 1)
            for n in range(tiles):
                square(n)
                high_part(n, 0)
                high_part(n, 1)
            for g in range(groups):
                act.wait_ge(stored, g * tiles * 16)
                for t in range(tiles):
                    act.dma_start(total[:, t], src_tiles[g * tiles + t]).then_inc(total_landed, 16)
                each_quarter(act, g, quarter(g))

        @block.vector
        def _(dve):
            dve.memset(eps[:], D * EPS).then_inc(eps_ready, 1)
            dve.wait_ge(gain_landed, 16)
            dve.tensor_scalar(g_rep[:], g_rep[:], math.sqrt(D), None, ALU.mult).then_inc(gain_ready, 1)
            dve.wait_ge(gain_ready, 1)

            def normalise(n):
                if n >= 2:
                    dve.wait_ge(turned, 2 * (n - 1))
                s = slice(n % 2, n % 2 + 1)
                dve.wait_ge(root_ready, n + 1)
                dve.tensor_scalar(sumsq[:, s], sumsq[:, s], D * EPS, None, ALU.add).then_inc(rstd_chain, 1)
                dve.reciprocal(rstd[:, s], root[:, s]).then_inc(rstd_chain, 1)
                dve.wait_ge(rstd_chain, n * 6 + 2)
                newton(dve, rstd_chain, n * 6 + 2, rstd[:, s], sumsq[:, s], scratch[:, s])
                dve.engine_nop().then_inc(rstd_ready, 1)
                dve.wait_ge(rstd_ready, n + 1)
                dve.scalar_tensor_tensor(h[:, n % 2], x_in[:, n % 2], rstd[:, s], g_rep[:],
                                         ALU.mult, ALU.mult).then_inc(h_ready, 1)

            def low_part(n, b):
                dve.wait_ge(a_hi_ready, 2 * n + b + 1)
                g, t = divmod(n, tiles)
                at = (slice(None), slice(b * HK, (b + 1) * HK), slice(t * P, (t + 1) * P))
                dve.tensor_tensor(a_lo[g % 2][at], turn[:, b].rearrange("p (k c) -> p k c", k=HK),
                                  a_hi[g % 2].bitcast(F32)[at], ALU.subtract).then_inc(a_ready, 1)

            def split_weights(m, half):
                dve.wait_ge(raw_landed[half], m * 16 + 16)
                dve.wait_ge(acc_full[tiles - 1] if half else first_half_used, m)
                dve.tensor_copy(w_hi[:, half], raw[:, half]).then_inc(w_hi_ready[half], 1)

            def low_square(n, i, t):
                s, m = t % 2, n * 4 + i * 2 + t // 2
                dve.wait_ge(u_hi_ready[s], m + 1)
                dve.tensor_tensor(u_lo[:, i * tiles + t], square_sb[:, s], u_hi[:, i * tiles + t].bitcast(F32),
                                  ALU.subtract).then_inc(u_ready, 1)

            def quarter(g):
                def body(q, n, last):
                    for i in range(PER):
                        c = n * PER + i
                        for step in range(2 * tiles):
                            if step == 0:
                                split_weights(c, 1)
                            elif step == tiles and not (last and g + 1 == groups and i == PER - 1):
                                split_weights(c + 1, 0)
                            if prepares(g, last, i):
                                at = (g + 1) * tiles + step // 2
                                if step % 2 == 0:
                                    normalise(at)
                                low_part(at, step % 2)
                            t = step - tiles
                            if t < 0:
                                continue
                            if i < 2:
                                m = n * 4 + i * 2 + t // 2
                                dve.wait_ge(acc_read[t], c + 1)
                                dve.wait_ge(u_ready, n * 2 * tiles + i * tiles + max(t - 1, 0))
                                dve.tensor_tensor(square_sb[:, t % 2], relu[:, t % 2], relu[:, t % 2], ALU.mult
                                                  ).then_inc(squared[t % 2], 1)
                                if t:
                                    low_square(n, i, t - 1)
                            else:
                                dve.wait_ge(acc_full[t], c + 1)
                                dve.wait_ge(total_landed, (g + 1) * tiles * 16)
                                at = (slice(None), t, slice((i - 2) * BANK, (i - 1) * BANK))
                                dve.tensor_tensor(total[at], acc[:, t], total[at], ALU.add).then_inc(acc_read[t], 1)
                        if i < 2:
                            low_square(n, i, tiles - 1)
                return body

            for n in range(tiles):
                normalise(n)
                low_part(n, 0)
                low_part(n, 1)
            split_weights(0, 0)
            for g in range(groups):
                each_quarter(dve, g, quarter(g))

        @block.tensor
        def _(pe):
            def turn_rows(n, b):
                pe.wait_ge(h_ready, n + 1)
                if n >= 1:
                    pe.wait_ge(a_ready, 2 * (n - 1) + b + 1)
                for k in range(HK):
                    at = (b * HK + k) * P
                    mm = pe.transpose(turn[:, b, k * P:(k + 1) * P], h[:, n % 2, at:at + P], ident[:])
                mm.then_inc(turned, 1)

            def products(i, s, half, t, n):
                cut = slice(t * P, (t + 1) * P)
                for k in range(HK):
                    a = half * HK + k
                    if i < 2:
                        terms = [(w_hi[:, half, k, cut], a_hi[s][:, a]), (w_hi[:, half, k, cut], a_lo[s][:, a]),
                                 (w_lo[:, half, k, cut], a_hi[s][:, a])]
                    else:
                        if t == 0:
                            pe.wait_ge(u_ready, n * 2 * tiles + a + 1)
                        terms = [(u_hi[:, a, cut], w_hi[:, half, k]), (u_hi[:, a, cut], w_lo[:, half, k]),
                                 (u_lo[:, a, cut], w_hi[:, half, k])]
                    for j, (left, right) in enumerate(terms):
                        mm = pe.matmul(acc[:, t], left, right, start=(half == 0 and k == 0 and j == 0),
                                       stop=(half == 1 and k == HK - 1 and j == 2))
                return mm

            def quarter(g):
                def body(q, n, last):
                    for i in range(PER):
                        c = n * PER + i
                        for half in range(2):
                            pe.wait_ge(w_ready[half], c + 1)
                            for t in range(tiles):
                                if half == 0:
                                    pe.wait_ge(acc_read[t], c)
                                mm = products(i, g % 2, half, t, n)
                                if half == 1:
                                    mm.then_inc(acc_full[t], 1)
                                elif t == tiles - 1:
                                    mm.then_inc(first_half_used, 1)
                                if prepares(g, last, i):
                                    step = half * tiles + t
                                    turn_rows((g + 1) * tiles + step // 2, step % 2)
                return body

            for n in range(tiles):
                turn_rows(n, 0)
                turn_rows(n, 1)
            for g in range(groups):
                pe.wait_ge(a_ready, 2 * (g + 1) * tiles)
                each_quarter(pe, g, quarter(g))


def decoder_layer(nc, x, mem, norm1_g, w_in, attn_qn_g, attn_kn_g, hg_lb, hg_onorm_g, w_out, norm2_g, mem_norm_g,
                  w_mq, w_mkv, mq_norm_g, mk_norm_g, w_mo, norm3_g, w_ff1, w_ff2, out):
    S = x.shape[0]
    groups = S // BANK

    def scratch(what, rows, cols):
        return nc.dram_tensor(what, [rows, cols], F32, kind="Internal").ap()

    z_rows = scratch("z_rows", S, 2560)
    z_columns = scratch("z_columns", 1536, S)
    branch_rows = [scratch(f"branch{b}", S, 528) for b in range(3)]
    y = scratch("y", S, D)
    x1 = scratch("x1", S, D)
    kvm = scratch("kvm", MEM, 2 * D)
    qm = scratch("qm", S, D)
    om = scratch("om", S, D)
    x2 = scratch("x2", S, D)

    with nc.cleanup_on_exit(), ExitStack() as ctx:
        ident = ctx.enter_context(nc.sbuf_tensor("ident", [P, P], F32))
        lb = ctx.enter_context(nc.sbuf_tensor("lb", [P, 4], F32))
        lb_exp = ctx.enter_context(nc.sbuf_tensor("lb_exp", [P, 4], F32))
        lb_p = ctx.enter_context(nc.sbuf_tensor("lb_p", [P, 4], F32))
        lower = ctx.enter_context(nc.sbuf_tensor("lower", [P, 4], F32))
        upper = ctx.enter_context(nc.sbuf_tensor("upper", [P, 4], F32))
        cleared = nc.alloc_semaphore("ident_cleared")
        ident_ready = nc.alloc_semaphore("ident_ready")
        lb_landed = nc.alloc_semaphore("lb_landed")
        lb_chain = nc.alloc_semaphore("lb_chain")
        lb_exped = nc.alloc_semaphore("lb_exped")
        with nc.Block() as block:
            @block.sync
            def _(sp):
                for t in range(4):
                    sp.dma_start(lb[:, t:t + 1], hg_lb[t * P:(t + 1) * P, :]).then_inc(lb_landed, 16)

            @block.gpsimd
            def _(pool):
                pool.memset(ident[:], 0.0).then_inc(cleared, 1)
                pool.wait_ge(cleared, 1)
                pool.affine_select(out=ident[:], in_=ident[:], compare_op=ALU.not_equal, fill=1.0, base=0,
                                   pattern=[[-1, P]], channel_multiplier=1).then_inc(ident_ready, 1)

            @block.vector
            def _(dve):
                dve.wait_ge(lb_landed, 64)
                dve.tensor_tensor(lb_exp[:], lb[:], lb[:], ALU.subtract).then_inc(lb_chain, 1)
                dve.wait_ge(lb_exped, 1)
                dve.reciprocal(lb_p[:], lb_exp[:]).then_inc(lb_chain, 1)
                dve.wait_ge(lb_chain, 2)
                dve.tensor_tensor(lb_p[:], lb_p[:], lb_exp[:], ALU.mult).then_inc(lb_chain, 1)
                dve.wait_ge(lb_chain, 3)
                dve.tensor_tensor(lower[:], lb_p[:], lb_p[:], ALU.subtract).then_inc(lb_chain, 1)
                dve.wait_ge(lb_chain, 4)
                dve.tensor_scalar(upper[:], lower[:], -1.0, 1.0, ALU.mult, ALU.add).then_inc(lb_chain, 1)

            @block.scalar
            def _(act):
                act.wait_ge(lb_chain, 1)
                act.activation(lb_exp[:], lb_exp[:], ACT.Exp).then_inc(lb_exped, 1)

        project(nc, "in", x, norm1_g, w_in,
                [("heads 64", 0, 2, z_rows, 0), ("rows", 2, 1, z_rows, 2), ("silu columns", 3, 1, z_columns, 0),
                 ("gates", 4, 1, (z_columns[BANK:2 * BANK], z_columns[2 * BANK:3 * BANK]), 0),
                 ("rows", 5, 1, z_rows, 3), ("silu rows", 6, 1, z_rows, 4)],
                groups, 4, ident, lower=(lower, upper))
        attend(nc, z_rows, branch_rows, attn_qn_g, attn_kn_g, ident)
        recur(nc, z_columns, z_rows, y, hg_onorm_g, ident)
        merge(nc, branch_rows, y)
        project(nc, "mkv", mem, mem_norm_g, w_mkv, [("heads 256", 0, 2, kvm, 0), ("rows", 2, 2, kvm, 2)], 1, 2, ident)
        project(nc, "out", y, None, w_out, [("rows", 0, 2, x1, 0)], groups, 4, ident, residual=x)
        project(nc, "mq", x1, norm2_g, w_mq, [("heads 256", 0, 2, qm, 0)], groups, 4, ident)
        attend_memory(nc, qm, kvm, om, mq_norm_g, mk_norm_g, ident)
        project(nc, "mo", om, None, w_mo, [("rows", 0, 2, x2, 0)], groups, 4, ident, residual=x1)
        feed_forward(nc, x2, norm3_g, w_ff1, w_ff2, out, ident)


_SHAPES = {
    "x": (2048, 1024), "mem": (256, 1024), "norm1_g": (1, 1024), "w_in": (1024, 3584), "attn_qn_g": (64, 1),
    "attn_kn_g": (64, 1), "hg_lb": (512, 1), "hg_onorm_g": (1, 512), "w_out": (1024, 1024), "norm2_g": (1, 1024),
    "mem_norm_g": (1, 1024), "w_mq": (1024, 1024), "w_mkv": (1024, 2048), "mq_norm_g": (256, 1),
    "mk_norm_g": (256, 1), "w_mo": (1024, 1024), "norm3_g": (1, 1024), "w_ff1": (1024, 4096), "w_ff2": (4096, 1024),
}


def kernel(**inputs):
    import numpy as _np
    import concourse.bacc as _bacc
    from concourse import mybir as _mybir
    from concourse.bass_utils import run_bass_kernel_spmd as _run

    nc = _bacc.Bacc("TRN2", target_bir_lowering=False, num_devices=1)
    arrays, args = {}, []
    for name, shape in _SHAPES.items():
        a = _np.ascontiguousarray(inputs[name]).reshape(shape)
        arrays[f"in_{name}"] = a
        args.append(nc.dram_tensor(f"in_{name}", shape, _mybir.dt.from_np(a.dtype), kind="ExternalInput").ap())
    args.append(nc.dram_tensor("out_0", (2048, 1024), F32, kind="ExternalOutput").ap())
    decoder_layer(nc, *args)
    r = _run(nc, [arrays], core_ids=[0])
    return r.results[0]["out_0"].reshape(1, 2048, 1024)
```

```python
import math

import concourse.bass as bass
from concourse import mybir
from contextlib import ExitStack

F32 = mybir.dt.float32
F32R = mybir.dt.float32r
ALU = mybir.AluOpType
ACT = mybir.ActivationFunctionType
AX = mybir.AxisListType

P = 128
BANK = 512
D = 1024
KT = D // P
HK = KT // 2
EPS = 1e-6
F_MIN = 1e-12


def newton(dve, chain, at, r, v, t):
    dve.tensor_tensor(t, r, r, ALU.mult).then_inc(chain, 1)
    dve.wait_ge(chain, at + 1)
    dve.tensor_tensor(t, t, v, ALU.mult).then_inc(chain, 1)
    dve.wait_ge(chain, at + 2)
    dve.tensor_scalar(t, t, -0.5, 1.5, ALU.mult, ALU.add).then_inc(chain, 1)
    dve.wait_ge(chain, at + 3)
    dve.tensor_tensor(r, r, t, ALU.mult).then_inc(chain, 1)
    dve.wait_ge(chain, at + 4)


def project(nc, name, src, gain, weight, plan, groups, tiles, ident, residual=None, lower=None):
    T = tiles * P
    chunks = sum(p[2] for p in plan)
    kinds = {p[0].split()[0]: sum(q[2] for q in plan if q[0].split()[0] == p[0].split()[0]) for p in plan}
    head_width = next((int(p[0].split()[1]) for p in plan if p[0].startswith("heads")), BANK)
    NH = BANK // head_width
    with nc.cleanup_on_exit(), ExitStack() as ctx:
        def sb(what, shape, dt=F32):
            return ctx.enter_context(nc.sbuf_tensor(f"{name}_{what}", shape, dt))

        def ps(what, shape):
            return ctx.enter_context(nc.psum_tensor(f"{name}_{what}", shape, F32))

        def sem(what):
            return nc.alloc_semaphore(f"{name}_{what}")

        x_in = sb("x_in", [P, 2, D])
        junk = sb("junk", [P, D])
        sumsq = sb("sumsq", [P, 2])
        root = sb("root", [P, 2])
        scratch = sb("scratch", [P, 2])
        eps = sb("eps", [P, 1])
        rstd = sb("rstd", [P, 2])
        h = sb("h", [P, 2, D]) if gain is not None else x_in
        g_rep = sb("g_rep", [P, D])
        a_hi = [sb(f"a_hi{s}", [P, KT, T], F32R) for s in range(2)]
        a_lo = [sb(f"a_lo{s}", [P, KT, T], F32R) for s in range(2)]
        raw = sb("raw", [P, 2, HK, BANK])
        w_hi = sb("w_hi", [P, 2, HK, BANK], F32R)
        w_lo = sb("w_lo", [P, 2, HK, BANK], F32R)
        out_sb = sb("out", [P, tiles, BANK])
        res = sb("res", [P, tiles, BANK]) if residual is not None else None
        side = sb("side", [P, 2, BANK])
        keys = sb("keys", [P, tiles, BANK]) if "gates" in kinds else None
        head_sum = sb("head_sum", [P, 2, NH])
        head_rstd = sb("head_rstd", [P, 2, NH])
        head_scratch = sb("head_scratch", [P, 2, NH])
        acc = ps("acc", [P, 4, BANK])
        turn = ps("turn", [P, 2, BANK])

        gain_landed = sem("gain_landed")
        gain_ready = sem("gain_ready")
        x_landed = [sem(f"x_landed{s}") for s in range(2)]
        sumsq_ready = sem("sumsq_ready")
        eps_ready = sem("eps_ready")
        root_ready = sem("root_ready")
        rstd_chain = sem("rstd_chain")
        side_ready = {k: [sem(f"{k}_side{s}") for s in range(2)] for k in kinds}
        side_used = {k: [sem(f"{k}_used{s}") for s in range(2)] for k in kinds}
        side_free = [sem(f"side_free{s}") for s in range(2)]
        keys_stored = [sem(f"keys_stored{t}") for t in range(tiles)]
        head_summed = sem("head_summed")
        head_rooted = sem("head_rooted")
        head_chain = sem("head_chain")
        rstd_ready = sem("rstd_ready")
        h_ready = sem("h_ready")
        turned = sem("turned")
        a_hi_ready = sem("a_hi_ready")
        a_ready = sem("a_ready")
        raw_landed = [sem(f"raw_landed{s}") for s in range(2)]
        w_hi_ready = [sem(f"w_hi_ready{s}") for s in range(2)]
        w_ready = [sem(f"w_ready{s}") for s in range(2)]
        first_half_used = sem("first_half_used")
        acc_full = [sem(f"acc_full{t}") for t in range(tiles)]
        acc_read = [sem(f"acc_read{t}") for t in range(tiles)]
        out_stored = [sem(f"out_stored{t}") for t in range(tiles)]
        res_landed = [sem(f"res_landed{t}") for t in range(tiles)]
        block = ctx.enter_context(nc.Block())

        src_tiles = src.rearrange("(n p) d -> n p d", p=P)
        w_rows = weight.rearrange("(h k p) c -> h p k c", k=HK, p=P)

        def destination(kind, dst, j, g, t):
            if by_rows(kind):
                return dst[g * T + t * P:g * T + (t + 1) * P, bass.ds(j * BANK, BANK)]
            return dst[bass.ds(j * BANK + t * P, P), g * T:(g + 1) * T]

        def each_chunk(eng, g, body):
            n0 = g * chunks
            seen = {k: g * v for k, v in kinds.items()}
            for i, (what, c0, count, dst, d0) in enumerate(plan):
                final = i == len(plan) - 1
                looped = count - 1 if final else count
                m0 = seen[what.split()[0]]
                if looped > 1:
                    with eng.Fori(0, looped) as r:
                        body(what, r + c0, dst, r + d0, r + n0, r + m0, False)
                elif looped == 1:
                    body(what, c0, dst, d0, n0, m0, False)
                n0 += count
                seen[what.split()[0]] += count
                if final:
                    body(what, c0 + count - 1, dst, d0 + count - 1, n0 - 1, m0 + count - 1, True)

        def by_rows(kind):
            return kind.startswith("heads") or kind.endswith("rows")

        def prepares(g, last):
            return last and g + 1 < groups

        @block.sync
        def _(sp):
            if gain is not None:
                sp.dma_start(g_rep[:], gain.broadcast_to([P, D])).then_inc(gain_landed, 16)

            def load_rows(n):
                if n >= 2 and gain is not None:
                    sp.wait_ge(h_ready, n - 1)
                if n >= 2 and gain is None:
                    sp.wait_ge(turned, 2 * (n - 1))
                sp.dma_start(x_in[:, n % 2, :], src_tiles[n]).then_inc(x_landed[n % 2], 16)

            def chunk(g):
                def body(kind, c, dst, j, n, m, last):
                    for half in range(2):
                        sp.wait_ge(w_ready[half], n)
                        sp.dma_start(raw[:, half], w_rows[half, :, :, bass.ds(c * BANK, BANK)]
                                     ).then_inc(raw_landed[half], 16)
                    if residual is not None:
                        for t in range(tiles):
                            sp.wait_ge(acc_read[t], n)
                            sp.dma_start(res[:, t], destination("rows", residual, j, g, t)
                                         ).then_inc(res_landed[t], 16)
                    if prepares(g, last):
                        for t in range(tiles):
                            load_rows((g + 1) * tiles + t)
                return body

            for t in range(tiles):
                load_rows(t)
            for g in range(groups):
                each_chunk(sp, g, chunk(g))
            for t in range(tiles):
                sp.wait_ge(out_stored[t], 16 * groups * chunks)
                if "gates" in kinds:
                    sp.wait_ge(keys_stored[t], 16 * groups * kinds["gates"])

        @block.gpsimd
        def _(pool):
            def chunk(kind, c, dst, j, n, m, last):
                for half in range(2):
                    pool.wait_ge(w_hi_ready[half], n + 1)
                    pool.tensor_tensor(w_lo[:, half], raw[:, half], w_hi[:, half].bitcast(F32), ALU.subtract
                                       ).then_inc(w_ready[half], 1)
            for g in range(groups):
                each_chunk(pool, g, chunk)

        @block.scalar
        def _(act):
            def square(n):
                act.wait_ge(x_landed[n % 2], 16 * (n // 2 + 1))
                if n >= 1:
                    act.wait_ge(sumsq_ready, n)
                if n >= 2:
                    act.wait_ge(rstd_ready, n - 1)
                act.activation(junk[:], x_in[:, n % 2, :], ACT.Square,
                               accum_out=sumsq[:, n % 2:n % 2 + 1]).then_inc(sumsq_ready, 1)
                act.wait_ge(sumsq_ready, n + 1)
                act.activation(root[:, n % 2:n % 2 + 1], sumsq[:, n % 2:n % 2 + 1], ACT.Sqrt,
                               bias=eps[:]).then_inc(root_ready, 1)

            def high_part(n, b):
                act.wait_ge(turned, 2 * n + b + 1)
                g, t = divmod(n, tiles)
                act.activation(a_hi[g % 2][:, b * HK:(b + 1) * HK, t * P:(t + 1) * P],
                               turn[:, b].rearrange("p (k c) -> p k c", k=HK), ACT.Copy
                               ).then_inc(a_hi_ready, 1)

            def finish(kind, t, n, m):
                s, w = t % 2, m * (tiles // 2) + t // 2
                if residual is not None:
                    return
                if kind in ("rows", "columns"):
                    act.wait_ge(out_stored[t], n * 16)
                    act.activation(out_sb[:, t], acc[:, t], ACT.Copy).then_inc(acc_read[t], 1)
                elif kind == "silu":
                    act.activation(side[:, s], acc[:, t], ACT.Sigmoid).then_inc(side_ready[kind][s], 1)
                elif kind == "gates":
                    act.wait_ge(keys_stored[t], m * 16)
                    act.activation(keys[:, t], acc[:, t], ACT.Sigmoid, scale=-1.0)
                    act.activation(side[:, s], acc[:, t], ACT.Sigmoid).then_inc(side_ready[kind][s], 1)
                elif kind == "heads":
                    act.activation(side[:, s], acc[:, t], ACT.Square).then_inc(side_ready[kind][s], 1)
                    act.wait_ge(head_summed, m * tiles + t + 1)
                    act.activation(head_rstd[:, s], head_sum[:, s], ACT.Sqrt).then_inc(head_rooted, 1)

            def chunk(g):
                def body(kind, c, dst, j, n, m, last):
                    for step in range(2 * tiles):
                        if prepares(g, last):
                            at = (g + 1) * tiles + step // 2
                            if gain is not None and step == 0:
                                square(at)
                            if gain is not None and step % 2 == 0 and step < 2 * tiles - 2:
                                square(at + 1)
                            high_part(at, step % 2)
                        t = step - tiles
                        if t < 0:
                            continue
                        act.wait_ge(acc_full[t], n + 1)
                        finish(kind.split()[0], t, n, m)
                        act.wait_ge(acc_read[t], n + 1)
                        first = dst[0] if kind == "gates" else dst
                        act.dma_start(destination(kind, first, j, g, t), out_sb[:, t]).then_inc(out_stored[t], 16)
                        if kind == "gates":
                            act.dma_start(destination(kind, dst[1], j, g, t), keys[:, t]).then_inc(keys_stored[t], 16)
                return body

            act.wait_ge(eps_ready, 1)
            for n in range(tiles):
                if gain is not None:
                    square(n)
                high_part(n, 0)
                high_part(n, 1)
            for g in range(groups):
                each_chunk(act, g, chunk(g))

        @block.vector
        def _(dve):
            dve.memset(eps[:], D * EPS).then_inc(eps_ready, 1)
            if gain is not None:
                dve.wait_ge(gain_landed, 16)
                dve.tensor_scalar(g_rep[:], g_rep[:], math.sqrt(D), None, ALU.mult
                                  ).then_inc(gain_ready, 1)
                dve.wait_ge(gain_ready, 1)

            def normalise(n):
                if n >= 2:
                    dve.wait_ge(turned, 2 * (n - 1))
                s = slice(n % 2, n % 2 + 1)
                dve.wait_ge(root_ready, n + 1)
                dve.tensor_scalar(sumsq[:, s], sumsq[:, s], D * EPS, None, ALU.add).then_inc(rstd_chain, 1)
                dve.reciprocal(rstd[:, s], root[:, s]).then_inc(rstd_chain, 1)
                dve.wait_ge(rstd_chain, n * 6 + 2)
                newton(dve, rstd_chain, n * 6 + 2, rstd[:, s], sumsq[:, s], scratch[:, s])
                dve.engine_nop().then_inc(rstd_ready, 1)
                dve.wait_ge(rstd_ready, n + 1)
                dve.scalar_tensor_tensor(h[:, n % 2], x_in[:, n % 2], rstd[:, s], g_rep[:],
                                         ALU.mult, ALU.mult).then_inc(h_ready, 1)

            def low_part(n, b):
                dve.wait_ge(a_hi_ready, 2 * n + b + 1)
                g, t = divmod(n, tiles)
                at = (slice(None), slice(b * HK, (b + 1) * HK), slice(t * P, (t + 1) * P))
                dve.tensor_tensor(a_lo[g % 2][at], turn[:, b].rearrange("p (k c) -> p k c", k=HK),
                                  a_hi[g % 2].bitcast(F32)[at], ALU.subtract).then_inc(a_ready, 1)

            def split_weights(n, half):
                dve.wait_ge(raw_landed[half], n * 16 + 16)
                dve.wait_ge(acc_full[tiles - 1] if half else first_half_used, n)
                dve.tensor_copy(w_hi[:, half], raw[:, half]).then_inc(w_hi_ready[half], 1)

            def finish(kind, t, n, m):
                s, w = t % 2, m * (tiles // 2) + t // 2
                if kind in ("rows", "columns"):
                    return
                dve.wait_ge(side_ready[kind][s], w + 1)
                dve.wait_ge(out_stored[t], n * 16)
                if kind == "silu":
                    dve.tensor_tensor(out_sb[:, t], acc[:, t], side[:, s], ALU.mult).then_inc(acc_read[t], 1)
                elif kind == "gates":
                    dve.tensor_scalar(keys[:, t], keys[:, t], lower[1][:, t:t + 1], None, ALU.mult)
                    dve.tensor_scalar(out_sb[:, t], side[:, s], lower[1][:, t:t + 1], lower[0][:, t:t + 1],
                                      ALU.mult, ALU.add).then_inc(side_used[kind][s], 1)
                    dve.wait_ge(side_used[kind][s], w + 1)
                    dve.tensor_scalar(out_sb[:, t], out_sb[:, t], F_MIN, None, ALU.max).then_inc(acc_read[t], 1)
                elif kind == "heads":
                    at = (m * tiles + t) * 6
                    dve.tensor_reduce(head_sum[:, s], side[:, s].rearrange("p (h e) -> p h e", h=NH), AX.X, ALU.add
                                      ).then_inc(head_chain, 1)
                    dve.wait_ge(head_chain, at + 1)
                    dve.tensor_scalar(head_sum[:, s], head_sum[:, s], head_width * EPS, None, ALU.add
                                      ).then_inc(head_summed, 1)
                    dve.wait_ge(head_rooted, m * tiles + t + 1)
                    dve.reciprocal(head_rstd[:, s], head_rstd[:, s]).then_inc(head_chain, 1)
                    dve.wait_ge(head_chain, at + 2)
                    newton(dve, head_chain, at + 2, head_rstd[:, s], head_sum[:, s], head_scratch[:, s])
                    dve.scalar_tensor_tensor(out_sb[:, t].rearrange("p (h e) -> p h e", h=NH),
                                             acc[:, t].rearrange("p (h e) -> p h e", h=NH), math.sqrt(head_width),
                                             head_rstd[:, s].unsqueeze(2).broadcast_to([P, NH, head_width]),
                                             ALU.mult, ALU.mult).then_inc(acc_read[t], 1)

            def chunk(g):
                def body(kind, c, dst, j, n, m, last):
                    for step in range(2 * tiles):
                        if step % tiles == 0:
                            if step == 0:
                                split_weights(n, 1)
                            elif not (last and g + 1 == groups):
                                split_weights(n + 1, 0)
                        if prepares(g, last):
                            at = (g + 1) * tiles + step // 2
                            if step % 2 == 0 and gain is not None:
                                normalise(at)
                            low_part(at, step % 2)
                        t = step - tiles
                        if t >= 0 and residual is not None:
                            dve.wait_ge(acc_full[t], n + 1)
                            dve.wait_ge(res_landed[t], n * 16 + 16)
                            dve.wait_ge(out_stored[t], n * 16)
                            dve.tensor_tensor(out_sb[:, t], acc[:, t], res[:, t], ALU.add
                                              ).then_inc(acc_read[t], 1)
                        elif t >= 0:
                            finish(kind.split()[0], t, n, m)
                return body

            for n in range(tiles):
                if gain is not None:
                    normalise(n)
                low_part(n, 0)
                low_part(n, 1)
            split_weights(0, 0)
            for g in range(groups):
                each_chunk(dve, g, chunk(g))

        @block.tensor
        def _(pe):
            def turn_rows(n, b):
                if gain is not None:
                    pe.wait_ge(h_ready, n + 1)
                else:
                    pe.wait_ge(x_landed[n % 2], 16 * (n // 2 + 1))
                if n >= 1:
                    pe.wait_ge(a_ready, 2 * (n - 1) + b + 1)
                for k in range(HK):
                    at = (b * HK + k) * P
                    mm = pe.transpose(turn[:, b, k * P:(k + 1) * P], h[:, n % 2, at:at + P], ident[:])
                mm.then_inc(turned, 1)

            def products(kind, s, half, t, first, final):
                for k in range(HK):
                    a = half * HK + k
                    cut = slice(t * P, (t + 1) * P)
                    if by_rows(kind):
                        terms = [(a_hi[s][:, a, cut], w_hi[:, half, k]), (a_hi[s][:, a, cut], w_lo[:, half, k]),
                                 (a_lo[s][:, a, cut], w_hi[:, half, k])]
                    else:
                        terms = [(w_hi[:, half, k, cut], a_hi[s][:, a]), (w_hi[:, half, k, cut], a_lo[s][:, a]),
                                 (w_lo[:, half, k, cut], a_hi[s][:, a])]
                    for i, (left, right) in enumerate(terms):
                        mm = pe.matmul(acc[:, t], left, right, start=(first and k == 0 and i == 0),
                                       stop=(final and k == HK - 1 and i == 2))
                return mm

            def chunk(g):
                def body(kind, c, dst, j, n, m, last):
                    for half in range(2):
                        pe.wait_ge(w_ready[half], n + 1)
                        for t in range(tiles):
                            if half == 0:
                                pe.wait_ge(acc_read[t], n)
                            mm = products(kind, g % 2, half, t, half == 0, half == 1)
                            if half == 1:
                                mm.then_inc(acc_full[t], 1)
                            elif t == tiles - 1:
                                mm.then_inc(first_half_used, 1)
                            if prepares(g, last):
                                step = half * tiles + t
                                turn_rows((g + 1) * tiles + step // 2, step % 2)
                return body

            for n in range(tiles):
                turn_rows(n, 0)
                turn_rows(n, 1)
            for g in range(groups):
                pe.wait_ge(a_ready, 2 * (g + 1) * tiles)
                each_chunk(pe, g, chunk(g))


HEADS, HD = 8, 64
AW = HEADS * HD
SEQ = 2048
DILATIONS = (16, 4, 1)
NEG = -1e30
OW = AW + 2 * HEADS
HH, HK_ = 4, 128
HGW = HH * HK_
LEVELS = 7
C = P
STEPS = 2 * HEADS


def mix(nc, z_rows, z_columns, branch_rows, y, q_gain, k_gain, onorm_g, ident):
    name = "mix"
    with nc.cleanup_on_exit(), ExitStack() as ctx:
        def sb(what, shape, dt=F32):
            return ctx.enter_context(nc.sbuf_tensor(f"{name}_{what}", shape, dt))

        def ps(what, shape):
            return ctx.enter_context(nc.psum_tensor(f"{name}_{what}", shape, F32))

        def sem(what):
            return nc.alloc_semaphore(f"{name}_{what}")

        gains = sb("gains", [P, 2])
        gain = sb("gain", [P, 1])
        step = sb("step", [P, 2 * P])
        hidden = sb("hidden", [P, 2 * P])
        bias = sb("bias", [P, len(DILATIONS) * HEADS, 2 * P])
        qk_in = sb("qk_in", [P, 2, 2 * AW])
        v_in = sb("v_in", [P, 4, AW])
        a_gate = sb("a_gate", [1, 2])
        q_t = sb("q_t", [P, 2, 4, P])
        k_t = sb("k_t", [P, 2, 4, P])
        p_sb = sb("p", [P, 2, 2 * P])
        pt_sb = sb("pt_sb", [P, 2, 2, P])
        o_sb = sb("o", [P, 2, OW])
        score = ps("score", [P, 2, BANK])
        pt = ps("pt", [P, 2, BANK])
        o_acc = ps("o_acc", [P, BANK])
        turn = ps("turn", [P, BANK])
        others = sb("others", [P, 2, 2, OW])
        least = sb("least", [P, 2, HEADS])
        gap = sb("gap", [P, 2, 3, HEADS])
        total = sb("total", [P, 2, 3, HEADS])
        norm = sb("norm", [P, 2, HEADS])
        scaled = sb("scaled", [P, 2, 3, AW])
        joined_sb = sb("joined_sb", [P, 2, AW])

        gains_landed = sem("gains_landed")
        gain_ready = sem("gain_ready")
        step_ready = sem("step_ready")
        hidden_set = sem("hidden_set")
        hidden_ready = sem("hidden_ready")
        bias_ready = sem("bias_ready")
        qk_landed = [sem(f"qk_landed{s}") for s in range(2)]
        v_landed = [sem(f"v_landed{s}") for s in range(2)]
        q_turned = [sem(f"q_turned{s}") for s in range(2)]
        k_turned_a = [sem(f"k_turned_a{s}") for s in range(2)]
        q_staged = [sem(f"q_staged{s}") for s in range(2)]
        k_staged = [sem(f"k_staged{s}") for s in range(2)]
        a_full = [sem(f"a_full{p}") for p in range(2)]
        masked = [sem(f"masked{p}") for p in range(2)]
        weighed = [sem(f"weighed{p}") for p in range(2)]
        pt_full = [sem(f"pt_full{p}") for p in range(2)]
        pt_read = [sem(f"pt_read{p}") for p in range(2)]
        pv_done = [sem(f"pv_done{p}") for p in range(2)]
        o_read = [sem(f"o_read{s}") for s in range(2)]
        o_stored = [sem(f"o_stored{s}") for s in range(2)]
        others_landed = [sem(f"others_landed{s}") for s in range(2)]
        join_chain = sem("join_chain")
        gap_ready = sem("gap_ready")
        gap_exped = sem("gap_exped")
        shares_ready = sem("shares_ready")
        own_scaled = [sem(f"own_scaled{s}") for s in range(2)]
        other_scaled = sem("other_scaled")
        paired = sem("paired")
        joined = [sem(f"joined{s}") for s in range(2)]
        y_stored = [sem(f"y_stored{s}") for s in range(2)]

        I32 = mybir.dt.int32
        row_i = sb("row_i", [P, C], I32)
        col_i = sb("col_i", [P, C], I32)
        after = sb("after", [P, C], I32)
        differ = sb("differ", [P, C], I32)
        later = sb("later", [P, C], I32)
        gate = sb("gate", [1, LEVELS + 1])
        top = sb("top", [P, C], I32)
        mask = sb("mask", [P, LEVELS + 1, C], I32)
        restart = sb("restart", [P, HH, C])
        og = sb("og", [P, HGW])
        q_in = sb("q_in", [P, 2, HH, C])
        k_in = sb("k_in", [P, 2, HH, C])
        f_in = sb("f_in", [P, 2, HH, C])
        ig_in = sb("ig_in", [P, 2, 2 * HGW])
        b = sb("b", [P, 2, HH, C])
        diff = sb("diff", [P, 2, HH, C])
        decay = sb("decay", [P, 2, HH, C])
        q_dec = sb("q_dec", [P, LEVELS + 1, HH, C])
        k_dec = sb("k_dec", [P, LEVELS + 1, HH, C])
        b_exp = sb("b_exp", [P, HH, C])
        last_exp = sb("last_exp", [P, HH])
        k_rows = sb("k_rows", [P, HH, C])
        s_sb = sb("s_sb", [P, 2, HH, C])
        state = sb("state", [P, HH, C])
        squares = sb("squares", [P, HH, C])
        ms = sb("ms", [P, 4, HH])
        gated = sb("gated", [P, 2, HGW])
        out = sb("out", [P, 2, HGW])
        s_ps = ps("s_ps", [P, 2, BANK])
        st_ps, o_ps = s_ps[:, 0], s_ps[:, 1]

        consts = sem("consts")
        og_landed = sem("og_landed")
        iotas = sem("iotas")
        masks = sem("masks")
        cleared = sem("cleared")
        in_landed = [sem(f"in_landed{s}") for s in range(2)]
        ig_landed = [sem(f"ig_landed{s}") for s in range(2)]
        logged = sem("logged")
        summed = sem("summed")
        diffed = [sem(f"diffed{p}") for p in range(2)]
        exped = [sem(f"exped{p}") for p in range(2)]
        b_exped = sem("b_exped")
        last_exped = sem("last_exped")
        q_scaled = sem("q_scaled")
        k_scaled = sem("k_scaled")
        s_full = [sem(f"s_full{p}") for p in range(2)]
        s_read = [sem(f"s_read{p}") for p in range(2)]
        k_turned = sem("k_turned")
        k_rows_ready = sem("k_rows_ready")
        st_full = sem("st_full")
        st_ready = sem("st_ready")
        o_full = [sem(f"o_full{s}") for s in range(2)]
        squared = sem("squared")
        mean_ready = sem("mean_ready")
        ln_ready = sem("ln_ready")
        rstd0 = sem("rstd0")
        chain = sem("chain")
        gated_ready = sem("gated_ready")
        out_ready = [sem(f"out_ready{s}") for s in range(2)]
        out_stored = [sem(f"out_stored{s}") for s in range(2)]
        block = ctx.enter_context(nc.Block())

        def rows(t, d, r, n, cols):
            if d == 1:
                return t[bass.ds(n * P, P), cols]
            v = t.rearrange("(j d) c -> j d c", d=d)
            return v[n * P:(n + 1) * P, bass.ds(r, 1), cols].rearrange("j o c -> j (o c)")

        def pt_of(p, lo):
            return pt[:, p, lo:2 * P].rearrange("p (k c) -> p k c", c=P)

        def run(eng, attention, recurrence, join):
            def beside(one, other):
                for _ in zip(one, other):
                    pass

            with eng.Fori(0, 4) as m:
                def blocks():
                    for n in range(4):
                        yield from attention(m * 4 + n, m * 2 + n // 2, n, (0, DILATIONS[0], m * 4 + n, 0), False, False)

                def chunks():
                    for s in range(2):
                        yield from recurrence(m * 2 + s, m, s)
                beside(blocks(), chunks())
            with eng.Fori(0, 4) as r:
                def blocks():
                    for n in range(4):
                        yield from attention(r * 4 + 16 + n, r * 2 + 8 + n // 2, n, (1, DILATIONS[1], r, n), n > 0, n < 3)

                def chunks():
                    for s in range(2):
                        yield from recurrence(r * 2 + 8 + s, r + 4, s)
                beside(blocks(), chunks())

            def four(m, first, final):
                for n in range(4):
                    nxt = None if final and n == 3 else True
                    a = attention(m * 4 + 32 + n, m * 2 + 16 + n // 2, n, (2, DILATIONS[2], 0, m * 4 + n),
                                  not (first and n == 0), nxt)
                    if first and n == 0:
                        for _ in a:
                            pass
                    else:
                        v = m * 4 + n - 1
                        w = m * 2 + (n - 1) // 2
                        beside(a, join(v, w, (n - 1) % 2))

            four(0, True, False)
            with eng.Fori(1, 3) as m:
                four(m, False, False)
            four(3, False, True)
            for _ in join(15, 7, 1):
                pass

        def idle_blocks(*args):
            yield from range(HEADS)

        def blocks_of(t, lev):
            half = C >> (lev + 1)
            return t.rearrange("p h (n two c) -> p (h n) two c", two=2, c=half)

        @block.sync
        def _(sp):
            for i, g in enumerate((q_gain, k_gain)):
                for half in range(2):
                    sp.dma_start(gains[half * HD:(half + 1) * HD, i:i + 1], g).then_inc(gains_landed, 16)
            sp.dma_start(og[:], onorm_g.broadcast_to([P, HGW])).then_inc(og_landed, 16)

            def attention(u, c, n4, at, prev, nxt):
                _, d, r, n = at
                s = n4 % 2
                sp.wait_ge(k_turned_a[s], c)
                sp.dma_start(qk_in[:, s], rows(z_rows, d, r, n, slice(0, 2 * AW))).then_inc(qk_landed[s], 16)
                sp.wait_ge(o_read[s], c)
                sp.dma_start(v_in[:, n4], rows(z_rows, d, r, n, slice(2 * AW, 3 * AW))
                             ).then_inc(v_landed[s], 16)
                yield from range(HEADS)

            def recurrence(u, c, s):
                sp.wait_ge(out_ready[s], c)
                for t, r0 in ((q_in, 0), (f_in, HGW), (k_in, 2 * HGW)):
                    sp.dma_start(t[:, s], z_columns[r0:r0 + HGW, bass.ds(u * C, C)].rearrange("(h p) c -> p h c", p=P)
                                 ).then_inc(in_landed[s], 16)
                sp.dma_start(ig_in[:, s], z_rows[bass.ds(u * C, C), 3 * AW:3 * AW + 2 * HGW]).then_inc(ig_landed[s], 16)
                yield from range(STEPS)

            def join(v, w, s):
                sp.wait_ge(o_stored[0], 16 * 16)
                sp.wait_ge(o_stored[1], 16 * 16)
                sp.wait_ge(joined[s], w)
                for i in range(2):
                    sp.dma_start(others[:, s, i], branch_rows[i][bass.ds(v * P, P), :]).then_inc(others_landed[s], 16)
                yield from range(HEADS)

            run(sp, attention, recurrence, join)
            for s in range(2):
                sp.wait_ge(o_stored[s], 16 * 16)
                sp.wait_ge(y_stored[s], 16 * 8)
                sp.wait_ge(out_stored[s], 16 * 8)

        @block.gpsimd
        def _(pool):
            pool.iota(step[:], pattern=[[-1, 2 * P]], base=P, channel_multiplier=1,
                      allow_small_or_imprecise_dtypes=True).then_inc(step_ready, 1)
            pool.memset(hidden[:], 0.0).then_inc(hidden_set, 1)
            pool.wait_ge(hidden_set, 1)
            pool.affine_select(out=hidden[:], in_=hidden[:], compare_op=ALU.is_ge, fill=NEG, base=P,
                               pattern=[[-1, 2 * P]], channel_multiplier=1).then_inc(hidden_set, 1)
            pool.wait_ge(hidden_set, 2)
            pool.affine_select(out=hidden[:], in_=hidden[:], compare_op=ALU.is_ge, fill=NEG, base=0,
                               pattern=[[1, 2 * P]], channel_multiplier=-1).then_inc(hidden_ready, 1)
            pool.iota(row_i[:], pattern=[[0, C]], base=0, channel_multiplier=1).then_inc(iotas, 1)
            pool.iota(col_i[:], pattern=[[1, C]], base=0, channel_multiplier=0).then_inc(iotas, 1)
            pool.iota(later[:], pattern=[[1, C]], base=0, channel_multiplier=-1).then_inc(iotas, 1)
            pool.memset(restart[:], 1.0).then_inc(consts, 1)
            pool.wait_ge(consts, 1)
            pool.memset(restart[:, :, 0:1], 0.0).then_inc(consts, 1)
            for t in (s_sb, state, k_dec, q_dec):
                pool.memset(t[:], 0.0).then_inc(cleared, 1)
            pool.wait_ge(cleared, 4)

            def recurrence(u, c, s):
                for at in range(STEPS):
                    lev = at - 3
                    if 0 <= lev <= LEVELS:
                        if lev == 0:
                            pool.wait_ge(in_landed[s], c * 48 + 48)
                        p, w = lev % 2, u * 4 + lev // 2
                        if lev < LEVELS:
                            pool.wait_ge(s_full[(lev + 1) % 2], u * 4)
                            pool.wait_ge(exped[p], w + 1)
                            o, i, e = (blocks_of(t, lev)[:, :, 0] for t in (k_dec[:, lev], k_in[:, s], decay[:, p]))
                            pool.tensor_tensor(o, i, e, ALU.mult).then_inc(k_scaled, 1)
                        else:
                            pool.wait_ge(k_turned, u)
                            pool.wait_ge(exped[p], w + 1)
                            pool.tensor_tensor(k_dec[:, lev], k_in[:, s], decay[:, p], ALU.mult).then_inc(k_scaled, 1)
                    if lev == LEVELS + 1:
                        pool.wait_ge(ig_landed[s], c * 16 + 16)
                        pool.wait_ge(og_landed, 16)
                        pool.wait_ge(out_ready[s], c)
                        pool.tensor_tensor(gated[:, s], ig_in[:, s, HGW:], og[:], ALU.mult).then_inc(gated_ready, 1)
                    yield

            def join(v, w, s):
                for at in range(HEADS):
                    if at == 4:
                        pool.wait_ge(shares_ready, v + 1)
                        pool.wait_ge(joined[s], w)
                        for i in range(2):
                            x = pool.tensor_tensor(scaled[:, s, i].rearrange("p (h e) -> p h e", e=HD),
                                                   others[:, s, i, 0:AW].rearrange("p (h e) -> p h e", e=HD),
                                                   gap[:, s, i].unsqueeze(2).broadcast_to([P, HEADS, HD]), ALU.mult)
                        x.then_inc(other_scaled, 1)
                    if at == 6:
                        pool.wait_ge(other_scaled, v + 1)
                        pool.tensor_tensor(scaled[:, s, 0], scaled[:, s, 0], scaled[:, s, 1], ALU.add).then_inc(paired, 1)
                    yield

            run(pool, idle_blocks, recurrence, join)

        @block.vector
        def _(dve):
            dve.wait_ge(gains_landed, 64)
            dve.scalar_tensor_tensor(gain[:], gains[:, 0:1], 1 / math.sqrt(HD), gains[:, 1:2],
                                     ALU.mult, ALU.mult).then_inc(gain_ready, 1)
            dve.wait_ge(step_ready, 1)
            dve.wait_ge(hidden_ready, 1)
            for i, d in enumerate(DILATIONS):
                for e in range(HEADS):
                    slope = 2.0 ** (-8.0 / HEADS * (e + 1))
                    dve.scalar_tensor_tensor(bias[:, i * HEADS + e], step[:], -slope * d, hidden[:],
                                             ALU.mult, ALU.add).then_inc(bias_ready, 1)
            dve.wait_ge(iotas, 3)
            dve.tensor_tensor(differ[:], row_i[:], col_i[:], ALU.bitwise_xor).then_inc(masks, 1)
            dve.tensor_scalar(after[:], later[:], 0, None, ALU.is_gt).then_inc(masks, 1)
            dve.wait_ge(masks, 2)
            dve.tensor_scalar(mask[:, 0], differ[:], 0, None, ALU.is_equal).then_inc(masks, 1)
            for lev in range(LEVELS):
                dve.wait_ge(masks, 3 + 2 * lev)
                dve.tensor_scalar(top[:], differ[:], LEVELS - 1 - lev, None, ALU.logical_shift_right).then_inc(masks, 1)
                dve.wait_ge(masks, 4 + 2 * lev)
                dve.scalar_tensor_tensor(mask[:, lev + 1], top[:], 1, after[:], ALU.is_equal, ALU.mult
                                         ).then_inc(masks, 1)
            dve.wait_ge(masks, 3 + 2 * LEVELS)
            dve.wait_ge(consts, 2)
            dve.wait_ge(cleared, 4)
            dve.wait_ge(bias_ready, len(DILATIONS) * HEADS)
            dve.wait_ge(gain_ready, 1)
            dve.engine_nop().then_inc(st_ready, 1)

            def stage_q(s, c):
                dve.wait_ge(q_turned[s], c + 1)
                dve.tensor_scalar(q_t[:, s], turn[:].rearrange("p (k c) -> p k c", k=4), gain[:], None,
                                  ALU.mult).then_inc(q_staged[s], 1)

            def attention(u, c, n4, at, prev, nxt):
                i, s = at[0], n4 % 2
                lo = 0 if prev else P
                for e in range(HEADS):
                    p, w = e % 2, u * 4 + e // 2
                    if e == 0 and (i < 2 or type(u) is int and u < 34):
                        dve.wait_ge(o_stored[s], c * 16)
                    elif e == 0:
                        dve.wait_ge(joined[s], c - 16)
                    dve.wait_ge(a_full[p], w + 1)
                    dve.wait_ge(pt_full[p], w)
                    dve.memset(a_gate[:, p:p + 1], 0.0)
                    dve.tensor_tensor_reduce(p_sb[:, p, lo:], score[:, p, lo:2 * P],
                                             bias[:, i * HEADS + e, lo:], -1.0, 3e38, ALU.add,
                                             ALU.min, o_sb[:, s, AW + e:AW + e + 1]
                                             ).then_inc(masked[p], 1)
                    if e == 4 and nxt is not None:
                        stage_q(1 - s, c + s)
                    if e % 2 == 1:
                        q = 0
                        dve.wait_ge(pt_full[q], w + 1)
                        dve.wait_ge(pv_done[q], w)
                        dve.tensor_copy(pt_sb[:, q, lo // P:], pt_of(q, lo)).then_inc(pt_read[q], 1)
                    yield

            def differences(u, s, lev):
                p, w = lev % 2, u * 4 + lev // 2
                dve.wait_ge(exped[p], w)
                if lev == LEVELS:
                    edge = b[:, s, :, C - 1:C].broadcast_to([P, HH, C])
                    dve.tensor_tensor(diff[:, p], edge, b[:, s], ALU.subtract).then_inc(diffed[p], 1)
                    return
                half = C >> (lev + 1)
                bb, dd = blocks_of(b[:, s], lev), blocks_of(diff[:, p], lev)
                edge = bb[:, :, 0, half - 1:half].broadcast_to([P, HH * C // half // 2, half])
                dve.tensor_tensor(dd[:, :, 0], edge, bb[:, :, 0], ALU.subtract)
                dve.tensor_tensor(dd[:, :, 1], bb[:, :, 1], edge, ALU.subtract).then_inc(diffed[p], 1)

            def scale_q(u, c, s, lev):
                p, w = lev % 2, u * 4 + lev // 2
                if lev == LEVELS:
                    dve.wait_ge(o_full[1 - s], c + s)
                    dve.wait_ge(b_exped, u + 1)
                    dve.tensor_tensor(q_dec[:, lev], q_in[:, s], b_exp[:], ALU.mult).then_inc(q_scaled, 1)
                    return
                dve.wait_ge(exped[p], w + 1)
                dve.wait_ge(s_full[(lev + 1) % 2], u * 4)
                o, i, e = (blocks_of(t, lev)[:, :, 1] for t in (q_dec[:, lev], q_in[:, s], decay[:, p]))
                dve.tensor_tensor(o, i, e, ALU.mult).then_inc(q_scaled, 1)

            def pick(u, c, s, j):
                if j == 0:
                    dve.wait_ge(o_full[s], c)
                else:
                    dve.wait_ge(s_read[(j - 1) % 2], u * 4 + (j - 1) // 2 + 1)
                dve.wait_ge(s_full[j % 2], u * 4 + j // 2 + 1)
                dve.memset(gate[:, j:j + 1], 0.0)
                m = mask[:, j:j + 1].broadcast_to([P, HH, C])
                dve.copy_predicated(s_sb[:, s], m, s_ps[:, j % 2].rearrange("p (h c) -> p h c", h=HH)
                                    ).then_inc(s_read[j % 2], 1)

            def recurrence(u, c, s):
                for at in range(STEPS):
                    if at == 1:
                        dve.wait_ge(logged, u + 1)
                        dve.tensor_tensor_scan(b[:, s].rearrange("p h c -> p (h c)"),
                                               restart[:].rearrange("p h c -> p (h c)"),
                                               f_in[:, s].rearrange("p h c -> p (h c)"), 0.0, ALU.mult, ALU.add
                                               ).then_inc(summed, 1)
                        dve.wait_ge(summed, u + 1)
                    if 0 <= at - 1 <= LEVELS:
                        differences(u, s, at - 1)
                    if 0 <= at - 3 <= LEVELS:
                        scale_q(u, c, s, at - 3)
                    if at == 3:
                        pick(u, c, s, 0)
                    if 1 <= at - 4 <= LEVELS:
                        pick(u, c, s, at - 4)
                    if at == 14:
                        dve.wait_ge(o_full[s], c + 1)
                        dve.wait_ge(last_exped, u + 1)
                        dve.wait_ge(st_full, u + 1)
                        for h in range(HH):
                            x = dve.scalar_tensor_tensor(state[:, h], state[:, h], last_exp[:, h:h + 1],
                                                         st_ps[:, h * C:(h + 1) * C], ALU.mult, ALU.add)
                        x.then_inc(st_ready, 1)
                        dve.wait_ge(squared, u + 1)
                        dve.tensor_reduce(ms[:, 0], squares[:], AX.X, ALU.add).then_inc(chain, 1)
                        dve.wait_ge(chain, u * 5 + 1)
                        dve.tensor_scalar(ms[:, 0], ms[:, 0], 1 / C, EPS, ALU.mult, ALU.add).then_inc(mean_ready, 1)
                    if at == 15:
                        dve.wait_ge(rstd0, u + 1)
                        newton(dve, chain, u * 5 + 1, ms[:, 2], ms[:, 0], ms[:, 3])
                        dve.wait_ge(gated_ready, u + 1)
                        dve.wait_ge(out_stored[s], c * 16)
                        for h in range(HH):
                            cols = slice(h * C, (h + 1) * C)
                            x = dve.scalar_tensor_tensor(out[:, s, cols], o_ps[:, cols], ms[:, 2, h:h + 1],
                                                         gated[:, s, cols], ALU.mult, ALU.mult)
                        x.then_inc(out_ready[s], 1)
                    yield

            def join(v, w, s):
                n = v * 6
                for at in range(HEADS):
                    if at == 0:
                        dve.wait_ge(others_landed[s], w * 32 + 32)
                        dve.wait_ge(o_read[s], w + 17)
                        dve.wait_ge(joined[s], w)
                        minus_max = [others[:, s, 0, AW:AW + HEADS], others[:, s, 1, AW:AW + HEADS],
                                     o_sb[:, s, AW:AW + HEADS]]
                        dve.tensor_tensor(least[:, s], minus_max[0], minus_max[1], ALU.min).then_inc(join_chain, 1)
                        dve.wait_ge(join_chain, n + 1)
                        dve.tensor_tensor(least[:, s], least[:, s], minus_max[2], ALU.min).then_inc(join_chain, 1)
                        dve.wait_ge(join_chain, n + 2)
                        for i in range(3):
                            x = dve.tensor_tensor(gap[:, s, i], least[:, s], minus_max[i], ALU.subtract)
                        x.then_inc(gap_ready, 1)
                    if at == 2:
                        dve.wait_ge(gap_exped, v + 1)
                        for i, t in enumerate((others[:, s, 0], others[:, s, 1], o_sb[:, s])):
                            x = dve.tensor_tensor(total[:, s, i], gap[:, s, i], t[:, AW + HEADS:OW], ALU.mult)
                        x.then_inc(join_chain, 1)
                        dve.wait_ge(join_chain, n + 3)
                        dve.tensor_reduce(norm[:, s], total[:, s].rearrange("p b h -> p h b"), AX.X, ALU.add
                                          ).then_inc(join_chain, 1)
                        dve.wait_ge(join_chain, n + 4)
                        dve.reciprocal(norm[:, s], norm[:, s]).then_inc(join_chain, 1)
                        dve.wait_ge(join_chain, n + 5)
                        dve.tensor_tensor(gap[:, s], gap[:, s], norm[:, s:s + 1].broadcast_to([P, 3, HEADS]), ALU.mult
                                          ).then_inc(shares_ready, 1)
                        dve.engine_nop().then_inc(join_chain, 1)
                    if at == 4:
                        dve.wait_ge(shares_ready, v + 1)
                        dve.tensor_tensor(scaled[:, s, 2].rearrange("p (h e) -> p h e", e=HD),
                                          o_sb[:, s, 0:AW].rearrange("p (h e) -> p h e", e=HD),
                                          gap[:, s, 2].unsqueeze(2).broadcast_to([P, HEADS, HD]), ALU.mult
                                          ).then_inc(own_scaled[s], 1)
                    if at == 7:
                        dve.wait_ge(own_scaled[s], w + 1)
                        dve.wait_ge(y_stored[s], w * 16)
                        dve.wait_ge(paired, v + 1)
                        dve.tensor_tensor(joined_sb[:, s], scaled[:, s, 0], scaled[:, s, 2], ALU.add).then_inc(joined[s], 1)
                    yield

            stage_q(0, 0)
            run(dve, attention, recurrence, join)

        @block.scalar
        def _(act):
            nc.scalar.preload_act_table_set("natural_log_exp_and_others")

            def stage_k(s, c):
                act.wait_ge(k_turned_a[s], c + 1)
                act.activation(k_t[:, s], turn[:].rearrange("p (k c) -> p k c", k=4), ACT.Copy
                               ).then_inc(k_staged[s], 1)

            def attention(u, c, n4, at, prev, nxt):
                i, d, r, n = at
                s = n4 % 2
                lo = 0 if prev else P
                for e in range(HEADS):
                    p, w = e % 2, u * 4 + e // 2
                    act.wait_ge(masked[p], w + 1)
                    act.activation(p_sb[:, p, lo:], p_sb[:, p, lo:], ACT.Exp, scale=-1.0,
                                   bias=o_sb[:, s, AW + e:AW + e + 1],
                                   accum_out=o_sb[:, s, AW + HEADS + e:AW + HEADS + e + 1]
                                   ).then_inc(weighed[p], 1)
                    if e == 6 and nxt is not None:
                        stage_k(1 - s, c + s)
                    for o in ((e - 1,) if e % 2 == 0 and e else (e,) if e == HEADS - 1 else ()):
                        v = u * 4 + o // 2
                        act.wait_ge(pt_full[1], v + 1)
                        act.wait_ge(pv_done[1], v)
                        act.activation(pt_sb[:, 1, lo // P:], pt_of(1, lo), ACT.Copy).then_inc(pt_read[1], 1)
                    if e == HEADS - 1:
                        act.wait_ge(pv_done[1], u * 4 + 4)
                        act.activation(o_sb[:, s, 0:AW], o_acc[:], ACT.Copy).then_inc(o_read[s], 1)
                        if i < 2:
                            act.wait_ge(o_read[s], c + 1)
                            act.dma_start(rows(branch_rows[i], d, r, n, slice(0, OW)), o_sb[:, s]).then_inc(o_stored[s], 16)
                    yield

            def recurrence(u, c, s):
                for at in range(STEPS):
                    if at == 0:
                        act.wait_ge(in_landed[s], c * 48 + 48)
                        act.activation(f_in[:, s], f_in[:, s], ACT.Ln).then_inc(logged, 1)
                    if at == 1:
                        act.wait_ge(q_scaled, u * 8)
                        act.wait_ge(st_ready, u + 1)
                        act.wait_ge(summed, u + 1)
                        act.activation(b_exp[:], b[:, s], ACT.Exp).then_inc(b_exped, 1)
                        act.activation(last_exp[:], b[:, s, :, C - 1], ACT.Exp).then_inc(last_exped, 1)
                    lev = at - 2
                    if 0 <= lev <= LEVELS:
                        p, w = lev % 2, u * 4 + lev // 2
                        act.wait_ge(q_scaled, u * 8 + max(lev - 1, 0))
                        act.wait_ge(k_scaled, u * 8 + max(lev - 1, 0))
                        act.wait_ge(diffed[p], w + 1)
                        act.activation(decay[:, p], diff[:, p], ACT.Exp).then_inc(exped[p], 1)
                    if at == 12:
                        act.wait_ge(st_full, u)
                        act.wait_ge(k_turned, u + 1)
                        act.activation(k_rows[:], st_ps.rearrange("p (h c) -> p h c", h=HH), ACT.Copy
                                       ).then_inc(k_rows_ready, 1)
                    if at == 13:
                        act.wait_ge(o_full[s], c + 1)
                        act.activation(squares[:], o_ps.rearrange("p (h c) -> p h c", h=HH), ACT.Square
                                       ).then_inc(squared, 1)
                    if at == 14:
                        act.wait_ge(mean_ready, u + 1)
                        act.activation(ms[:, 1], ms[:, 0], ACT.Ln).then_inc(ln_ready, 1)
                        act.wait_ge(ln_ready, u + 1)
                        act.activation(ms[:, 2], ms[:, 1], ACT.Exp, scale=-0.5).then_inc(rstd0, 1)
                    if at == 15:
                        act.wait_ge(out_ready[s], c + 1)
                        act.dma_start(y[bass.ds(u * C, C), AW:AW + HGW], out[:, s]).then_inc(out_stored[s], 16)
                    yield

            def join(v, w, s):
                for at in range(HEADS):
                    if at == 1:
                        act.wait_ge(gap_ready, v + 1)
                        act.activation(gap[:, s], gap[:, s], ACT.Exp).then_inc(gap_exped, 1)
                    if at == 7:
                        act.wait_ge(joined[s], w + 1)
                        act.dma_start(y[bass.ds(v * P, P), 0:AW], joined_sb[:, s]).then_inc(y_stored[s], 16)
                    yield

            stage_k(0, 0)
            run(act, attention, recurrence, join)

        @block.tensor
        def _(pe):
            def turn_rows(s, c, which):
                if which == 0:
                    pe.wait_ge(qk_landed[s], c * 16 + 16)
                    pe.wait_ge(k_staged[1 - s], c + s)
                else:
                    pe.wait_ge(q_staged[s], c + 1)
                for j in range(4):
                    at = (4 * which + j) * P
                    mm = pe.transpose(turn[:, j * P:(j + 1) * P], qk_in[:, s, at:at + P], ident[:])
                mm.then_inc((q_turned, k_turned_a)[which][s], 1)

            def scores(u, s, e, prev):
                p, w = e % 2, u * 4 + e // 2
                pe.wait_ge(masked[p], w)
                pair, base = e // 2, (e % 2) * HD
                at = slice(base, base + HD)
                for side in ((0, 1) if prev else (1,)):
                    k_slot = s if side else 1 - s
                    mm = pe.matmul(score[:, p, side * P:(side + 1) * P], q_t[at, s, pair], k_t[at, k_slot, pair],
                                   start=True, stop=True)
                mm.then_inc(a_full[p], 1)

            def transposes(u, e, prev):
                p, w = e % 2, u * 4 + e // 2
                pe.wait_ge(weighed[p], w + 1)
                pe.wait_ge(pt_read[p], w)
                for side in ((0, 1) if prev else (1,)):
                    cols = slice(side * P, (side + 1) * P)
                    mm = pe.transpose(pt[:, p, cols], p_sb[:, p, cols], ident[:])
                mm.then_inc(pt_full[p], 1)

            def sums(u, c, n4, e, prev):
                p, w, s = e % 2, u * 4 + e // 2, n4 % 2
                if e == 0:
                    pe.wait_ge(v_landed[s], c * 16 + 16)
                    pe.wait_ge(o_read[1 - s], c + s)
                pe.wait_ge(pt_read[p], w + 1)
                cols = slice(e * HD, (e + 1) * HD)
                for side in ((0, 1) if prev else (1,)):
                    mm = pe.matmul(o_acc[:, cols], pt_sb[:, p, side], v_in[:, n4 if side else (n4 - 1) % 4, cols],
                                   start=(side == 0 or not prev), stop=(side == 1))
                mm.then_inc(pv_done[p], 1)

            def attention(u, c, n4, at, prev, nxt):
                s = n4 % 2
                for e in range(HEADS):
                    transposes(u, e, prev)
                    if e < HEADS - 2:
                        scores(u, s, e + 2, prev)
                    elif nxt is not None:
                        if e == HEADS - 2:
                            pe.wait_ge(k_staged[1 - s], c + s + 1)
                        scores(u + 1, 1 - s, e + 2 - HEADS, nxt)
                    if e == 3 and nxt is not None:
                        turn_rows(1 - s, c + s, 0)
                    if e == 5 and nxt is not None:
                        turn_rows(1 - s, c + s, 1)
                    if e:
                        sums(u, c, n4, e - 1, prev)
                    if e == HEADS - 1:
                        sums(u, c, n4, e, prev)
                    yield

            def recurrence(u, c, s):
                for at in range(STEPS):
                    j = 0 if at == 2 else at - 3 if 1 <= at - 3 <= LEVELS else None
                    if j is not None:
                        pe.wait_ge(s_read[j % 2], u * 4 + j // 2)
                        if j == 0:
                            pe.wait_ge(st_ready, u + 1)
                            pe.wait_ge(in_landed[s], c * 48 + 48)
                            kk, qq = k_in[:, s], q_in[:, s]
                        else:
                            if j == 1:
                                pe.wait_ge(out_ready[1 - s], c + s)
                            pe.wait_ge(q_scaled, u * 8 + j)
                            pe.wait_ge(k_scaled, u * 8 + j)
                            kk, qq = k_dec[:, j - 1], q_dec[:, j - 1]
                        for h in range(HH):
                            mm = pe.matmul(s_ps[:, j % 2, h * C:(h + 1) * C], kk[:, h], qq[:, h], start=True, stop=True)
                        mm.then_inc(s_full[j % 2], 1)
                    if at == 11:
                        pe.wait_ge(s_read[0], u * 4 + 4)
                        pe.wait_ge(k_scaled, u * 8 + 8)
                        for h in range(HH):
                            mm = pe.transpose(st_ps[:, h * C:(h + 1) * C], k_dec[:, LEVELS, h], ident[:])
                        mm.then_inc(k_turned, 1)
                    if at == 12:
                        pe.wait_ge(q_scaled, u * 8 + 8)
                        pe.wait_ge(s_read[1], u * 4 + 4)
                        pe.wait_ge(ig_landed[s], c * 16 + 16)
                        for h in range(HH):
                            cols = slice(h * C, (h + 1) * C)
                            pe.matmul(o_ps[:, cols], s_sb[:, s, h], ig_in[:, s, cols], start=True, stop=False)
                            mm = pe.matmul(o_ps[:, cols], q_dec[:, LEVELS, h], state[:, h], start=False, stop=True)
                        mm.then_inc(o_full[s], 1)
                    if at == 13:
                        pe.wait_ge(k_rows_ready, u + 1)
                        for h in range(HH):
                            cols = slice(h * C, (h + 1) * C)
                            mm = pe.matmul(st_ps[:, cols], k_rows[:, h], ig_in[:, s, cols], start=True, stop=True)
                        mm.then_inc(st_full, 1)
                    yield

            pe.wait_ge(cleared, 4)
            turn_rows(0, 0, 0)
            turn_rows(0, 0, 1)
            pe.wait_ge(k_staged[0], 1)
            scores(0, 0, 0, False)
            scores(0, 0, 1, False)
            run(pe, attention, recurrence, idle_blocks)


MEM, MH, MD = 256, 4, 256


def attend_memory(nc, qm, kvm, om, q_gain, k_gain, ident):
    name = "ma"
    M2 = MEM // P
    with nc.cleanup_on_exit(), ExitStack() as ctx:
        def sb(what, shape, dt=F32):
            return ctx.enter_context(nc.sbuf_tensor(f"{name}_{what}", shape, dt))

        def ps(what, shape):
            return ctx.enter_context(nc.psum_tensor(f"{name}_{what}", shape, F32))

        def sem(what):
            return nc.alloc_semaphore(f"{name}_{what}")

        gains = sb("gains", [P, 2, MD // P])
        gain = sb("gain", [P, MD // P])
        k_in = sb("k_in", [P, M2, D])
        v_in = sb("v_in", [P, M2, D])
        k_t = sb("k_t", [P, KT, MEM])
        q_in = sb("q_in", [P, 2, D])
        q_t = sb("q_t", [P, 2, KT, P])
        top = sb("top", [P, 2, MH])
        minus = sb("minus", [P, 2, MH])
        weight = sb("weight", [P, 2, MH])
        inverse = sb("inverse", [P, 2, MH])
        p_sb = sb("p", [P, 2, MEM])
        pt_sb = sb("pt_sb", [P, 2, M2, P])
        o_sb = sb("o", [P, 2, D])
        turn = ps("turn", [P, 2, BANK])
        score = ps("score", [P, 2, BANK])
        pt = ps("pt", [P, 2, BANK])
        o_ps = ps("o_ps", [P, 2, BANK])

        const_landed = sem("const_landed")
        gain_ready = sem("gain_ready")
        k_turned = sem("k_turned")
        k_ready = sem("k_ready")
        q_landed = [sem(f"q_landed{s}") for s in range(2)]
        q_turned = [sem(f"q_turned{i}") for i in range(2)]
        q_ready = [sem(f"q_ready{i}") for i in range(2)]
        s_full = [sem(f"s_full{p}") for p in range(2)]
        topped = [sem(f"topped{p}") for p in range(2)]
        minus_ready = [sem(f"minus_ready{p}") for p in range(2)]
        exped = [sem(f"exped{p}") for p in range(2)]
        inverted = [sem(f"inverted{p}") for p in range(2)]
        pt_full = [sem(f"pt_full{p}") for p in range(2)]
        pt_read = [sem(f"pt_read{p}") for p in range(2)]
        o_full = [sem(f"o_full{p}") for p in range(2)]
        o_read = [sem(f"o_read{p}") for p in range(2)]
        o_stored = [sem(f"o_stored{s}") for s in range(2)]
        block = ctx.enter_context(nc.Block())

        def each_tile(eng, body):
            with eng.Fori(0, SEQ // P // 2) as c:
                for s in range(2):
                    body(c * 2 + s, c, s)

        @block.sync
        def _(sp):
            for i, g in enumerate((q_gain, k_gain)):
                for t in range(MD // P):
                    sp.dma_start(gains[:, i, t:t + 1], g[t * P:(t + 1) * P, :]).then_inc(const_landed, 16)
            for m in range(M2):
                sp.dma_start(k_in[:, m], kvm[m * P:(m + 1) * P, 0:D]).then_inc(const_landed, 16)
                sp.dma_start(v_in[:, m], kvm[m * P:(m + 1) * P, D:2 * D]).then_inc(const_landed, 16)

            def body(u, c, s):
                sp.wait_ge(q_ready[1], u)
                sp.dma_start(q_in[:, s], qm[bass.ds(u * P, P), :]).then_inc(q_landed[s], 16)
            each_tile(sp, body)
            for s in range(2):
                sp.wait_ge(o_stored[s], 16 * 8)

        @block.vector
        def _(dve):
            dve.wait_ge(const_landed, 16 * (4 + 2 * M2))
            dve.scalar_tensor_tensor(gain[:], gains[:, 0], 1 / math.sqrt(MD), gains[:, 1], ALU.mult, ALU.mult
                                     ).then_inc(gain_ready, 1)
            dve.wait_ge(gain_ready, 1)
            for i in range(2 * M2):
                m, b = divmod(i, 2)
                dve.wait_ge(k_turned, i + 1)
                for j in range(4):
                    at = 4 * b + j
                    x = dve.tensor_scalar(k_t[:, at, m * P:(m + 1) * P], turn[:, b, j * P:(j + 1) * P],
                                          gain[:, at % 2:at % 2 + 1], None, ALU.mult)
                x.then_inc(k_ready, 1)

            def body(u, c, s):
                for e in range(MH):
                    p, w = e % 2, u * 2 + e // 2
                    if e == 0:
                        dve.wait_ge(o_stored[s], c * 16)
                    dve.wait_ge(s_full[p], w + 1)
                    dve.tensor_reduce(top[:, s, e:e + 1], score[:, p, 0:MEM], AX.X, ALU.max).then_inc(topped[p], 1)
                    dve.wait_ge(topped[p], w + 1)
                    dve.tensor_scalar(minus[:, s, e:e + 1], top[:, s, e:e + 1], -1.0, None, ALU.mult
                                      ).then_inc(minus_ready[p], 1)
                    if e:
                        finish(u, s, e - 1)
                finish(u, s, MH - 1)

            def finish(u, s, e):
                p, w = e % 2, u * 2 + e // 2
                dve.wait_ge(exped[p], w + 1)
                dve.reciprocal(inverse[:, s, e:e + 1], weight[:, s, e:e + 1]).then_inc(inverted[p], 1)
                dve.wait_ge(pt_full[p], w + 1)
                dve.wait_ge(o_full[p], w)
                dve.tensor_copy(pt_sb[:, p], pt[:, p, 0:MEM].rearrange("p (k c) -> p k c", c=P)).then_inc(pt_read[p], 1)

            each_tile(dve, body)

        @block.scalar
        def _(act):
            def body(u, c, s):
                for i in range(2):
                    act.wait_ge(q_turned[i], u + 1)
                    act.activation(q_t[:, s, 4 * i:4 * i + 4], turn[:, i].rearrange("p (k c) -> p k c", k=4), ACT.Copy
                                   ).then_inc(q_ready[i], 1)
                for e in range(MH):
                    p, w = e % 2, u * 2 + e // 2
                    act.wait_ge(minus_ready[p], w + 1)
                    act.wait_ge(pt_full[p], w)
                    act.activation(p_sb[:, p], score[:, p, 0:MEM], ACT.Exp, bias=minus[:, s, e:e + 1],
                                   accum_out=weight[:, s, e:e + 1]).then_inc(exped[p], 1)
                    if e:
                        finish(u, c, s, e - 1)
                finish(u, c, s, MH - 1)
                for p in range(2):
                    act.wait_ge(o_read[p], u * 2 + 2)
                act.dma_start(om[bass.ds(u * P, P), :], o_sb[:, s]).then_inc(o_stored[s], 16)

            def finish(u, c, s, e):
                p, w = e % 2, u * 2 + e // 2
                act.wait_ge(o_full[p], w + 1)
                act.wait_ge(inverted[p], w + 1)
                act.wait_ge(o_stored[s], c * 16)
                act.activation(o_sb[:, s, e * MD:(e + 1) * MD], o_ps[:, p, 0:MD], ACT.Copy,
                               scale=inverse[:, s, e:e + 1]).then_inc(o_read[p], 1)

            each_tile(act, body)

        @block.tensor
        def _(pe):
            pe.wait_ge(const_landed, 16 * (4 + 2 * M2))
            for i in range(2 * M2):
                m, b = divmod(i, 2)
                if i >= 2:
                    pe.wait_ge(k_ready, i - 1)
                for j in range(4):
                    at = (4 * b + j) * P
                    mm = pe.transpose(turn[:, b, j * P:(j + 1) * P], k_in[:, m, at:at + P], ident[:])
                mm.then_inc(k_turned, 1)
            pe.wait_ge(k_ready, 2 * M2)

            def body(u, c, s):
                pe.wait_ge(q_landed[s], c * 16 + 16)
                for i in range(2):
                    pe.wait_ge(q_ready[i], u)
                    for j in range(4):
                        at = (4 * i + j) * P
                        mm = pe.transpose(turn[:, i, j * P:(j + 1) * P], q_in[:, s, at:at + P], ident[:])
                    mm.then_inc(q_turned[i], 1)
                scores(u, s, 0)
                for e in range(MH):
                    if e + 1 < MH:
                        scores(u, s, e + 1)
                    p, w = e % 2, u * 2 + e // 2
                    pe.wait_ge(exped[p], w + 1)
                    pe.wait_ge(pt_read[p], w)
                    for m in range(M2):
                        mm = pe.transpose(pt[:, p, m * P:(m + 1) * P], p_sb[:, p, m * P:(m + 1) * P], ident[:])
                    mm.then_inc(pt_full[p], 1)
                    pe.wait_ge(pt_read[p], w + 1)
                    pe.wait_ge(o_read[p], w)
                    for m in range(M2):
                        mm = pe.matmul(o_ps[:, p, 0:MD], pt_sb[:, p, m], v_in[:, m, e * MD:(e + 1) * MD],
                                       start=(m == 0), stop=(m == M2 - 1))
                    mm.then_inc(o_full[p], 1)

            def scores(u, s, e):
                p, w = e % 2, u * 2 + e // 2
                pe.wait_ge(q_ready[e // 2], u + 1)
                pe.wait_ge(exped[p], w)
                for i in range(MD // P):
                    at = e * (MD // P) + i
                    mm = pe.matmul(score[:, p, 0:MEM], q_t[:, s, at], k_t[:, at], start=(i == 0), stop=(i == 1))
                mm.then_inc(s_full[p], 1)

            each_tile(pe, body)


def feed_forward(nc, src, gain, w1, w2, dst, ident):
    name = "ff"
    S = src.shape[0]
    T = BANK
    groups, tiles = S // T, T // P
    QUARTERS = w1.shape[1] // D
    PER = 4
    with nc.cleanup_on_exit(), ExitStack() as ctx:
        def sb(what, shape, dt=F32):
            return ctx.enter_context(nc.sbuf_tensor(f"{name}_{what}", shape, dt))

        def ps(what, shape):
            return ctx.enter_context(nc.psum_tensor(f"{name}_{what}", shape, F32))

        def sem(what):
            return nc.alloc_semaphore(f"{name}_{what}")

        x_in = sb("x_in", [P, 2, D])
        junk = sb("junk", [P, D])
        sumsq = sb("sumsq", [P, 2])
        root = sb("root", [P, 2])
        scratch = sb("scratch", [P, 2])
        eps = sb("eps", [P, 1])
        rstd = sb("rstd", [P, 2])
        h = sb("h", [P, 2, D])
        g_rep = sb("g_rep", [P, D])
        a_hi = [sb(f"a_hi{s}", [P, KT, T], F32R) for s in range(2)]
        a_lo = [sb(f"a_lo{s}", [P, KT, T], F32R) for s in range(2)]
        raw = sb("raw", [P, 2, HK, BANK])
        w_hi = sb("w_hi", [P, 2, HK, BANK], F32R)
        w_lo = sb("w_lo", [P, 2, HK, BANK], F32R)
        relu = sb("relu", [P, 2, BANK])
        square_sb = sb("square", [P, 2, BANK])
        u_hi = sb("u_hi", [P, KT, T], F32R)
        u_lo = sb("u_lo", [P, KT, T], F32R)
        total = sb("total", [P, tiles, D])
        acc = ps("acc", [P, 4, BANK])
        turn = ps("turn", [P, 2, BANK])

        eps_ready = sem("eps_ready")
        gain_landed = sem("gain_landed")
        gain_ready = sem("gain_ready")
        x_landed = [sem(f"x_landed{s}") for s in range(2)]
        sumsq_ready = sem("sumsq_ready")
        root_ready = sem("root_ready")
        rstd_chain = sem("rstd_chain")
        rstd_ready = sem("rstd_ready")
        h_ready = sem("h_ready")
        turned = sem("turned")
        a_hi_ready = sem("a_hi_ready")
        a_ready = sem("a_ready")
        raw_landed = [sem(f"raw_landed{s}") for s in range(2)]
        w_hi_ready = [sem(f"w_hi_ready{s}") for s in range(2)]
        w_ready = [sem(f"w_ready{s}") for s in range(2)]
        first_half_used = sem("first_half_used")
        acc_full = [sem(f"acc_full{t}") for t in range(tiles)]
        acc_read = [sem(f"acc_read{t}") for t in range(tiles)]
        squared = [sem(f"squared{s}") for s in range(2)]
        u_hi_ready = [sem(f"u_hi_ready{s}") for s in range(2)]
        u_ready = sem("u_ready")
        total_landed = sem("total_landed")
        stored = sem("stored")
        block = ctx.enter_context(nc.Block())

        src_tiles = src.rearrange("(n p) d -> n p d", p=P)
        w1_rows = w1.rearrange("(h k p) c -> h p k c", k=HK, p=P)

        def each_quarter(eng, g, body):
            with eng.Fori(0, QUARTERS - 1) as q:
                body(q, q + g * QUARTERS, False)
            body(QUARTERS - 1, (g + 1) * QUARTERS - 1, True)

        def prepares(g, last, i):
            return last and g + 1 < groups and i == 0

        @block.sync
        def _(sp):
            sp.dma_start(g_rep[:], gain.broadcast_to([P, D])).then_inc(gain_landed, 16)

            def load_rows(n):
                if n >= 2:
                    sp.wait_ge(h_ready, n - 1)
                sp.dma_start(x_in[:, n % 2, :], src_tiles[n]).then_inc(x_landed[n % 2], 16)

            def quarter(g):
                def body(q, n, last):
                    for i in range(PER):
                        for half in range(2):
                            sp.wait_ge(w_ready[half], n * PER + i)
                            if i < 2:
                                w = w1_rows[half, :, :, bass.ds(q * D + i * BANK, BANK)]
                            else:
                                w = w2[bass.ds(q * D + half * BANK, BANK), (i - 2) * BANK:(i - 1) * BANK
                                       ].rearrange("(k p) c -> p k c", p=P)
                            sp.dma_start(raw[:, half], w).then_inc(raw_landed[half], 16)
                        if prepares(g, last, i):
                            for t in range(tiles):
                                load_rows((g + 1) * tiles + t)
                return body

            for t in range(tiles):
                load_rows(t)
            for g in range(groups):
                each_quarter(sp, g, quarter(g))
            sp.wait_ge(stored, groups * tiles * 16)

        @block.gpsimd
        def _(pool):
            def body(q, n, last):
                for i in range(PER):
                    for half in range(2):
                        m = n * PER + i
                        pool.wait_ge(w_hi_ready[half], m + 1)
                        pool.tensor_tensor(w_lo[:, half], raw[:, half], w_hi[:, half].bitcast(F32), ALU.subtract
                                           ).then_inc(w_ready[half], 1)
            for g in range(groups):
                each_quarter(pool, g, body)

        @block.scalar
        def _(act):
            def square(n):
                act.wait_ge(x_landed[n % 2], 16 * (n // 2 + 1))
                if n >= 1:
                    act.wait_ge(sumsq_ready, n)
                if n >= 2:
                    act.wait_ge(rstd_ready, n - 1)
                at = slice(n % 2, n % 2 + 1)
                act.activation(junk[:], x_in[:, n % 2, :], ACT.Square, accum_out=sumsq[:, at]
                               ).then_inc(sumsq_ready, 1)
                act.wait_ge(sumsq_ready, n + 1)
                act.activation(root[:, at], sumsq[:, at], ACT.Sqrt, bias=eps[:]).then_inc(root_ready, 1)

            def high_part(n, b):
                act.wait_ge(turned, 2 * n + b + 1)
                g, t = divmod(n, tiles)
                act.activation(a_hi[g % 2][:, b * HK:(b + 1) * HK, t * P:(t + 1) * P],
                               turn[:, b].rearrange("p (k c) -> p k c", k=HK), ACT.Copy
                               ).then_inc(a_hi_ready, 1)

            def high_square(n, i, t):
                s, m = t % 2, n * 4 + i * 2 + t // 2
                act.wait_ge(squared[s], m + 1)
                act.activation(u_hi[:, i * tiles + t], square_sb[:, s], ACT.Copy).then_inc(u_hi_ready[s], 1)

            def quarter(g):
                def body(q, n, last):
                    for i in range(PER):
                        for step in range(2 * tiles):
                            if prepares(g, last, i):
                                at = (g + 1) * tiles + step // 2
                                if step == 0:
                                    square(at)
                                if step % 2 == 0 and step < 2 * tiles - 2:
                                    square(at + 1)
                                high_part(at, step % 2)
                            t = step - tiles
                            if t < 0 or i >= 2:
                                continue
                            m = n * 4 + i * 2 + t // 2
                            act.wait_ge(acc_full[t], n * PER + i + 1)
                            act.wait_ge(squared[t % 2], m)
                            act.activation(relu[:, t % 2], acc[:, t], ACT.Relu).then_inc(acc_read[t], 1)
                            if t:
                                high_square(n, i, t - 1)
                        if i < 2:
                            high_square(n, i, tiles - 1)
                    if last:
                        for t in range(tiles):
                            act.wait_ge(acc_read[t], (n + 1) * PER)
                            act.dma_start(dst[(g * tiles + t) * P:(g * tiles + t + 1) * P, :], total[:, t]
                                          ).then_inc(stored, 16)
                return body

            act.wait_ge(eps_ready, 1)
            for n in range(tiles):
                square(n)
                high_part(n, 0)
                high_part(n, 1)
            for g in range(groups):
                act.wait_ge(stored, g * tiles * 16)
                for t in range(tiles):
                    act.dma_start(total[:, t], src_tiles[g * tiles + t]).then_inc(total_landed, 16)
                each_quarter(act, g, quarter(g))

        @block.vector
        def _(dve):
            dve.memset(eps[:], D * EPS).then_inc(eps_ready, 1)
            dve.wait_ge(gain_landed, 16)
            dve.tensor_scalar(g_rep[:], g_rep[:], math.sqrt(D), None, ALU.mult).then_inc(gain_ready, 1)
            dve.wait_ge(gain_ready, 1)

            def normalise(n):
                if n >= 2:
                    dve.wait_ge(turned, 2 * (n - 1))
                s = slice(n % 2, n % 2 + 1)
                dve.wait_ge(root_ready, n + 1)
                dve.tensor_scalar(sumsq[:, s], sumsq[:, s], D * EPS, None, ALU.add).then_inc(rstd_chain, 1)
                dve.reciprocal(rstd[:, s], root[:, s]).then_inc(rstd_chain, 1)
                dve.wait_ge(rstd_chain, n * 6 + 2)
                newton(dve, rstd_chain, n * 6 + 2, rstd[:, s], sumsq[:, s], scratch[:, s])
                dve.engine_nop().then_inc(rstd_ready, 1)
                dve.wait_ge(rstd_ready, n + 1)
                dve.scalar_tensor_tensor(h[:, n % 2], x_in[:, n % 2], rstd[:, s], g_rep[:],
                                         ALU.mult, ALU.mult).then_inc(h_ready, 1)

            def low_part(n, b):
                dve.wait_ge(a_hi_ready, 2 * n + b + 1)
                g, t = divmod(n, tiles)
                at = (slice(None), slice(b * HK, (b + 1) * HK), slice(t * P, (t + 1) * P))
                dve.tensor_tensor(a_lo[g % 2][at], turn[:, b].rearrange("p (k c) -> p k c", k=HK),
                                  a_hi[g % 2].bitcast(F32)[at], ALU.subtract).then_inc(a_ready, 1)

            def split_weights(m, half):
                dve.wait_ge(raw_landed[half], m * 16 + 16)
                dve.wait_ge(acc_full[tiles - 1] if half else first_half_used, m)
                dve.tensor_copy(w_hi[:, half], raw[:, half]).then_inc(w_hi_ready[half], 1)

            def low_square(n, i, t):
                s, m = t % 2, n * 4 + i * 2 + t // 2
                dve.wait_ge(u_hi_ready[s], m + 1)
                dve.tensor_tensor(u_lo[:, i * tiles + t], square_sb[:, s], u_hi[:, i * tiles + t].bitcast(F32),
                                  ALU.subtract).then_inc(u_ready, 1)

            def quarter(g):
                def body(q, n, last):
                    for i in range(PER):
                        c = n * PER + i
                        for step in range(2 * tiles):
                            if step == 0:
                                split_weights(c, 1)
                            elif step == tiles and not (last and g + 1 == groups and i == PER - 1):
                                split_weights(c + 1, 0)
                            if prepares(g, last, i):
                                at = (g + 1) * tiles + step // 2
                                if step % 2 == 0:
                                    normalise(at)
                                low_part(at, step % 2)
                            t = step - tiles
                            if t < 0:
                                continue
                            if i < 2:
                                m = n * 4 + i * 2 + t // 2
                                dve.wait_ge(acc_read[t], c + 1)
                                dve.wait_ge(u_ready, n * 2 * tiles + i * tiles + max(t - 1, 0))
                                dve.tensor_tensor(square_sb[:, t % 2], relu[:, t % 2], relu[:, t % 2], ALU.mult
                                                  ).then_inc(squared[t % 2], 1)
                                if t:
                                    low_square(n, i, t - 1)
                            else:
                                dve.wait_ge(acc_full[t], c + 1)
                                dve.wait_ge(total_landed, (g + 1) * tiles * 16)
                                at = (slice(None), t, slice((i - 2) * BANK, (i - 1) * BANK))
                                dve.tensor_tensor(total[at], acc[:, t], total[at], ALU.add).then_inc(acc_read[t], 1)
                        if i < 2:
                            low_square(n, i, tiles - 1)
                return body

            for n in range(tiles):
                normalise(n)
                low_part(n, 0)
                low_part(n, 1)
            split_weights(0, 0)
            for g in range(groups):
                each_quarter(dve, g, quarter(g))

        @block.tensor
        def _(pe):
            def turn_rows(n, b):
                pe.wait_ge(h_ready, n + 1)
                if n >= 1:
                    pe.wait_ge(a_ready, 2 * (n - 1) + b + 1)
                for k in range(HK):
                    at = (b * HK + k) * P
                    mm = pe.transpose(turn[:, b, k * P:(k + 1) * P], h[:, n % 2, at:at + P], ident[:])
                mm.then_inc(turned, 1)

            def products(i, s, half, t, n):
                cut = slice(t * P, (t + 1) * P)
                for k in range(HK):
                    a = half * HK + k
                    if i < 2:
                        terms = [(w_hi[:, half, k, cut], a_hi[s][:, a]), (w_hi[:, half, k, cut], a_lo[s][:, a]),
                                 (w_lo[:, half, k, cut], a_hi[s][:, a])]
                    else:
                        if t == 0:
                            pe.wait_ge(u_ready, n * 2 * tiles + a + 1)
                        terms = [(u_hi[:, a, cut], w_hi[:, half, k]), (u_hi[:, a, cut], w_lo[:, half, k]),
                                 (u_lo[:, a, cut], w_hi[:, half, k])]
                    for j, (left, right) in enumerate(terms):
                        mm = pe.matmul(acc[:, t], left, right, start=(half == 0 and k == 0 and j == 0),
                                       stop=(half == 1 and k == HK - 1 and j == 2))
                return mm

            def quarter(g):
                def body(q, n, last):
                    for i in range(PER):
                        c = n * PER + i
                        for half in range(2):
                            pe.wait_ge(w_ready[half], c + 1)
                            for t in range(tiles):
                                if half == 0:
                                    pe.wait_ge(acc_read[t], c)
                                mm = products(i, g % 2, half, t, n)
                                if half == 1:
                                    mm.then_inc(acc_full[t], 1)
                                elif t == tiles - 1:
                                    mm.then_inc(first_half_used, 1)
                                if prepares(g, last, i):
                                    step = half * tiles + t
                                    turn_rows((g + 1) * tiles + step // 2, step % 2)
                return body

            for n in range(tiles):
                turn_rows(n, 0)
                turn_rows(n, 1)
            for g in range(groups):
                pe.wait_ge(a_ready, 2 * (g + 1) * tiles)
                each_quarter(pe, g, quarter(g))


def decoder_layer(nc, x, mem, norm1_g, w_in, attn_qn_g, attn_kn_g, hg_lb, hg_onorm_g, w_out, norm2_g, mem_norm_g,
                  w_mq, w_mkv, mq_norm_g, mk_norm_g, w_mo, norm3_g, w_ff1, w_ff2, out):
    S = x.shape[0]
    groups = S // BANK

    def scratch(what, rows, cols):
        return nc.dram_tensor(what, [rows, cols], F32, kind="Internal").ap()

    z_rows = scratch("z_rows", S, 2560)
    z_columns = scratch("z_columns", 1536, S)
    branch_rows = [scratch(f"branch{b}", S, 528) for b in range(2)]
    y = scratch("y", S, D)
    x1 = scratch("x1", S, D)
    kvm = scratch("kvm", MEM, 2 * D)
    qm = scratch("qm", S, D)
    om = scratch("om", S, D)
    x2 = scratch("x2", S, D)

    with nc.cleanup_on_exit(), ExitStack() as ctx:
        ident = ctx.enter_context(nc.sbuf_tensor("ident", [P, P], F32))
        lb = ctx.enter_context(nc.sbuf_tensor("lb", [P, 4], F32))
        lb_exp = ctx.enter_context(nc.sbuf_tensor("lb_exp", [P, 4], F32))
        lb_p = ctx.enter_context(nc.sbuf_tensor("lb_p", [P, 4], F32))
        lower = ctx.enter_context(nc.sbuf_tensor("lower", [P, 4], F32))
        upper = ctx.enter_context(nc.sbuf_tensor("upper", [P, 4], F32))
        cleared = nc.alloc_semaphore("ident_cleared")
        ident_ready = nc.alloc_semaphore("ident_ready")
        lb_landed = nc.alloc_semaphore("lb_landed")
        lb_chain = nc.alloc_semaphore("lb_chain")
        lb_exped = nc.alloc_semaphore("lb_exped")
        with nc.Block() as block:
            @block.sync
            def _(sp):
                for t in range(4):
                    sp.dma_start(lb[:, t:t + 1], hg_lb[t * P:(t + 1) * P, :]).then_inc(lb_landed, 16)

            @block.gpsimd
            def _(pool):
                pool.memset(ident[:], 0.0).then_inc(cleared, 1)
                pool.wait_ge(cleared, 1)
                pool.affine_select(out=ident[:], in_=ident[:], compare_op=ALU.not_equal, fill=1.0, base=0,
                                   pattern=[[-1, P]], channel_multiplier=1).then_inc(ident_ready, 1)

            @block.vector
            def _(dve):
                dve.wait_ge(lb_landed, 64)
                dve.tensor_tensor(lb_exp[:], lb[:], lb[:], ALU.subtract).then_inc(lb_chain, 1)
                dve.wait_ge(lb_exped, 1)
                dve.reciprocal(lb_p[:], lb_exp[:]).then_inc(lb_chain, 1)
                dve.wait_ge(lb_chain, 2)
                dve.tensor_tensor(lb_p[:], lb_p[:], lb_exp[:], ALU.mult).then_inc(lb_chain, 1)
                dve.wait_ge(lb_chain, 3)
                dve.tensor_tensor(lower[:], lb_p[:], lb_p[:], ALU.subtract).then_inc(lb_chain, 1)
                dve.wait_ge(lb_chain, 4)
                dve.tensor_scalar(upper[:], lower[:], -1.0, 1.0, ALU.mult, ALU.add).then_inc(lb_chain, 1)

            @block.scalar
            def _(act):
                act.wait_ge(lb_chain, 1)
                act.activation(lb_exp[:], lb_exp[:], ACT.Exp).then_inc(lb_exped, 1)

        project(nc, "in", x, norm1_g, w_in,
                [("heads 64", 0, 2, z_rows, 0), ("rows", 2, 1, z_rows, 2), ("silu columns", 3, 1, z_columns, 0),
                 ("gates", 4, 1, (z_columns[BANK:2 * BANK], z_columns[2 * BANK:3 * BANK]), 0),
                 ("rows", 5, 1, z_rows, 3), ("silu rows", 6, 1, z_rows, 4)],
                groups, 4, ident, lower=(lower, upper))
        mix(nc, z_rows, z_columns, branch_rows, y, attn_qn_g, attn_kn_g, hg_onorm_g, ident)
        project(nc, "mkv", mem, mem_norm_g, w_mkv, [("heads 256", 0, 2, kvm, 0), ("rows", 2, 2, kvm, 2)], 1, 2, ident)
        project(nc, "out", y, None, w_out, [("rows", 0, 2, x1, 0)], groups, 4, ident, residual=x)
        project(nc, "mq", x1, norm2_g, w_mq, [("heads 256", 0, 2, qm, 0)], groups, 4, ident)
        attend_memory(nc, qm, kvm, om, mq_norm_g, mk_norm_g, ident)
        project(nc, "mo", om, None, w_mo, [("rows", 0, 2, x2, 0)], groups, 4, ident, residual=x1)
        feed_forward(nc, x2, norm3_g, w_ff1, w_ff2, out, ident)


_SHAPES = {
    "x": (2048, 1024), "mem": (256, 1024), "norm1_g": (1, 1024), "w_in": (1024, 3584), "attn_qn_g": (64, 1),
    "attn_kn_g": (64, 1), "hg_lb": (512, 1), "hg_onorm_g": (1, 512), "w_out": (1024, 1024), "norm2_g": (1, 1024),
    "mem_norm_g": (1, 1024), "w_mq": (1024, 1024), "w_mkv": (1024, 2048), "mq_norm_g": (256, 1),
    "mk_norm_g": (256, 1), "w_mo": (1024, 1024), "norm3_g": (1, 1024), "w_ff1": (1024, 4096), "w_ff2": (4096, 1024),
}


def kernel(**inputs):
    import numpy as _np
    import concourse.bacc as _bacc
    from concourse import mybir as _mybir
    from concourse.bass_utils import run_bass_kernel_spmd as _run

    nc = _bacc.Bacc("TRN2", target_bir_lowering=False, num_devices=1)
    arrays, args = {}, []
    for name, shape in _SHAPES.items():
        a = _np.ascontiguousarray(inputs[name]).reshape(shape)
        arrays[f"in_{name}"] = a
        args.append(nc.dram_tensor(f"in_{name}", shape, _mybir.dt.from_np(a.dtype), kind="ExternalInput").ap())
    args.append(nc.dram_tensor("out_0", (2048, 1024), F32, kind="ExternalOutput").ap())
    decoder_layer(nc, *args)
    r = _run(nc, [arrays], core_ids=[0])
    return r.results[0]["out_0"].reshape(1, 2048, 1024)
```

```python
import math

import concourse.bass as bass
from concourse import mybir
from contextlib import ExitStack

F32 = mybir.dt.float32
F32R = mybir.dt.float32r
ALU = mybir.AluOpType
ACT = mybir.ActivationFunctionType
AX = mybir.AxisListType

P = 128
BANK = 512
D = 1024
KT = D // P
HK = KT // 2
EPS = 1e-6
F_MIN = 1e-12


BESIDE_ONE = dict(square={0: [0], 1: [1], 3: [2], 5: [3]}, normalise={0: [0], 1: [1], 5: [2], 6: [3]},
                  turn={3: [0], 4: [1], 5: [2, 3], 6: [4, 5], 7: [6, 7]})
BESIDE_TWO = dict(square={0: [0], 2: [1], 6: [2], 10: [3]}, normalise={1: [0], 3: [1], 7: [2], 11: [3]},
                  turn={3: [0], 4: [1], 6: [2], 7: [3], 9: [4], 10: [5], 13: [6], 14: [7]})
TURN_ONLY = {1: [0], 2: [1], 3: [2], 4: [3], 5: [4], 6: [5], 7: [6, 7]}


def newton(dve, chain, at, r, v, t):
    dve.tensor_tensor(t, r, r, ALU.mult).then_inc(chain, 1)
    dve.wait_ge(chain, at + 1)
    dve.tensor_tensor(t, t, v, ALU.mult).then_inc(chain, 1)
    dve.wait_ge(chain, at + 2)
    dve.tensor_scalar(t, t, -0.5, 1.5, ALU.mult, ALU.add).then_inc(chain, 1)
    dve.wait_ge(chain, at + 3)
    dve.tensor_tensor(r, r, t, ALU.mult).then_inc(chain, 1)
    dve.wait_ge(chain, at + 4)


def project(nc, name, jobs, groups, tiles, ident, lower=None):
    T = tiles * P
    plans = [job[3] for job in jobs]
    chunks = sum(p[2] for p in plans[0])
    total = len(jobs) * groups
    gain = next((job[1] for job in jobs if job[1] is not None), None)

    def kinds_of(plan):
        return {p[0].split()[0]: sum(q[2] for q in plan if q[0].split()[0] == p[0].split()[0]) for p in plan}

    kinds = {k for plan in plans for k in kinds_of(plan)}
    head_width = next((int(p[0].split()[1]) for plan in plans for p in plan if p[0].startswith("heads")), BANK)
    NH = BANK // head_width
    with nc.cleanup_on_exit(), ExitStack() as ctx:
        def sb(what, shape, dt=F32):
            return ctx.enter_context(nc.sbuf_tensor(f"{name}_{what}", shape, dt))

        def ps(what, shape):
            return ctx.enter_context(nc.psum_tensor(f"{name}_{what}", shape, F32))

        def sem(what):
            return nc.alloc_semaphore(f"{name}_{what}")

        x_in = sb("x_in", [P, tiles, D])
        junk = sb("junk", [P, D])
        sumsq = sb("sumsq", [P, 2])
        root = sb("root", [P, 2])
        scratch = sb("scratch", [P, 2])
        eps = sb("eps", [P, 1])
        rstd = sb("rstd", [P, 2])
        h = sb("h", [P, 2, D]) if gain is not None else None
        g_rep = sb("g_rep", [P, D])
        a_hi = [sb(f"a_hi{s}", [P, KT, T], F32R) for s in range(2)]
        a_lo = [sb(f"a_lo{s}", [P, KT, T], F32R) for s in range(2)]
        raw = sb("raw", [P, 2, HK, BANK])
        w_hi = sb("w_hi", [P, 2, HK, BANK], F32R)
        w_lo = sb("w_lo", [P, 2, HK, BANK], F32R)
        out_sb = sb("out", [P, tiles, BANK])
        res = sb("res", [P, tiles, BANK]) if any(job[4] is not None for job in jobs) else None
        side = sb("side", [P, 2, BANK])
        keys = sb("keys", [P, tiles, BANK]) if "gates" in kinds else None
        head_sum = sb("head_sum", [P, 2, NH])
        head_rstd = sb("head_rstd", [P, 2, NH])
        head_scratch = sb("head_scratch", [P, 2, NH])
        acc = ps("acc", [P, 4, BANK])
        turn = ps("turn", [P, 2, BANK])

        gain_landed = sem("gain_landed")
        gain_ready = sem("gain_ready")
        x_landed = [sem(f"x_landed{t}") for t in range(tiles)]
        sumsq_ready = sem("sumsq_ready")
        eps_ready = sem("eps_ready")
        root_ready = sem("root_ready")
        rstd_chain = sem("rstd_chain")
        side_ready = {k: [sem(f"{k}_side{s}") for s in range(2)] for k in kinds}
        side_used = {k: [sem(f"{k}_used{s}") for s in range(2)] for k in kinds}
        keys_stored = [sem(f"keys_stored{t}") for t in range(tiles)]
        head_summed = sem("head_summed")
        head_rooted = sem("head_rooted")
        head_chain = sem("head_chain")
        rstd_ready = sem("rstd_ready")
        h_ready = sem("h_ready")
        turned = sem("turned")
        a_hi_ready = sem("a_hi_ready")
        a_ready = sem("a_ready")
        raw_landed = [sem(f"raw_landed{s}") for s in range(2)]
        w_hi_ready = [sem(f"w_hi_ready{s}") for s in range(2)]
        w_ready = [sem(f"w_ready{s}") for s in range(2)]
        first_half_used = sem("first_half_used")
        acc_full = [sem(f"acc_full{t}") for t in range(tiles)]
        acc_read = [sem(f"acc_read{t}") for t in range(tiles)]
        out_stored = [sem(f"out_stored{t}") for t in range(tiles)]
        res_landed = [sem(f"res_landed{t}") for t in range(tiles)]
        block = ctx.enter_context(nc.Block())

        def job_of(g):
            return jobs[g // groups], g % groups

        def has_gain(n):
            return job_of(n // tiles)[0][1] is not None

        def turns_beside(g, step):
            return (BESIDE_ONE["turn"] if has_gain((g + 1) * tiles) else TURN_ONLY).get(step, [])

        def gained(n):
            return sum(has_gain(i) for i in range(n))

        def destination(kind, dst, j, g, t):
            if by_rows(kind):
                return dst[g * T + t * P:g * T + (t + 1) * P, bass.ds(j * BANK, BANK)]
            return dst[bass.ds(j * BANK + t * P, P), g * T:(g + 1) * T]

        def each_chunk(eng, g, body):
            n0 = g * chunks
            (_, _, _, plan, _), own = job_of(g)
            seen = {k: own * v for k, v in kinds_of(plan).items()}
            for i, (what, c0, count, dst, d0) in enumerate(plan):
                final = i == len(plan) - 1
                looped = count - 1 if final else count
                m0 = seen[what.split()[0]]
                if looped > 1:
                    with eng.Fori(0, looped) as r:
                        body(what, r + c0, dst, r + d0, r + n0, r + m0, False)
                elif looped == 1:
                    body(what, c0, dst, d0, n0, m0, False)
                n0 += count
                seen[what.split()[0]] += count
                if final:
                    body(what, c0 + count - 1, dst, d0 + count - 1, n0 - 1, m0 + count - 1, True)

        def by_rows(kind):
            return kind.startswith("heads") or kind.endswith("rows")

        def prepares(g, last):
            return last and g + 1 < total

        @block.sync
        def _(sp):
            def load_rows(n):
                if n >= tiles and has_gain(n - tiles):
                    sp.wait_ge(h_ready, gained(n - tiles) + 1)
                elif n >= tiles:
                    sp.wait_ge(turned, 2 * (n - tiles + 1))
                (src, _, _, _, _), own = job_of(n // tiles)
                t = n % tiles
                if n >= groups * tiles:
                    sp.wait_ge(out_stored[t], 16 * chunks * (n // tiles - groups + 1))
                sp.dma_start(x_in[:, t, :], src[(own * tiles + t) * P:(own * tiles + t + 1) * P, :]
                             ).then_inc(x_landed[t], 16)

            def chunk(g):
                (_, _, weight, _, residual), own = job_of(g)
                w_rows = weight.rearrange("(h k p) c -> h p k c", k=HK, p=P)

                def body(kind, c, dst, j, n, m, last):
                    for half in range(2):
                        sp.wait_ge(w_ready[half], n)
                        sp.dma_start(raw[:, half], w_rows[half, :, :, bass.ds(c * BANK, BANK)]
                                     ).then_inc(raw_landed[half], 16)
                        if prepares(g, last):
                            for t in (0, 1) if half == 0 else (2, 3):
                                load_rows((g + 1) * tiles + t)
                    if residual is not None:
                        for t in range(tiles):
                            sp.wait_ge(acc_read[t], n)
                            sp.dma_start(res[:, t], destination("rows", residual, j, own, t)
                                         ).then_inc(res_landed[t], 16)
                return body

            for t in range(tiles):
                load_rows(t)
                if t == 0 and gain is not None:
                    sp.dma_start(g_rep[:], gain.broadcast_to([P, D])).then_inc(gain_landed, 16)
            for g in range(total):
                each_chunk(sp, g, chunk(g))
            for t in range(tiles):
                sp.wait_ge(out_stored[t], 16 * total * chunks)
                if "gates" in kinds:
                    sp.wait_ge(keys_stored[t], 16 * groups * kinds_of(plans[0])["gates"])

        @block.gpsimd
        def _(pool):
            def chunk(kind, c, dst, j, n, m, last):
                for half in range(2):
                    pool.wait_ge(w_hi_ready[half], n + 1)
                    pool.tensor_tensor(w_lo[:, half], raw[:, half], w_hi[:, half].bitcast(F32), ALU.subtract
                                       ).then_inc(w_ready[half], 1)
            for g in range(total):
                each_chunk(pool, g, chunk)

        @block.scalar
        def _(act):
            def square(n):
                i = gained(n)
                at = slice(i % 2, i % 2 + 1)
                act.wait_ge(x_landed[n % tiles], 16 * (n // tiles + 1))
                if i >= 1:
                    act.wait_ge(sumsq_ready, i)
                if i >= 2:
                    act.wait_ge(rstd_ready, i - 1)
                act.activation(junk[:], x_in[:, n % tiles, :], ACT.Square, accum_out=sumsq[:, at]
                               ).then_inc(sumsq_ready, 1)
                act.wait_ge(sumsq_ready, i + 1)
                act.activation(root[:, at], sumsq[:, at], ACT.Sqrt, bias=eps[:]).then_inc(root_ready, 1)

            def high_part(n, b):
                act.wait_ge(turned, 2 * n + b + 1)
                g, t = divmod(n, tiles)
                act.activation(a_hi[g % 2][:, b * HK:(b + 1) * HK, t * P:(t + 1) * P],
                               turn[:, b].rearrange("p (k c) -> p k c", k=HK), ACT.Copy
                               ).then_inc(a_hi_ready, 1)

            def finish(kind, t, n, m):
                s, w = t % 2, m * (tiles // 2) + t // 2
                if kind in ("rows", "columns"):
                    act.wait_ge(out_stored[t], n * 16)
                    act.activation(out_sb[:, t], acc[:, t], ACT.Copy).then_inc(acc_read[t], 1)
                elif kind == "silu":
                    act.activation(side[:, s], acc[:, t], ACT.Sigmoid).then_inc(side_ready[kind][s], 1)
                elif kind == "gates":
                    act.wait_ge(keys_stored[t], m * 16)
                    act.activation(keys[:, t], acc[:, t], ACT.Sigmoid, scale=-1.0)
                    act.activation(side[:, s], acc[:, t], ACT.Sigmoid).then_inc(side_ready[kind][s], 1)
                elif kind == "heads":
                    act.activation(side[:, s], acc[:, t], ACT.Square).then_inc(side_ready[kind][s], 1)
                    if s == 1:
                        act.wait_ge(head_summed, w + 1)
                        act.activation(head_rstd[:], head_sum[:], ACT.Sqrt).then_inc(head_rooted, 1)

            def chunk(g):
                (_, _, _, _, residual), own = job_of(g)

                def body(kind, c, dst, j, n, m, last):
                    for step in range(2 * tiles):
                        if prepares(g, last):
                            for i in BESIDE_ONE["square"].get(step, []) if has_gain((g + 1) * tiles) else []:
                                square((g + 1) * tiles + i)
                            for i in turns_beside(g, step):
                                high_part((g + 1) * tiles + i // 2, i % 2)
                        t = step - tiles
                        if t < 0:
                            continue
                        act.wait_ge(acc_full[t], n + 1)
                        if residual is None:
                            finish(kind.split()[0], t, n, m)
                        first = dst[0] if kind == "gates" else dst
                        for o in (t,) if not kind.startswith("heads") else (t - 1, t) if t % 2 else ():
                            act.wait_ge(acc_read[o], n + 1)
                            act.dma_start(destination(kind, first, j, own, o), out_sb[:, o]).then_inc(out_stored[o], 16)
                        if kind == "gates":
                            act.dma_start(destination(kind, dst[1], j, own, t), keys[:, t]).then_inc(keys_stored[t], 16)
                return body

            act.wait_ge(eps_ready, 1)
            for n in range(tiles):
                if has_gain(n) and n == 0:
                    square(0)
                if has_gain(n) and n + 1 < tiles:
                    square(n + 1)
                high_part(n, 0)
                high_part(n, 1)
            for g in range(total):
                each_chunk(act, g, chunk(g))

        @block.vector
        def _(dve):
            dve.memset(eps[:], D * EPS).then_inc(eps_ready, 1)
            if gain is not None:
                dve.wait_ge(gain_landed, 16)
                dve.tensor_scalar(g_rep[:], g_rep[:], math.sqrt(D), None, ALU.mult
                                  ).then_inc(gain_ready, 1)
                dve.wait_ge(gain_ready, 1)

            def normalise(n):
                i = gained(n)
                if i >= 2:
                    dve.wait_ge(turned, 2 * (n - 1))
                s = slice(i % 2, i % 2 + 1)
                dve.wait_ge(root_ready, i + 1)
                dve.tensor_scalar(sumsq[:, s], sumsq[:, s], D * EPS, None, ALU.add).then_inc(rstd_chain, 1)
                dve.reciprocal(rstd[:, s], root[:, s]).then_inc(rstd_chain, 1)
                dve.wait_ge(rstd_chain, i * 6 + 2)
                newton(dve, rstd_chain, i * 6 + 2, rstd[:, s], sumsq[:, s], scratch[:, s])
                dve.engine_nop().then_inc(rstd_ready, 1)
                dve.wait_ge(rstd_ready, i + 1)
                dve.scalar_tensor_tensor(h[:, i % 2], x_in[:, n % tiles], rstd[:, s], g_rep[:],
                                         ALU.mult, ALU.mult).then_inc(h_ready, 1)

            def low_part(n, b):
                dve.wait_ge(a_hi_ready, 2 * n + b + 1)
                g, t = divmod(n, tiles)
                at = (slice(None), slice(b * HK, (b + 1) * HK), slice(t * P, (t + 1) * P))
                dve.tensor_tensor(a_lo[g % 2][at], turn[:, b].rearrange("p (k c) -> p k c", k=HK),
                                  a_hi[g % 2].bitcast(F32)[at], ALU.subtract).then_inc(a_ready, 1)

            def split_weights(n, half):
                dve.wait_ge(raw_landed[half], n * 16 + 16)
                dve.wait_ge(acc_full[tiles - 1] if half else first_half_used, n)
                dve.tensor_copy(w_hi[:, half], raw[:, half]).then_inc(w_hi_ready[half], 1)

            def finish(kind, t, n, m):
                s, w = t % 2, m * (tiles // 2) + t // 2
                if kind in ("rows", "columns"):
                    return
                dve.wait_ge(out_stored[t], n * 16)
                dve.wait_ge(side_ready[kind][s], w + 1)
                if kind == "silu":
                    dve.tensor_tensor(out_sb[:, t], acc[:, t], side[:, s], ALU.mult).then_inc(acc_read[t], 1)
                elif kind == "gates":
                    dve.tensor_scalar(keys[:, t], keys[:, t], lower[1][:, t:t + 1], None, ALU.mult)
                    dve.tensor_scalar(out_sb[:, t], side[:, s], lower[1][:, t:t + 1], lower[0][:, t:t + 1],
                                      ALU.mult, ALU.add).then_inc(side_used[kind][s], 1)
                    dve.wait_ge(side_used[kind][s], w + 1)
                    dve.tensor_scalar(out_sb[:, t], out_sb[:, t], F_MIN, None, ALU.max).then_inc(acc_read[t], 1)
                elif kind == "heads":
                    at = w * 7
                    dve.tensor_reduce(head_sum[:, s], side[:, s].rearrange("p (h e) -> p h e", h=NH), AX.X, ALU.add
                                      ).then_inc(head_chain, 1)
                    if s == 0:
                        return
                    dve.wait_ge(head_chain, at + 2)
                    dve.tensor_scalar(head_sum[:], head_sum[:], head_width * EPS, None, ALU.add
                                      ).then_inc(head_summed, 1)
                    dve.wait_ge(head_rooted, w + 1)
                    dve.reciprocal(head_rstd[:], head_rstd[:]).then_inc(head_chain, 1)
                    dve.wait_ge(head_chain, at + 3)
                    newton(dve, head_chain, at + 3, head_rstd[:], head_sum[:], head_scratch[:])
                    for i, o in enumerate((t - 1, t)):
                        dve.scalar_tensor_tensor(out_sb[:, o].rearrange("p (h e) -> p h e", h=NH),
                                                 acc[:, o].rearrange("p (h e) -> p h e", h=NH), math.sqrt(head_width),
                                                 head_rstd[:, i].unsqueeze(2).broadcast_to([P, NH, head_width]),
                                                 ALU.mult, ALU.mult).then_inc(acc_read[o], 1)

            def chunk(g):
                (_, _, _, _, residual), _ = job_of(g)

                def body(kind, c, dst, j, n, m, last):
                    for step in range(2 * tiles):
                        if step == tiles and not (last and g + 1 == total):
                            split_weights(n + 1, 0)
                        if prepares(g, last):
                            for i in BESIDE_ONE["normalise"].get(step, []) if has_gain((g + 1) * tiles) else []:
                                normalise((g + 1) * tiles + i)
                            for i in turns_beside(g, step):
                                low_part((g + 1) * tiles + i // 2, i % 2)
                        t = step - tiles
                        if t == tiles - 1 and not last:
                            split_weights(n + 1, 1)
                        if t >= 0 and residual is not None:
                            dve.wait_ge(acc_full[t], n + 1)
                            dve.wait_ge(res_landed[t], n * 16 + 16)
                            dve.wait_ge(out_stored[t], n * 16)
                            dve.tensor_tensor(out_sb[:, t], acc[:, t], res[:, t], ALU.add
                                              ).then_inc(acc_read[t], 1)
                        elif t >= 0:
                            finish(kind.split()[0], t, n, m)
                    if prepares(g, last):
                        split_weights(n + 1, 1)
                return body

            for n in range(tiles):
                if has_gain(n) and n == 0:
                    normalise(0)
                if has_gain(n) and n + 1 < tiles:
                    normalise(n + 1)
                low_part(n, 0)
                low_part(n, 1)
                if n == 1:
                    split_weights(0, 0)
            split_weights(0, 1)
            for g in range(total):
                each_chunk(dve, g, chunk(g))

        @block.tensor
        def _(pe):
            def turn_rows(n, b):
                if has_gain(n):
                    pe.wait_ge(h_ready, gained(n) + 1)
                else:
                    pe.wait_ge(x_landed[n % tiles], 16 * (n // tiles + 1))
                if n >= 1:
                    pe.wait_ge(a_ready, 2 * (n - 1) + b + 1)
                rows = h[:, gained(n) % 2] if has_gain(n) else x_in[:, n % tiles]
                for k in range(HK):
                    at = (b * HK + k) * P
                    mm = pe.transpose(turn[:, b, k * P:(k + 1) * P], rows[:, at:at + P], ident[:])
                mm.then_inc(turned, 1)

            def products(kind, s, half, t, first, final):
                for k in range(HK):
                    a = half * HK + k
                    cut = slice(t * P, (t + 1) * P)
                    if by_rows(kind):
                        terms = [(a_hi[s][:, a, cut], w_hi[:, half, k]), (a_hi[s][:, a, cut], w_lo[:, half, k]),
                                 (a_lo[s][:, a, cut], w_hi[:, half, k])]
                    else:
                        terms = [(w_hi[:, half, k, cut], a_hi[s][:, a]), (w_hi[:, half, k, cut], a_lo[s][:, a]),
                                 (w_lo[:, half, k, cut], a_hi[s][:, a])]
                    for i, (left, right) in enumerate(terms):
                        mm = pe.matmul(acc[:, t], left, right, start=(first and k == 0 and i == 0),
                                       stop=(final and k == HK - 1 and i == 2))
                return mm

            def chunk(g):
                def body(kind, c, dst, j, n, m, last):
                    for half in range(2):
                        pe.wait_ge(w_ready[half], n + 1)
                        for t in range(tiles):
                            if prepares(g, last):
                                for i in turns_beside(g, half * tiles + t):
                                    turn_rows((g + 1) * tiles + i // 2, i % 2)
                            if half == 0:
                                pe.wait_ge(acc_read[t], n)
                            mm = products(kind, g % 2, half, t, half == 0, half == 1)
                            if half == 1:
                                mm.then_inc(acc_full[t], 1)
                            elif t == tiles - 1:
                                mm.then_inc(first_half_used, 1)
                return body

            for n in range(tiles):
                turn_rows(n, 0)
                turn_rows(n, 1)
            for g in range(total):
                pe.wait_ge(a_ready, 2 * (g + 1) * tiles)
                each_chunk(pe, g, chunk(g))


HEADS, HD = 8, 64
AW = HEADS * HD
SEQ = 2048
DILATIONS = (16, 4, 1)
NEG = -1e30
OW = AW + 2 * HEADS
HH = 4
HGW = HH * P
LEVELS = 7
C = P
STEPS = 2 * HEADS


def mix(nc, z_rows, z_columns, branch_rows, y, q_gain, k_gain, onorm_g, ident):
    name = "mix"
    with nc.cleanup_on_exit(), ExitStack() as ctx:
        def sb(what, shape, dt=F32):
            return ctx.enter_context(nc.sbuf_tensor(f"{name}_{what}", shape, dt))

        def ps(what, shape):
            return ctx.enter_context(nc.psum_tensor(f"{name}_{what}", shape, F32))

        def sem(what):
            return nc.alloc_semaphore(f"{name}_{what}")

        gains = sb("gains", [P, 2])
        gain = sb("gain", [P, 1])
        step = sb("step", [P, 2 * P])
        hidden = sb("hidden", [P, 2 * P])
        bias = sb("bias", [P, len(DILATIONS) * HEADS, 2 * P])
        qk_in = sb("qk_in", [P, 2, 2 * AW])
        v_in = sb("v_in", [P, 4, AW])
        a_gate = sb("a_gate", [1, 2])
        q_t = sb("q_t", [P, 2, 4, P])
        k_t = sb("k_t", [P, 2, 4, P])
        p_sb = sb("p", [P, 2, 2 * P])
        pt_sb = sb("pt_sb", [P, 2, 2, P])
        o_sb = sb("o", [P, 2, OW])
        score = ps("score", [P, 2, BANK])
        pt = ps("pt", [P, 2, BANK])
        o_acc = ps("o_acc", [P, BANK])
        turn = ps("turn", [P, BANK])
        others = sb("others", [P, 2, 2, OW])
        least = sb("least", [P, 2, HEADS])
        gap = sb("gap", [P, 2, 3, HEADS])
        total = sb("total", [P, 2, 3, HEADS])
        norm = sb("norm", [P, 2, HEADS])
        scaled = sb("scaled", [P, 2, 3, AW])
        joined_sb = sb("joined_sb", [P, 2, AW])

        gains_landed = sem("gains_landed")
        gain_ready = sem("gain_ready")
        step_ready = sem("step_ready")
        hidden_set = sem("hidden_set")
        hidden_ready = sem("hidden_ready")
        bias_ready = sem("bias_ready")
        qk_landed = [sem(f"qk_landed{s}") for s in range(2)]
        v_landed = [sem(f"v_landed{s}") for s in range(2)]
        q_turned = [sem(f"q_turned{s}") for s in range(2)]
        k_turned_a = [sem(f"k_turned_a{s}") for s in range(2)]
        q_staged = [sem(f"q_staged{s}") for s in range(2)]
        k_staged = [sem(f"k_staged{s}") for s in range(2)]
        a_full = [sem(f"a_full{p}") for p in range(2)]
        masked = [sem(f"masked{p}") for p in range(2)]
        weighed = [sem(f"weighed{p}") for p in range(2)]
        pt_full = [sem(f"pt_full{p}") for p in range(2)]
        pt_read = [sem(f"pt_read{p}") for p in range(2)]
        pv_done = [sem(f"pv_done{p}") for p in range(2)]
        o_read = [sem(f"o_read{s}") for s in range(2)]
        o_stored = [sem(f"o_stored{s}") for s in range(2)]
        others_landed = [sem(f"others_landed{s}") for s in range(2)]
        join_chain = sem("join_chain")
        gap_ready = sem("gap_ready")
        gap_exped = sem("gap_exped")
        shares_ready = sem("shares_ready")
        own_scaled = [sem(f"own_scaled{s}") for s in range(2)]
        other_scaled = sem("other_scaled")
        paired = sem("paired")
        joined = [sem(f"joined{s}") for s in range(2)]
        y_stored = [sem(f"y_stored{s}") for s in range(2)]

        I32 = mybir.dt.int32
        row_i = sb("row_i", [P, C], I32)
        col_i = sb("col_i", [P, C], I32)
        after = sb("after", [P, C], I32)
        differ = sb("differ", [P, C], I32)
        later = sb("later", [P, C], I32)
        gate = sb("gate", [1, LEVELS + 1])
        top = sb("top", [P, C], I32)
        mask = sb("mask", [P, LEVELS + 1, C], I32)
        restart = sb("restart", [P, HH, C])
        og = sb("og", [P, HGW])
        q_in = sb("q_in", [P, 2, HH, C])
        k_in = sb("k_in", [P, 2, HH, C])
        f_in = sb("f_in", [P, 2, HH, C])
        ig_in = sb("ig_in", [P, 2, 2 * HGW])
        b = sb("b", [P, 2, HH, C])
        diff = sb("diff", [P, 2, HH, C])
        decay = sb("decay", [P, 2, HH, C])
        q_dec = sb("q_dec", [P, LEVELS + 1, HH, C])
        k_dec = sb("k_dec", [P, LEVELS + 1, HH, C])
        b_exp = sb("b_exp", [P, HH, C])
        last_exp = sb("last_exp", [P, HH])
        k_rows = sb("k_rows", [P, HH, C])
        s_sb = sb("s_sb", [P, 2, HH, C])
        state = sb("state", [P, HH, C])
        squares = sb("squares", [P, HH, C])
        ms = sb("ms", [P, 4, HH])
        gated = sb("gated", [P, 2, HGW])
        out = sb("out", [P, 2, HGW])
        s_ps = ps("s_ps", [P, 2, BANK])
        st_ps, o_ps = s_ps[:, 0], s_ps[:, 1]

        consts = sem("consts")
        og_landed = sem("og_landed")
        iotas = sem("iotas")
        masks = sem("masks")
        cleared = sem("cleared")
        in_landed = [sem(f"in_landed{s}") for s in range(2)]
        ig_landed = [sem(f"ig_landed{s}") for s in range(2)]
        logged = sem("logged")
        summed = sem("summed")
        diffed = [sem(f"diffed{p}") for p in range(2)]
        k_diffed = [sem(f"k_diffed{p}") for p in range(2)]
        exped = [sem(f"exped{p}") for p in range(2)]
        b_exped = sem("b_exped")
        last_exped = sem("last_exped")
        q_scaled = sem("q_scaled")
        k_scaled = sem("k_scaled")
        s_full = [sem(f"s_full{p}") for p in range(2)]
        s_read = [sem(f"s_read{p}") for p in range(2)]
        k_turned = sem("k_turned")
        k_rows_ready = sem("k_rows_ready")
        st_full = sem("st_full")
        st_ready = sem("st_ready")
        o_full = [sem(f"o_full{s}") for s in range(2)]
        squared = sem("squared")
        mean_ready = sem("mean_ready")
        ln_ready = sem("ln_ready")
        rstd0 = sem("rstd0")
        chain = sem("chain")
        gated_ready = sem("gated_ready")
        out_ready = [sem(f"out_ready{s}") for s in range(2)]
        out_stored = [sem(f"out_stored{s}") for s in range(2)]
        block = ctx.enter_context(nc.Block())

        def rows(t, d, r, n, cols):
            if d == 1:
                return t[bass.ds(n * P, P), cols]
            v = t.rearrange("(j d) c -> j d c", d=d)
            return v[n * P:(n + 1) * P, bass.ds(r, 1), cols].rearrange("j o c -> j (o c)")

        def pt_of(p, lo):
            return pt[:, p, lo:2 * P].rearrange("p (k c) -> p k c", c=P)

        def run(eng, attention, recurrence, join):
            def beside(one, other):
                for _ in zip(one, other):
                    pass

            with eng.Fori(0, 4) as m:
                def blocks():
                    before = None
                    for n in range(4):
                        this = (m * 4 + n, m * 2 + n // 2, n, (0, DILATIONS[0], m * 4 + n, 0), False)
                        yield from attention(*this, False, before)
                        before = this

                def chunks():
                    for s in range(2):
                        yield from recurrence(m * 2 + s, m, s)
                beside(blocks(), chunks())
            with eng.Fori(0, 4) as r:
                def blocks():
                    before = None
                    for n in range(4):
                        this = (r * 4 + 16 + n, r * 2 + 8 + n // 2, n, (1, DILATIONS[1], r, n), n > 0)
                        yield from attention(*this, n < 3, before)
                        before = this

                def chunks():
                    for s in range(2):
                        yield from recurrence(r * 2 + 8 + s, r + 4, s)
                beside(blocks(), chunks())

            def four(m, first, final):
                before = None
                for n in range(4):
                    this = (m * 4 + 32 + n, m * 2 + 16 + n // 2, n, (2, DILATIONS[2], 0, m * 4 + n),
                            not (first and n == 0))
                    a = attention(*this, None if final and n == 3 else True, before)
                    before = this
                    if first and n == 0:
                        for _ in a:
                            pass
                    else:
                        v = m * 4 + n - 1
                        w = m * 2 + (n - 1) // 2
                        beside(a, join(v, w, (n - 1) % 2))

            four(0, True, False)
            with eng.Fori(1, 3) as m:
                four(m, False, False)
            four(3, False, True)
            for _ in join(15, 7, 1):
                pass

        def idle_blocks(*args):
            yield from range(HEADS)

        def blocks_of(t, lev):
            half = C >> (lev + 1)
            return t.rearrange("p h (n two c) -> p (h n) two c", two=2, c=half)

        @block.sync
        def _(sp):
            for i, g in enumerate((q_gain, k_gain)):
                for half in range(2):
                    sp.dma_start(gains[half * HD:(half + 1) * HD, i:i + 1], g).then_inc(gains_landed, 16)
            sp.dma_start(og[:], onorm_g.broadcast_to([P, HGW])).then_inc(og_landed, 16)

            def attention(u, c, n4, at, prev, nxt, before):
                _, d, r, n = at
                s = n4 % 2
                sp.wait_ge(k_turned_a[s], c)
                sp.dma_start(qk_in[:, s], rows(z_rows, d, r, n, slice(0, 2 * AW))).then_inc(qk_landed[s], 16)
                sp.wait_ge(o_read[s], c)
                sp.dma_start(v_in[:, n4], rows(z_rows, d, r, n, slice(2 * AW, 3 * AW))
                             ).then_inc(v_landed[s], 16)
                yield from range(HEADS)

            def recurrence(u, c, s):
                sp.wait_ge(out_ready[s], c)
                for t, r0 in ((q_in, 0), (f_in, HGW), (k_in, 2 * HGW)):
                    sp.dma_start(t[:, s], z_columns[r0:r0 + HGW, bass.ds(u * C, C)].rearrange("(h p) c -> p h c", p=P)
                                 ).then_inc(in_landed[s], 16)
                sp.dma_start(ig_in[:, s], z_rows[bass.ds(u * C, C), 3 * AW:3 * AW + 2 * HGW]).then_inc(ig_landed[s], 16)
                yield from range(STEPS)

            def join(v, w, s):
                sp.wait_ge(o_stored[0], 16 * 16)
                sp.wait_ge(o_stored[1], 16 * 16)
                sp.wait_ge(joined[s], w)
                for i in range(2):
                    sp.dma_start(others[:, s, i], branch_rows[i][bass.ds(v * P, P), :]).then_inc(others_landed[s], 16)
                yield from range(HEADS)

            run(sp, attention, recurrence, join)
            for s in range(2):
                sp.wait_ge(o_stored[s], 16 * 16)
                sp.wait_ge(y_stored[s], 16 * 8)
                sp.wait_ge(out_stored[s], 16 * 8)

        @block.gpsimd
        def _(pool):
            pool.iota(step[:], pattern=[[-1, 2 * P]], base=P, channel_multiplier=1,
                      allow_small_or_imprecise_dtypes=True).then_inc(step_ready, 1)
            pool.memset(hidden[:], 0.0).then_inc(hidden_set, 1)
            pool.wait_ge(hidden_set, 1)
            pool.affine_select(out=hidden[:], in_=hidden[:], compare_op=ALU.is_ge, fill=NEG, base=P,
                               pattern=[[-1, 2 * P]], channel_multiplier=1).then_inc(hidden_set, 1)
            pool.wait_ge(hidden_set, 2)
            pool.affine_select(out=hidden[:], in_=hidden[:], compare_op=ALU.is_ge, fill=NEG, base=0,
                               pattern=[[1, 2 * P]], channel_multiplier=-1).then_inc(hidden_ready, 1)
            pool.iota(row_i[:], pattern=[[0, C]], base=0, channel_multiplier=1).then_inc(iotas, 1)
            pool.iota(col_i[:], pattern=[[1, C]], base=0, channel_multiplier=0).then_inc(iotas, 1)
            pool.iota(later[:], pattern=[[1, C]], base=0, channel_multiplier=-1).then_inc(iotas, 1)
            pool.memset(restart[:], 1.0).then_inc(consts, 1)
            pool.wait_ge(consts, 1)
            pool.memset(restart[:, :, 0:1], 0.0).then_inc(consts, 1)
            for t in (s_sb, state, k_dec, q_dec):
                pool.memset(t[:], 0.0).then_inc(cleared, 1)
            pool.wait_ge(cleared, 4)

            def recurrence(u, c, s):
                for at in range(STEPS):
                    lev = at - 1
                    if 0 <= lev < LEVELS:
                        if lev == 0:
                            pool.wait_ge(summed, u + 1)
                        pool.wait_ge(exped[lev % 2], u * 4 + lev // 2)
                        half = C >> (lev + 1)
                        bb, dd = blocks_of(b[:, s], lev), blocks_of(diff[:, lev % 2], lev)
                        edge = bb[:, :, 0, half - 1:half].broadcast_to([P, HH * C // half // 2, half])
                        pool.tensor_tensor(dd[:, :, 0], edge, bb[:, :, 0], ALU.subtract).then_inc(k_diffed[lev % 2], 1)
                    lev = at - 3
                    if 0 <= lev <= LEVELS:
                        if lev == 0:
                            pool.wait_ge(in_landed[s], c * 48 + 48)
                        p, w = lev % 2, u * 4 + lev // 2
                        if lev < LEVELS:
                            pool.wait_ge(s_full[(lev + 1) % 2], u * 4)
                            pool.wait_ge(exped[p], w + 1)
                            o, i, e = (blocks_of(t, lev)[:, :, 0] for t in (k_dec[:, lev], k_in[:, s], decay[:, p]))
                            pool.tensor_tensor(o, i, e, ALU.mult).then_inc(k_scaled, 1)
                        else:
                            pool.wait_ge(k_turned, u)
                            pool.wait_ge(exped[p], w + 1)
                            pool.tensor_tensor(k_dec[:, lev], k_in[:, s], decay[:, p], ALU.mult).then_inc(k_scaled, 1)
                    if lev == LEVELS + 1:
                        pool.wait_ge(ig_landed[s], c * 16 + 16)
                        pool.wait_ge(og_landed, 16)
                        pool.wait_ge(out_ready[s], c)
                        pool.tensor_tensor(gated[:, s], ig_in[:, s, HGW:], og[:], ALU.mult).then_inc(gated_ready, 1)
                    yield

            def join(v, w, s):
                for at in range(HEADS):
                    if at == 5:
                        pool.wait_ge(shares_ready, v + 1)
                        pool.wait_ge(joined[s], w)
                        for i in range(2):
                            x = pool.tensor_tensor(scaled[:, s, i].rearrange("p (h e) -> p h e", e=HD),
                                                   others[:, s, i, 0:AW].rearrange("p (h e) -> p h e", e=HD),
                                                   gap[:, s, i].unsqueeze(2).broadcast_to([P, HEADS, HD]), ALU.mult)
                        x.then_inc(other_scaled, 1)
                    if at == 6:
                        pool.wait_ge(other_scaled, v + 1)
                        pool.tensor_tensor(scaled[:, s, 0], scaled[:, s, 0], scaled[:, s, 1], ALU.add).then_inc(paired, 1)
                    yield

            run(pool, idle_blocks, recurrence, join)

        @block.vector
        def _(dve):
            dve.wait_ge(gains_landed, 64)
            dve.scalar_tensor_tensor(gain[:], gains[:, 0:1], 1 / math.sqrt(HD), gains[:, 1:2],
                                     ALU.mult, ALU.mult).then_inc(gain_ready, 1)
            dve.wait_ge(step_ready, 1)
            dve.wait_ge(hidden_ready, 1)
            for i, d in enumerate(DILATIONS):
                for e in range(HEADS):
                    slope = 2.0 ** (-8.0 / HEADS * (e + 1))
                    dve.scalar_tensor_tensor(bias[:, i * HEADS + e], step[:], -slope * d, hidden[:],
                                             ALU.mult, ALU.add).then_inc(bias_ready, 1)
            dve.wait_ge(iotas, 3)
            dve.tensor_tensor(differ[:], row_i[:], col_i[:], ALU.bitwise_xor).then_inc(masks, 1)
            dve.tensor_scalar(after[:], later[:], 0, None, ALU.is_gt).then_inc(masks, 1)
            dve.wait_ge(masks, 2)
            dve.tensor_scalar(mask[:, 0], differ[:], 0, None, ALU.is_equal).then_inc(masks, 1)
            for lev in range(LEVELS):
                dve.wait_ge(masks, 3 + 2 * lev)
                dve.tensor_scalar(top[:], differ[:], LEVELS - 1 - lev, None, ALU.logical_shift_right).then_inc(masks, 1)
                dve.wait_ge(masks, 4 + 2 * lev)
                dve.scalar_tensor_tensor(mask[:, lev + 1], top[:], 1, after[:], ALU.is_equal, ALU.mult
                                         ).then_inc(masks, 1)
            dve.wait_ge(masks, 3 + 2 * LEVELS)
            dve.wait_ge(consts, 2)
            dve.wait_ge(cleared, 4)
            dve.wait_ge(bias_ready, len(DILATIONS) * HEADS)
            dve.wait_ge(gain_ready, 1)
            dve.engine_nop().then_inc(st_ready, 1)

            def stage_q(s, c):
                dve.wait_ge(q_turned[s], c + 1)
                dve.tensor_scalar(q_t[:, s], turn[:].rearrange("p (k c) -> p k c", k=4), gain[:], None,
                                  ALU.mult).then_inc(q_staged[s], 1)

            def attention(u, c, n4, at, prev, nxt, before):
                i, s = at[0], n4 % 2
                lo = 0 if prev else P
                for e in range(HEADS):
                    p, w = e % 2, u * 4 + e // 2
                    if e == 0 and (i < 2 or type(u) is int and u < 34):
                        dve.wait_ge(o_stored[s], c * 16)
                    elif e == 0:
                        dve.wait_ge(joined[s], c - 16)
                    dve.wait_ge(a_full[p], w + 1)
                    dve.wait_ge(pt_full[p], w)
                    dve.memset(a_gate[:, p:p + 1], 0.0)
                    dve.tensor_tensor_reduce(p_sb[:, p, lo:], score[:, p, lo:2 * P],
                                             bias[:, i * HEADS + e, lo:], -1.0, 3e38, ALU.add,
                                             ALU.min, o_sb[:, s, AW + e:AW + e + 1]
                                             ).then_inc(masked[p], 1)
                    if e == 4 and nxt is not None:
                        stage_q(1 - s, c + s)
                    if e % 2 == 1:
                        q = 0
                        dve.wait_ge(pt_full[q], w + 1)
                        dve.wait_ge(pv_done[q], w)
                        dve.tensor_copy(pt_sb[:, q, lo // P:], pt_of(q, lo)).then_inc(pt_read[q], 1)
                    yield

            def differences(u, s, lev):
                p, w = lev % 2, u * 4 + lev // 2
                dve.wait_ge(exped[p], w)
                if lev == LEVELS:
                    edge = b[:, s, :, C - 1:C].broadcast_to([P, HH, C])
                    dve.tensor_tensor(diff[:, p], edge, b[:, s], ALU.subtract).then_inc(diffed[p], 1)
                    return
                half = C >> (lev + 1)
                bb, dd = blocks_of(b[:, s], lev), blocks_of(diff[:, p], lev)
                edge = bb[:, :, 0, half - 1:half].broadcast_to([P, HH * C // half // 2, half])
                dve.tensor_tensor(dd[:, :, 1], bb[:, :, 1], edge, ALU.subtract).then_inc(diffed[p], 1)

            def scale_q(u, c, s, lev):
                p, w = lev % 2, u * 4 + lev // 2
                if lev == LEVELS:
                    dve.wait_ge(o_full[1 - s], c + s)
                    dve.wait_ge(b_exped, u + 1)
                    dve.tensor_tensor(q_dec[:, lev], q_in[:, s], b_exp[:], ALU.mult).then_inc(q_scaled, 1)
                    return
                dve.wait_ge(exped[p], w + 1)
                dve.wait_ge(s_full[(lev + 1) % 2], u * 4)
                o, i, e = (blocks_of(t, lev)[:, :, 1] for t in (q_dec[:, lev], q_in[:, s], decay[:, p]))
                dve.tensor_tensor(o, i, e, ALU.mult).then_inc(q_scaled, 1)

            def pick(u, c, s, j):
                if j == 0:
                    dve.wait_ge(o_full[s], c)
                else:
                    dve.wait_ge(s_read[(j - 1) % 2], u * 4 + (j - 1) // 2 + 1)
                dve.wait_ge(s_full[j % 2], u * 4 + j // 2 + 1)
                dve.memset(gate[:, j:j + 1], 0.0)
                m = mask[:, j:j + 1].broadcast_to([P, HH, C])
                dve.copy_predicated(s_sb[:, s], m, s_ps[:, j % 2].rearrange("p (h c) -> p h c", h=HH)
                                    ).then_inc(s_read[j % 2], 1)

            def recurrence(u, c, s):
                for at in range(STEPS):
                    if at == 1:
                        dve.wait_ge(logged, u + 1)
                        dve.tensor_tensor_scan(b[:, s].rearrange("p h c -> p (h c)"),
                                               restart[:].rearrange("p h c -> p (h c)"),
                                               f_in[:, s].rearrange("p h c -> p (h c)"), 0.0, ALU.mult, ALU.add
                                               ).then_inc(summed, 1)
                        dve.wait_ge(summed, u + 1)
                    if 0 <= at - 1 <= LEVELS:
                        differences(u, s, at - 1)
                    if 0 <= at - 3 <= LEVELS:
                        scale_q(u, c, s, at - 3)
                    if at == 3:
                        pick(u, c, s, 0)
                    if 1 <= at - 4 <= LEVELS:
                        pick(u, c, s, at - 4)
                    if at == 14:
                        dve.wait_ge(o_full[s], c + 1)
                        dve.wait_ge(last_exped, u + 1)
                        dve.wait_ge(st_full, u + 1)
                        for h in range(HH):
                            x = dve.scalar_tensor_tensor(state[:, h], state[:, h], last_exp[:, h:h + 1],
                                                         st_ps[:, h * C:(h + 1) * C], ALU.mult, ALU.add)
                        x.then_inc(st_ready, 1)
                        dve.wait_ge(squared, u + 1)
                        dve.tensor_reduce(ms[:, 0], squares[:], AX.X, ALU.add).then_inc(chain, 1)
                        dve.wait_ge(chain, u * 5 + 1)
                        dve.tensor_scalar(ms[:, 0], ms[:, 0], 1 / C, EPS, ALU.mult, ALU.add).then_inc(mean_ready, 1)
                    if at == 15:
                        dve.wait_ge(rstd0, u + 1)
                        newton(dve, chain, u * 5 + 1, ms[:, 2], ms[:, 0], ms[:, 3])
                        dve.wait_ge(gated_ready, u + 1)
                        dve.wait_ge(out_stored[s], c * 16)
                        for h in range(HH):
                            cols = slice(h * C, (h + 1) * C)
                            x = dve.scalar_tensor_tensor(out[:, s, cols], o_ps[:, cols], ms[:, 2, h:h + 1],
                                                         gated[:, s, cols], ALU.mult, ALU.mult)
                        x.then_inc(out_ready[s], 1)
                    yield

            def join(v, w, s):
                n = v * 6
                for at in range(HEADS):
                    if at == 2:
                        dve.wait_ge(others_landed[s], w * 32 + 32)
                        dve.wait_ge(o_read[s], w + 17)
                        dve.wait_ge(joined[s], w)
                        minus_max = [others[:, s, 0, AW:AW + HEADS], others[:, s, 1, AW:AW + HEADS],
                                     o_sb[:, s, AW:AW + HEADS]]
                        dve.tensor_tensor(least[:, s], minus_max[0], minus_max[1], ALU.min).then_inc(join_chain, 1)
                        dve.wait_ge(join_chain, n + 1)
                        dve.tensor_tensor(least[:, s], least[:, s], minus_max[2], ALU.min).then_inc(join_chain, 1)
                        dve.wait_ge(join_chain, n + 2)
                        for i in range(3):
                            x = dve.tensor_tensor(gap[:, s, i], least[:, s], minus_max[i], ALU.subtract)
                        x.then_inc(gap_ready, 1)
                    if at == 4:
                        dve.wait_ge(gap_exped, v + 1)
                        for i, t in enumerate((others[:, s, 0], others[:, s, 1], o_sb[:, s])):
                            x = dve.tensor_tensor(total[:, s, i], gap[:, s, i], t[:, AW + HEADS:OW], ALU.mult)
                        x.then_inc(join_chain, 1)
                        dve.wait_ge(join_chain, n + 3)
                        dve.tensor_reduce(norm[:, s], total[:, s].rearrange("p b h -> p h b"), AX.X, ALU.add
                                          ).then_inc(join_chain, 1)
                        dve.wait_ge(join_chain, n + 4)
                        dve.reciprocal(norm[:, s], norm[:, s]).then_inc(join_chain, 1)
                        dve.wait_ge(join_chain, n + 5)
                        dve.tensor_tensor(gap[:, s], gap[:, s], norm[:, s:s + 1].broadcast_to([P, 3, HEADS]), ALU.mult
                                          ).then_inc(shares_ready, 1)
                        dve.engine_nop().then_inc(join_chain, 1)
                    if at == 5:
                        dve.wait_ge(shares_ready, v + 1)
                        dve.tensor_tensor(scaled[:, s, 2].rearrange("p (h e) -> p h e", e=HD),
                                          o_sb[:, s, 0:AW].rearrange("p (h e) -> p h e", e=HD),
                                          gap[:, s, 2].unsqueeze(2).broadcast_to([P, HEADS, HD]), ALU.mult
                                          ).then_inc(own_scaled[s], 1)
                    if at == 7:
                        dve.wait_ge(own_scaled[s], w + 1)
                        dve.wait_ge(y_stored[s], w * 16)
                        dve.wait_ge(paired, v + 1)
                        dve.tensor_tensor(joined_sb[:, s], scaled[:, s, 0], scaled[:, s, 2], ALU.add).then_inc(joined[s], 1)
                    yield

            stage_q(0, 0)
            run(dve, attention, recurrence, join)

        @block.scalar
        def _(act):
            nc.scalar.preload_act_table_set("natural_log_exp_and_others")

            def stage_k(s, c):
                act.wait_ge(k_turned_a[s], c + 1)
                act.activation(k_t[:, s], turn[:].rearrange("p (k c) -> p k c", k=4), ACT.Copy
                               ).then_inc(k_staged[s], 1)

            def attention(u, c, n4, at, prev, nxt, before):
                i, d, r, n = at
                s = n4 % 2
                lo = 0 if prev else P
                for e in range(HEADS):
                    p, w = e % 2, u * 4 + e // 2
                    act.wait_ge(masked[p], w + 1)
                    act.activation(p_sb[:, p, lo:], p_sb[:, p, lo:], ACT.Exp, scale=-1.0,
                                   bias=o_sb[:, s, AW + e:AW + e + 1],
                                   accum_out=o_sb[:, s, AW + HEADS + e:AW + HEADS + e + 1]
                                   ).then_inc(weighed[p], 1)
                    if e == 6 and nxt is not None:
                        stage_k(1 - s, c + s)
                    if e % 2 == 0 and e:
                        stage_weights(u, e - 1, prev)
                    if e == 0 and before:
                        stage_weights(before[0], HEADS - 1, before[4])
                    if e == 1 and before:
                        read_sums(*before)
                    if e == 2 and before:
                        store(*before)
                    if e < HEADS - 1:
                        yield
                if n4 == 3:
                    stage_weights(u, HEADS - 1, prev)
                    read_sums(u, c, n4, at, prev)
                    store(u, c, n4, at, prev)
                yield

            def stage_weights(u, e, prev):
                lo, w = 0 if prev else P, u * 4 + e // 2
                act.wait_ge(pv_done[1], w)
                act.wait_ge(pt_full[1], w + 1)
                act.activation(pt_sb[:, 1, lo // P:], pt_of(1, lo), ACT.Copy).then_inc(pt_read[1], 1)

            def read_sums(u, c, n4, at, prev):
                act.wait_ge(pv_done[1], u * 4 + 4)
                act.activation(o_sb[:, n4 % 2, 0:AW], o_acc[:], ACT.Copy).then_inc(o_read[n4 % 2], 1)

            def store(u, c, n4, at, prev):
                i, d, r, n = at
                if i < 2:
                    act.wait_ge(o_read[n4 % 2], c + 1)
                    act.dma_start(rows(branch_rows[i], d, r, n, slice(0, OW)), o_sb[:, n4 % 2]
                                  ).then_inc(o_stored[n4 % 2], 16)

            def recurrence(u, c, s):
                for at in range(STEPS):
                    if at == 0:
                        act.wait_ge(in_landed[s], c * 48 + 48)
                        act.activation(f_in[:, s], f_in[:, s], ACT.Ln).then_inc(logged, 1)
                    if at == 1:
                        act.wait_ge(q_scaled, u * 8)
                        act.wait_ge(st_ready, u + 1)
                        act.wait_ge(summed, u + 1)
                        act.activation(b_exp[:], b[:, s], ACT.Exp).then_inc(b_exped, 1)
                        act.activation(last_exp[:], b[:, s, :, C - 1], ACT.Exp).then_inc(last_exped, 1)
                    lev = at - 2
                    if 0 <= lev <= LEVELS:
                        p, w = lev % 2, u * 4 + lev // 2
                        act.wait_ge(q_scaled, u * 8 + max(lev - 1, 0))
                        act.wait_ge(k_scaled, u * 8 + max(lev - 1, 0))
                        if lev < LEVELS:
                            act.wait_ge(k_diffed[p], u * (4 - p) + lev // 2 + 1)
                        act.wait_ge(diffed[p], w + 1)
                        act.activation(decay[:, p], diff[:, p], ACT.Exp).then_inc(exped[p], 1)
                    if at == 12:
                        act.wait_ge(st_full, u)
                        act.wait_ge(k_turned, u + 1)
                        act.activation(k_rows[:], st_ps.rearrange("p (h c) -> p h c", h=HH), ACT.Copy
                                       ).then_inc(k_rows_ready, 1)
                    if at == 13:
                        act.wait_ge(o_full[s], c + 1)
                        act.activation(squares[:], o_ps.rearrange("p (h c) -> p h c", h=HH), ACT.Square
                                       ).then_inc(squared, 1)
                    if at == 14:
                        act.wait_ge(mean_ready, u + 1)
                        act.activation(ms[:, 1], ms[:, 0], ACT.Ln).then_inc(ln_ready, 1)
                        act.wait_ge(ln_ready, u + 1)
                        act.activation(ms[:, 2], ms[:, 1], ACT.Exp, scale=-0.5).then_inc(rstd0, 1)
                    if at == 15:
                        act.wait_ge(out_ready[s], c + 1)
                        act.dma_start(y[bass.ds(u * C, C), AW:AW + HGW], out[:, s]).then_inc(out_stored[s], 16)
                    yield

            def join(v, w, s):
                for at in range(HEADS):
                    if at == 3:
                        act.wait_ge(gap_ready, v + 1)
                        act.activation(gap[:, s], gap[:, s], ACT.Exp).then_inc(gap_exped, 1)
                    if at == 7:
                        act.wait_ge(joined[s], w + 1)
                        act.dma_start(y[bass.ds(v * P, P), 0:AW], joined_sb[:, s]).then_inc(y_stored[s], 16)
                    yield

            stage_k(0, 0)
            run(act, attention, recurrence, join)

        @block.tensor
        def _(pe):
            def turn_rows(s, c, which):
                if which == 0:
                    pe.wait_ge(qk_landed[s], c * 16 + 16)
                    pe.wait_ge(k_staged[1 - s], c + s)
                else:
                    pe.wait_ge(q_staged[s], c + 1)
                for j in range(4):
                    at = (4 * which + j) * P
                    mm = pe.transpose(turn[:, j * P:(j + 1) * P], qk_in[:, s, at:at + P], ident[:])
                mm.then_inc((q_turned, k_turned_a)[which][s], 1)

            def scores(u, s, e, prev):
                p, w = e % 2, u * 4 + e // 2
                pe.wait_ge(masked[p], w)
                pair, base = e // 2, (e % 2) * HD
                at = slice(base, base + HD)
                for side in ((0, 1) if prev else (1,)):
                    k_slot = s if side else 1 - s
                    mm = pe.matmul(score[:, p, side * P:(side + 1) * P], q_t[at, s, pair], k_t[at, k_slot, pair],
                                   start=True, stop=True)
                mm.then_inc(a_full[p], 1)

            def transposes(u, e, prev):
                p, w = e % 2, u * 4 + e // 2
                pe.wait_ge(weighed[p], w + 1)
                pe.wait_ge(pt_read[p], w)
                for side in ((0, 1) if prev else (1,)):
                    cols = slice(side * P, (side + 1) * P)
                    mm = pe.transpose(pt[:, p, cols], p_sb[:, p, cols], ident[:])
                mm.then_inc(pt_full[p], 1)

            def sums(u, c, n4, e, prev):
                p, w, s = e % 2, u * 4 + e // 2, n4 % 2
                if e == 0:
                    pe.wait_ge(v_landed[s], c * 16 + 16)
                    pe.wait_ge(o_read[1 - s], c + s)
                pe.wait_ge(pt_read[p], w + 1)
                cols = slice(e * HD, (e + 1) * HD)
                for side in ((0, 1) if prev else (1,)):
                    mm = pe.matmul(o_acc[:, cols], pt_sb[:, p, side], v_in[:, n4 if side else (n4 - 1) % 4, cols],
                                   start=(side == 0 or not prev), stop=(side == 1))
                mm.then_inc(pv_done[p], 1)

            def attention(u, c, n4, at, prev, nxt, before):
                s = n4 % 2
                for e in range(HEADS):
                    transposes(u, e, prev)
                    if e < HEADS - 2:
                        scores(u, s, e + 2, prev)
                    elif nxt is not None:
                        if e == HEADS - 2:
                            pe.wait_ge(k_staged[1 - s], c + s + 1)
                        scores(u + 1, 1 - s, e + 2 - HEADS, nxt)
                    if e == 3 and nxt is not None:
                        turn_rows(1 - s, c + s, 0)
                    if e == 5 and nxt is not None:
                        turn_rows(1 - s, c + s, 1)
                    if e:
                        sums(u, c, n4, e - 1, prev)
                    elif before:
                        sums(*before[:3], HEADS - 1, before[4])
                    if e == HEADS - 1 and n4 == 3:
                        sums(u, c, n4, e, prev)
                    yield

            def recurrence(u, c, s):
                for at in range(STEPS):
                    j = 0 if at == 2 else at - 3 if 1 <= at - 3 <= LEVELS else None
                    if j is not None:
                        pe.wait_ge(s_read[j % 2], u * 4 + j // 2)
                        if j == 0:
                            pe.wait_ge(st_ready, u + 1)
                            pe.wait_ge(in_landed[s], c * 48 + 48)
                            kk, qq = k_in[:, s], q_in[:, s]
                        else:
                            if j == 1:
                                pe.wait_ge(out_ready[1 - s], c + s)
                            pe.wait_ge(q_scaled, u * 8 + j)
                            pe.wait_ge(k_scaled, u * 8 + j)
                            kk, qq = k_dec[:, j - 1], q_dec[:, j - 1]
                        for h in range(HH):
                            mm = pe.matmul(s_ps[:, j % 2, h * C:(h + 1) * C], kk[:, h], qq[:, h], start=True, stop=True)
                        mm.then_inc(s_full[j % 2], 1)
                    if at == 11:
                        pe.wait_ge(s_read[0], u * 4 + 4)
                        pe.wait_ge(k_scaled, u * 8 + 8)
                        for h in range(HH):
                            mm = pe.transpose(st_ps[:, h * C:(h + 1) * C], k_dec[:, LEVELS, h], ident[:])
                        mm.then_inc(k_turned, 1)
                    if at == 12:
                        pe.wait_ge(q_scaled, u * 8 + 8)
                        pe.wait_ge(s_read[1], u * 4 + 4)
                        pe.wait_ge(ig_landed[s], c * 16 + 16)
                        for h in range(HH):
                            cols = slice(h * C, (h + 1) * C)
                            pe.matmul(o_ps[:, cols], s_sb[:, s, h], ig_in[:, s, cols], start=True, stop=False)
                            mm = pe.matmul(o_ps[:, cols], q_dec[:, LEVELS, h], state[:, h], start=False, stop=True)
                        mm.then_inc(o_full[s], 1)
                    if at == 13:
                        pe.wait_ge(k_rows_ready, u + 1)
                        for h in range(HH):
                            cols = slice(h * C, (h + 1) * C)
                            mm = pe.matmul(st_ps[:, cols], k_rows[:, h], ig_in[:, s, cols], start=True, stop=True)
                        mm.then_inc(st_full, 1)
                    yield

            pe.wait_ge(cleared, 4)
            turn_rows(0, 0, 0)
            turn_rows(0, 0, 1)
            pe.wait_ge(k_staged[0], 1)
            scores(0, 0, 0, False)
            scores(0, 0, 1, False)
            run(pe, attention, recurrence, idle_blocks)


MEM, MH, MD = 256, 4, 256


def attend_memory(nc, qm, kvm, om, q_gain, k_gain, ident):
    name = "ma"
    M2 = MEM // P
    with nc.cleanup_on_exit(), ExitStack() as ctx:
        def sb(what, shape, dt=F32):
            return ctx.enter_context(nc.sbuf_tensor(f"{name}_{what}", shape, dt))

        def ps(what, shape):
            return ctx.enter_context(nc.psum_tensor(f"{name}_{what}", shape, F32))

        def sem(what):
            return nc.alloc_semaphore(f"{name}_{what}")

        gains = sb("gains", [P, 2, MD // P])
        gain = sb("gain", [P, MD // P])
        k_in = sb("k_in", [P, M2, D])
        v_in = sb("v_in", [P, M2, D])
        k_t = sb("k_t", [P, KT, MEM])
        q_in = sb("q_in", [P, 2, D])
        q_t = sb("q_t", [P, 2, KT, P])
        top = sb("top", [P, 2, MH])
        minus = sb("minus", [P, 2, MH])
        weight = sb("weight", [P, 2, MH])
        inverse = sb("inverse", [P, 2, MH])
        p_sb = sb("p", [P, 2, MEM])
        pt_sb = sb("pt_sb", [P, 2, M2, P])
        o_sb = sb("o", [P, 2, D])
        turn = ps("turn", [P, 2, BANK])
        score = ps("score", [P, 2, BANK])
        pt = ps("pt", [P, 2, BANK])
        o_ps = ps("o_ps", [P, 2, BANK])

        const_landed = sem("const_landed")
        gain_ready = sem("gain_ready")
        k_turned = sem("k_turned")
        k_ready = sem("k_ready")
        q_landed = [sem(f"q_landed{s}") for s in range(2)]
        q_turned = [sem(f"q_turned{i}") for i in range(2)]
        q_ready = [sem(f"q_ready{i}") for i in range(2)]
        s_full = [sem(f"s_full{p}") for p in range(2)]
        topped = [sem(f"topped{p}") for p in range(2)]
        minus_ready = [sem(f"minus_ready{p}") for p in range(2)]
        exped = [sem(f"exped{p}") for p in range(2)]
        inverted = [sem(f"inverted{p}") for p in range(2)]
        pt_full = [sem(f"pt_full{p}") for p in range(2)]
        pt_read = [sem(f"pt_read{p}") for p in range(2)]
        o_full = [sem(f"o_full{p}") for p in range(2)]
        o_read = [sem(f"o_read{p}") for p in range(2)]
        o_stored = [sem(f"o_stored{s}") for s in range(2)]
        block = ctx.enter_context(nc.Block())

        def each_tile(eng, body):
            last = SEQ // P // 2 - 1
            for s in range(2):
                body(s, 0, s, s == 1, True)
            with eng.Fori(1, last) as c:
                for s in range(2):
                    body(c * 2 + s, c, s, True, True)
            for s in range(2):
                body(last * 2 + s, last, s, True, s == 0)

        @block.sync
        def _(sp):
            for i, g in enumerate((q_gain, k_gain)):
                for t in range(MD // P):
                    sp.dma_start(gains[:, i, t:t + 1], g[t * P:(t + 1) * P, :]).then_inc(const_landed, 16)
            for m in range(M2):
                sp.dma_start(k_in[:, m], kvm[m * P:(m + 1) * P, 0:D]).then_inc(const_landed, 16)
                sp.dma_start(v_in[:, m], kvm[m * P:(m + 1) * P, D:2 * D]).then_inc(const_landed, 16)

            def body(u, c, s, before, more):
                sp.wait_ge(q_ready[1], u)
                sp.dma_start(q_in[:, s], qm[bass.ds(u * P, P), :]).then_inc(q_landed[s], 16)
            each_tile(sp, body)
            for s in range(2):
                sp.wait_ge(o_stored[s], 16 * 8)

        @block.vector
        def _(dve):
            dve.wait_ge(const_landed, 16 * (4 + 2 * M2))
            dve.scalar_tensor_tensor(gain[:], gains[:, 0], 1 / math.sqrt(MD), gains[:, 1], ALU.mult, ALU.mult
                                     ).then_inc(gain_ready, 1)
            dve.wait_ge(gain_ready, 1)
            for i in range(2 * M2):
                m, b = divmod(i, 2)
                dve.wait_ge(k_turned, i + 1)
                for j in range(4):
                    at = 4 * b + j
                    x = dve.tensor_scalar(k_t[:, at, m * P:(m + 1) * P], turn[:, b, j * P:(j + 1) * P],
                                          gain[:, at % 2:at % 2 + 1], None, ALU.mult)
                x.then_inc(k_ready, 1)

            def body(u, c, s, before, more):
                for e in range(MH):
                    p, w = e % 2, u * 2 + e // 2
                    if e == 0:
                        dve.wait_ge(o_stored[s], c * 16)
                    dve.wait_ge(s_full[p], w + 1)
                    dve.tensor_reduce(top[:, s, e:e + 1], score[:, p, 0:MEM], AX.X, ALU.max).then_inc(topped[p], 1)
                    dve.wait_ge(topped[p], w + 1)
                    dve.tensor_scalar(minus[:, s, e:e + 1], top[:, s, e:e + 1], -1.0, None, ALU.mult
                                      ).then_inc(minus_ready[p], 1)
                    if e or before:
                        stage_weights(*((u, s, e - 1) if e else (u - 1, 1 - s, MH - 1)))
                    if e >= 2 or before:
                        finish(*((u, s, e - 2) if e >= 2 else (u - 1, 1 - s, MH + e - 2)))
                if not more:
                    stage_weights(u, s, MH - 1)
                    finish(u, s, MH - 2)
                    finish(u, s, MH - 1)

            def stage_weights(u, s, e):
                p, w = e % 2, u * 2 + e // 2
                dve.wait_ge(exped[p], w + 1)
                dve.reciprocal(inverse[:, s, e:e + 1], weight[:, s, e:e + 1]).then_inc(inverted[p], 1)
                dve.wait_ge(o_full[p], w)
                dve.wait_ge(pt_full[p], w + 1)
                dve.tensor_copy(pt_sb[:, p], pt[:, p, 0:MEM].rearrange("p (k c) -> p k c", c=P)).then_inc(pt_read[p], 1)

            def finish(u, s, e):
                p, w = e % 2, u * 2 + e // 2
                dve.wait_ge(inverted[p], w + 1)
                dve.wait_ge(o_full[p], w + 1)
                dve.tensor_scalar(o_sb[:, s, e * MD:(e + 1) * MD], o_ps[:, p, 0:MD], inverse[:, s, e:e + 1], None,
                                  ALU.mult).then_inc(o_read[p], 1)

            each_tile(dve, body)

        @block.scalar
        def _(act):
            nc.scalar.preload_act_table_set("natural_log_exp_and_others")

            def stage_q(u, s, i):
                act.wait_ge(q_turned[i], u + 1)
                act.activation(q_t[:, s, 4 * i:4 * i + 4], turn[:, i].rearrange("p (k c) -> p k c", k=4), ACT.Copy
                               ).then_inc(q_ready[i], 1)

            def body(u, c, s, before, more):
                for e in range(MH):
                    p, w = e % 2, u * 2 + e // 2
                    act.wait_ge(minus_ready[p], w + 1)
                    act.wait_ge(pt_full[p], w)
                    act.activation(p_sb[:, p], score[:, p, 0:MEM], ACT.Exp, bias=minus[:, s, e:e + 1],
                                   accum_out=weight[:, s, e:e + 1]).then_inc(exped[p], 1)
                    if more and e < 2:
                        stage_q(u + 1, 1 - s, e)
                    if e == 2 and before:
                        store(u - 1, 1 - s)
                if not more:
                    store(u, s)

            def store(u, s):
                for p in range(2):
                    act.wait_ge(o_read[p], u * 2 + 2)
                act.dma_start(om[bass.ds(u * P, P), :], o_sb[:, s]).then_inc(o_stored[s], 16)

            stage_q(0, 0, 0)
            stage_q(0, 0, 1)
            each_tile(act, body)

        @block.tensor
        def _(pe):
            pe.wait_ge(const_landed, 16 * (4 + 2 * M2))
            for i in range(2 * M2):
                m, b = divmod(i, 2)
                if i >= 2:
                    pe.wait_ge(k_ready, i - 1)
                for j in range(4):
                    at = (4 * b + j) * P
                    mm = pe.transpose(turn[:, b, j * P:(j + 1) * P], k_in[:, m, at:at + P], ident[:])
                mm.then_inc(k_turned, 1)
            pe.wait_ge(k_ready, 2 * M2)

            def turn_q(u, c, s, i):
                if i == 0:
                    pe.wait_ge(q_landed[s], c * 16 + 16)
                pe.wait_ge(q_ready[i], u)
                for j in range(4):
                    at = (4 * i + j) * P
                    mm = pe.transpose(turn[:, i, j * P:(j + 1) * P], q_in[:, s, at:at + P], ident[:])
                mm.then_inc(q_turned[i], 1)

            def scores(u, s, e):
                p, w = e % 2, u * 2 + e // 2
                if e % 2 == 0:
                    pe.wait_ge(q_ready[e // 2], u + 1)
                pe.wait_ge(exped[p], w)
                for i in range(MD // P):
                    at = e * (MD // P) + i
                    mm = pe.matmul(score[:, p, 0:MEM], q_t[:, s, at], k_t[:, at], start=(i == 0), stop=(i == 1))
                mm.then_inc(s_full[p], 1)

            def transposes(u, e):
                p, w = e % 2, u * 2 + e // 2
                pe.wait_ge(exped[p], w + 1)
                pe.wait_ge(pt_read[p], w)
                for m in range(M2):
                    mm = pe.transpose(pt[:, p, m * P:(m + 1) * P], p_sb[:, p, m * P:(m + 1) * P], ident[:])
                mm.then_inc(pt_full[p], 1)

            def sums(u, e):
                p, w = e % 2, u * 2 + e // 2
                pe.wait_ge(pt_read[p], w + 1)
                pe.wait_ge(o_read[p], w)
                for m in range(M2):
                    mm = pe.matmul(o_ps[:, p, 0:MD], pt_sb[:, p, m], v_in[:, m, e * MD:(e + 1) * MD],
                                   start=(m == 0), stop=(m == M2 - 1))
                mm.then_inc(o_full[p], 1)

            def body(u, c, s, before, more):
                for e in range(MH):
                    if more and e < 2:
                        turn_q(u + 1, c + s, 1 - s, e)
                    transposes(u, e)
                    if e + 2 < MH:
                        scores(u, s, e + 2)
                    elif more:
                        scores(u + 1, 1 - s, e + 2 - MH)
                    if e or before:
                        sums(*((u, e - 1) if e else (u - 1, MH - 1)))
                if not more:
                    sums(u, MH - 1)

            turn_q(0, 0, 0, 0)
            turn_q(0, 0, 0, 1)
            scores(0, 0, 0)
            scores(0, 0, 1)
            each_tile(pe, body)


def feed_forward(nc, src, gain, w1, w2, dst, ident):
    name = "ff"
    S = src.shape[0]
    T = BANK
    groups, tiles = S // T, T // P
    QUARTERS = w1.shape[1] // D
    PER = 4
    with nc.cleanup_on_exit(), ExitStack() as ctx:
        def sb(what, shape, dt=F32):
            return ctx.enter_context(nc.sbuf_tensor(f"{name}_{what}", shape, dt))

        def ps(what, shape):
            return ctx.enter_context(nc.psum_tensor(f"{name}_{what}", shape, F32))

        def sem(what):
            return nc.alloc_semaphore(f"{name}_{what}")

        x_in = sb("x_in", [P, tiles, D])
        junk = sb("junk", [P, D])
        sumsq = sb("sumsq", [P, 2])
        root = sb("root", [P, 2])
        scratch = sb("scratch", [P, 2])
        eps = sb("eps", [P, 1])
        rstd = sb("rstd", [P, 2])
        h = sb("h", [P, 2, D])
        g_rep = sb("g_rep", [P, D])
        a_hi = [sb(f"a_hi{s}", [P, KT, T], F32R) for s in range(2)]
        a_lo = [sb(f"a_lo{s}", [P, KT, T], F32R) for s in range(2)]
        raw = sb("raw", [P, 2, HK, BANK])
        w_hi = sb("w_hi", [P, 2, HK, BANK], F32R)
        w_lo = sb("w_lo", [P, 2, HK, BANK], F32R)
        relu = sb("relu", [P, 2, BANK])
        square_sb = sb("square", [P, 2, BANK])
        u_hi = sb("u_hi", [P, KT, T], F32R)
        u_lo = sb("u_lo", [P, KT, T], F32R)
        total = sb("total", [P, tiles, D])
        acc = ps("acc", [P, 4, BANK])
        turn = ps("turn", [P, 2, BANK])

        eps_ready = sem("eps_ready")
        gain_landed = sem("gain_landed")
        gain_ready = sem("gain_ready")
        x_landed = [sem(f"x_landed{t}") for t in range(tiles)]
        sumsq_ready = sem("sumsq_ready")
        root_ready = sem("root_ready")
        rstd_chain = sem("rstd_chain")
        rstd_ready = sem("rstd_ready")
        h_ready = sem("h_ready")
        turned = sem("turned")
        a_hi_ready = sem("a_hi_ready")
        a_ready = sem("a_ready")
        raw_landed = [sem(f"raw_landed{s}") for s in range(2)]
        w_hi_ready = [sem(f"w_hi_ready{s}") for s in range(2)]
        w_ready = [sem(f"w_ready{s}") for s in range(2)]
        first_half_used = sem("first_half_used")
        acc_full = [sem(f"acc_full{t}") for t in range(tiles)]
        acc_read = [sem(f"acc_read{t}") for t in range(tiles)]
        squared = [sem(f"squared{s}") for s in range(2)]
        u_hi_ready = [sem(f"u_hi_ready{s}") for s in range(2)]
        u_ready = sem("u_ready")
        total_landed = sem("total_landed")
        stored = sem("stored")
        block = ctx.enter_context(nc.Block())

        src_tiles = src.rearrange("(n p) d -> n p d", p=P)
        w1_rows = w1.rearrange("(h k p) c -> h p k c", k=HK, p=P)

        def each_quarter(eng, g, body):
            with eng.Fori(0, QUARTERS - 1) as q:
                body(q, q + g * QUARTERS, False)
            body(QUARTERS - 1, (g + 1) * QUARTERS - 1, True)

        def prepares(g, last, i):
            return last and g + 1 < groups and i >= PER - 2

        @block.sync
        def _(sp):
            def load_rows(n):
                if n >= tiles:
                    sp.wait_ge(h_ready, n - tiles + 1)
                sp.dma_start(x_in[:, n % tiles, :], src_tiles[n]).then_inc(x_landed[n % tiles], 16)

            def quarter(g):
                def body(q, n, last):
                    for i in range(PER):
                        for half in range(2):
                            sp.wait_ge(w_ready[half], n * PER + i)
                            if i < 2:
                                w = w1_rows[half, :, :, bass.ds(q * D + i * BANK, BANK)]
                            else:
                                w = w2[bass.ds(q * D + half * BANK, BANK), (i - 2) * BANK:(i - 1) * BANK
                                       ].rearrange("(k p) c -> p k c", p=P)
                            sp.dma_start(raw[:, half], w).then_inc(raw_landed[half], 16)
                        if prepares(g, last, i + 1) and i == PER - 3:
                            for t in range(tiles):
                                load_rows((g + 1) * tiles + t)
                return body

            for t in range(tiles):
                load_rows(t)
                if t == 0:
                    sp.dma_start(g_rep[:], gain.broadcast_to([P, D])).then_inc(gain_landed, 16)
            for g in range(groups):
                each_quarter(sp, g, quarter(g))
            sp.wait_ge(stored, groups * tiles * 16)

        @block.gpsimd
        def _(pool):
            def body(q, n, last):
                for i in range(PER):
                    for half in range(2):
                        m = n * PER + i
                        pool.wait_ge(w_hi_ready[half], m + 1)
                        pool.tensor_tensor(w_lo[:, half], raw[:, half], w_hi[:, half].bitcast(F32), ALU.subtract
                                           ).then_inc(w_ready[half], 1)
            for g in range(groups):
                each_quarter(pool, g, body)

        @block.scalar
        def _(act):
            def square(n):
                act.wait_ge(x_landed[n % tiles], 16 * (n // tiles + 1))
                if n >= 1:
                    act.wait_ge(sumsq_ready, n)
                if n >= 2:
                    act.wait_ge(rstd_ready, n - 1)
                at = slice(n % 2, n % 2 + 1)
                act.activation(junk[:], x_in[:, n % tiles, :], ACT.Square, accum_out=sumsq[:, at]
                               ).then_inc(sumsq_ready, 1)
                act.wait_ge(sumsq_ready, n + 1)
                act.activation(root[:, at], sumsq[:, at], ACT.Sqrt, bias=eps[:]).then_inc(root_ready, 1)

            def high_part(n, b):
                act.wait_ge(turned, 2 * n + b + 1)
                g, t = divmod(n, tiles)
                act.activation(a_hi[g % 2][:, b * HK:(b + 1) * HK, t * P:(t + 1) * P],
                               turn[:, b].rearrange("p (k c) -> p k c", k=HK), ACT.Copy
                               ).then_inc(a_hi_ready, 1)

            def high_square(n, i, t):
                s, m = t % 2, n * 4 + i * 2 + t // 2
                act.wait_ge(squared[s], m + 1)
                act.activation(u_hi[:, i * tiles + t], square_sb[:, s], ACT.Copy).then_inc(u_hi_ready[s], 1)

            def quarter(g):
                def body(q, n, last):
                    for i in range(PER):
                        for step in range(2 * tiles):
                            if prepares(g, last, i):
                                beside = (i - PER + 2) * 2 * tiles + step
                                for j in BESIDE_TWO["square"].get(beside, []):
                                    square((g + 1) * tiles + j)
                                for j in BESIDE_TWO["turn"].get(beside, []):
                                    high_part((g + 1) * tiles + j // 2, j % 2)
                            t = step - tiles
                            if t < 0 or i >= 2:
                                continue
                            m = n * 4 + i * 2 + t // 2
                            act.wait_ge(acc_full[t], n * PER + i + 1)
                            act.wait_ge(squared[t % 2], m)
                            act.activation(relu[:, t % 2], acc[:, t], ACT.Relu).then_inc(acc_read[t], 1)
                            if t:
                                high_square(n, i, t - 1)
                        if i < 2:
                            high_square(n, i, tiles - 1)
                    if last:
                        for t in range(tiles):
                            act.wait_ge(acc_read[t], (n + 1) * PER)
                            act.dma_start(dst[(g * tiles + t) * P:(g * tiles + t + 1) * P, :], total[:, t]
                                          ).then_inc(stored, 16)
                return body

            act.wait_ge(eps_ready, 1)
            for n in range(tiles):
                if n == 0:
                    square(0)
                if n + 1 < tiles:
                    square(n + 1)
                high_part(n, 0)
                high_part(n, 1)
            for g in range(groups):
                act.wait_ge(stored, g * tiles * 16)
                for t in range(tiles):
                    act.dma_start(total[:, t], src_tiles[g * tiles + t]).then_inc(total_landed, 16)
                each_quarter(act, g, quarter(g))

        @block.vector
        def _(dve):
            dve.memset(eps[:], D * EPS).then_inc(eps_ready, 1)
            dve.wait_ge(gain_landed, 16)
            dve.tensor_scalar(g_rep[:], g_rep[:], math.sqrt(D), None, ALU.mult).then_inc(gain_ready, 1)
            dve.wait_ge(gain_ready, 1)

            def normalise(n):
                if n >= 2:
                    dve.wait_ge(turned, 2 * (n - 1))
                s = slice(n % 2, n % 2 + 1)
                dve.wait_ge(root_ready, n + 1)
                dve.tensor_scalar(sumsq[:, s], sumsq[:, s], D * EPS, None, ALU.add).then_inc(rstd_chain, 1)
                dve.reciprocal(rstd[:, s], root[:, s]).then_inc(rstd_chain, 1)
                dve.wait_ge(rstd_chain, n * 6 + 2)
                newton(dve, rstd_chain, n * 6 + 2, rstd[:, s], sumsq[:, s], scratch[:, s])
                dve.engine_nop().then_inc(rstd_ready, 1)
                dve.wait_ge(rstd_ready, n + 1)
                dve.scalar_tensor_tensor(h[:, n % 2], x_in[:, n % tiles], rstd[:, s], g_rep[:],
                                         ALU.mult, ALU.mult).then_inc(h_ready, 1)

            def low_part(n, b):
                dve.wait_ge(a_hi_ready, 2 * n + b + 1)
                g, t = divmod(n, tiles)
                at = (slice(None), slice(b * HK, (b + 1) * HK), slice(t * P, (t + 1) * P))
                dve.tensor_tensor(a_lo[g % 2][at], turn[:, b].rearrange("p (k c) -> p k c", k=HK),
                                  a_hi[g % 2].bitcast(F32)[at], ALU.subtract).then_inc(a_ready, 1)

            def split_weights(m, half):
                dve.wait_ge(raw_landed[half], m * 16 + 16)
                dve.wait_ge(acc_full[tiles - 1] if half else first_half_used, m)
                dve.tensor_copy(w_hi[:, half], raw[:, half]).then_inc(w_hi_ready[half], 1)

            def low_square(n, i, t):
                s, m = t % 2, n * 4 + i * 2 + t // 2
                dve.wait_ge(u_hi_ready[s], m + 1)
                dve.tensor_tensor(u_lo[:, i * tiles + t], square_sb[:, s], u_hi[:, i * tiles + t].bitcast(F32),
                                  ALU.subtract).then_inc(u_ready, 1)

            def quarter(g):
                def body(q, n, last):
                    for i in range(PER):
                        c = n * PER + i
                        for step in range(2 * tiles):
                            if step == 0:
                                split_weights(c, 1)
                            elif step == tiles and not (last and g + 1 == groups and i == PER - 1):
                                split_weights(c + 1, 0)
                            if prepares(g, last, i):
                                beside = (i - PER + 2) * 2 * tiles + step
                                for j in BESIDE_TWO["normalise"].get(beside, []):
                                    normalise((g + 1) * tiles + j)
                                for j in BESIDE_TWO["turn"].get(beside, []):
                                    low_part((g + 1) * tiles + j // 2, j % 2)
                            t = step - tiles
                            if t < 0:
                                continue
                            if i < 2:
                                m = n * 4 + i * 2 + t // 2
                                dve.wait_ge(acc_read[t], c + 1)
                                dve.wait_ge(u_ready, n * 2 * tiles + i * tiles + max(t - 1, 0))
                                dve.tensor_tensor(square_sb[:, t % 2], relu[:, t % 2], relu[:, t % 2], ALU.mult
                                                  ).then_inc(squared[t % 2], 1)
                                if t:
                                    low_square(n, i, t - 1)
                            else:
                                dve.wait_ge(acc_full[t], c + 1)
                                dve.wait_ge(total_landed, (g + 1) * tiles * 16)
                                at = (slice(None), t, slice((i - 2) * BANK, (i - 1) * BANK))
                                dve.tensor_tensor(total[at], acc[:, t], total[at], ALU.add).then_inc(acc_read[t], 1)
                        if i < 2:
                            low_square(n, i, tiles - 1)
                return body

            for n in range(tiles):
                if n == 0:
                    normalise(0)
                if n + 1 < tiles:
                    normalise(n + 1)
                low_part(n, 0)
                low_part(n, 1)
                if n == 1:
                    split_weights(0, 0)
            for g in range(groups):
                each_quarter(dve, g, quarter(g))

        @block.tensor
        def _(pe):
            def turn_rows(n, b):
                pe.wait_ge(h_ready, n + 1)
                if n >= 1:
                    pe.wait_ge(a_ready, 2 * (n - 1) + b + 1)
                for k in range(HK):
                    at = (b * HK + k) * P
                    mm = pe.transpose(turn[:, b, k * P:(k + 1) * P], h[:, n % 2, at:at + P], ident[:])
                mm.then_inc(turned, 1)

            def products(i, s, half, t, n):
                cut = slice(t * P, (t + 1) * P)
                for k in range(HK):
                    a = half * HK + k
                    if i < 2:
                        terms = [(w_hi[:, half, k, cut], a_hi[s][:, a]), (w_hi[:, half, k, cut], a_lo[s][:, a]),
                                 (w_lo[:, half, k, cut], a_hi[s][:, a])]
                    else:
                        if t == 0:
                            pe.wait_ge(u_ready, n * 2 * tiles + a + 1)
                        terms = [(u_hi[:, a, cut], w_hi[:, half, k]), (u_hi[:, a, cut], w_lo[:, half, k]),
                                 (u_lo[:, a, cut], w_hi[:, half, k])]
                    for j, (left, right) in enumerate(terms):
                        mm = pe.matmul(acc[:, t], left, right, start=(half == 0 and k == 0 and j == 0),
                                       stop=(half == 1 and k == HK - 1 and j == 2))
                return mm

            def quarter(g):
                def body(q, n, last):
                    for i in range(PER):
                        c = n * PER + i
                        for half in range(2):
                            pe.wait_ge(w_ready[half], c + 1)
                            for t in range(tiles):
                                if prepares(g, last, i):
                                    for j in BESIDE_TWO["turn"].get((i - PER + 2) * 2 * tiles + half * tiles + t, []):
                                        turn_rows((g + 1) * tiles + j // 2, j % 2)
                                if half == 0:
                                    pe.wait_ge(acc_read[t], c)
                                mm = products(i, g % 2, half, t, n)
                                if half == 1:
                                    mm.then_inc(acc_full[t], 1)
                                elif t == tiles - 1:
                                    mm.then_inc(first_half_used, 1)
                return body

            for n in range(tiles):
                turn_rows(n, 0)
                turn_rows(n, 1)
            for g in range(groups):
                pe.wait_ge(a_ready, 2 * (g + 1) * tiles)
                each_quarter(pe, g, quarter(g))


def decoder_layer(nc, x, mem, norm1_g, w_in, attn_qn_g, attn_kn_g, hg_lb, hg_onorm_g, w_out, norm2_g, mem_norm_g,
                  w_mq, w_mkv, mq_norm_g, mk_norm_g, w_mo, norm3_g, w_ff1, w_ff2, out):
    S = x.shape[0]
    groups = S // BANK

    def scratch(what, rows, cols):
        return nc.dram_tensor(what, [rows, cols], F32, kind="Internal").ap()

    z_rows = scratch("z_rows", S, 2560)
    z_columns = scratch("z_columns", 1536, S)
    branch_rows = [scratch(f"branch{b}", S, 528) for b in range(2)]
    y = scratch("y", S, D)
    x1 = scratch("x1", S, D)
    kvm = scratch("kvm", MEM, 2 * D)
    qm = scratch("qm", S, D)
    om = scratch("om", S, D)
    x2 = scratch("x2", S, D)

    with nc.cleanup_on_exit(), ExitStack() as ctx:
        ident = ctx.enter_context(nc.sbuf_tensor("ident", [P, P], F32))
        lb = ctx.enter_context(nc.sbuf_tensor("lb", [P, 4], F32))
        lb_exp = ctx.enter_context(nc.sbuf_tensor("lb_exp", [P, 4], F32))
        lb_p = ctx.enter_context(nc.sbuf_tensor("lb_p", [P, 4], F32))
        lower = ctx.enter_context(nc.sbuf_tensor("lower", [P, 4], F32))
        upper = ctx.enter_context(nc.sbuf_tensor("upper", [P, 4], F32))
        cleared = nc.alloc_semaphore("ident_cleared")
        ident_ready = nc.alloc_semaphore("ident_ready")
        lb_landed = nc.alloc_semaphore("lb_landed")
        lb_chain = nc.alloc_semaphore("lb_chain")
        lb_exped = nc.alloc_semaphore("lb_exped")
        with nc.Block() as block:
            @block.sync
            def _(sp):
                for t in range(4):
                    sp.dma_start(lb[:, t:t + 1], hg_lb[t * P:(t + 1) * P, :]).then_inc(lb_landed, 16)

            @block.gpsimd
            def _(pool):
                pool.memset(ident[:], 0.0).then_inc(cleared, 1)
                pool.wait_ge(cleared, 1)
                pool.affine_select(out=ident[:], in_=ident[:], compare_op=ALU.not_equal, fill=1.0, base=0,
                                   pattern=[[-1, P]], channel_multiplier=1).then_inc(ident_ready, 1)

            @block.vector
            def _(dve):
                dve.wait_ge(lb_landed, 64)
                dve.tensor_tensor(lb_exp[:], lb[:], lb[:], ALU.subtract).then_inc(lb_chain, 1)
                dve.wait_ge(lb_exped, 1)
                dve.reciprocal(lb_p[:], lb_exp[:]).then_inc(lb_chain, 1)
                dve.wait_ge(lb_chain, 2)
                dve.tensor_tensor(lb_p[:], lb_p[:], lb_exp[:], ALU.mult).then_inc(lb_chain, 1)
                dve.wait_ge(lb_chain, 3)
                dve.tensor_tensor(lower[:], lb_p[:], lb_p[:], ALU.subtract).then_inc(lb_chain, 1)
                dve.wait_ge(lb_chain, 4)
                dve.tensor_scalar(upper[:], lower[:], -1.0, 1.0, ALU.mult, ALU.add).then_inc(lb_chain, 1)

            @block.scalar
            def _(act):
                act.wait_ge(lb_chain, 1)
                act.activation(lb_exp[:], lb_exp[:], ACT.Exp).then_inc(lb_exped, 1)

        project(nc, "in", [(x, norm1_g, w_in,
                            [("heads 64", 0, 2, z_rows, 0), ("rows", 2, 1, z_rows, 2),
                             ("silu columns", 3, 1, z_columns, 0),
                             ("gates", 4, 1, (z_columns[BANK:2 * BANK], z_columns[2 * BANK:3 * BANK]), 0),
                             ("rows", 5, 1, z_rows, 3), ("silu rows", 6, 1, z_rows, 4)], None)],
                groups, 4, ident, lower=(lower, upper))
        mix(nc, z_rows, z_columns, branch_rows, y, attn_qn_g, attn_kn_g, hg_onorm_g, ident)
        project(nc, "mkv", [(mem, mem_norm_g, w_mkv, [("heads 256", 0, 2, kvm, 0), ("rows", 2, 2, kvm, 2)], None)],
                1, 2, ident)
        project(nc, "out", [(y, None, w_out, [("rows", 0, 2, x1, 0)], x),
                            (x1, norm2_g, w_mq, [("heads 256", 0, 2, qm, 0)], None)], groups, 4, ident)
        attend_memory(nc, qm, kvm, om, mq_norm_g, mk_norm_g, ident)
        project(nc, "mo", [(om, None, w_mo, [("rows", 0, 2, x2, 0)], x1)], groups, 4, ident)
        feed_forward(nc, x2, norm3_g, w_ff1, w_ff2, out, ident)


_SHAPES = {
    "x": (2048, 1024), "mem": (256, 1024), "norm1_g": (1, 1024), "w_in": (1024, 3584), "attn_qn_g": (64, 1),
    "attn_kn_g": (64, 1), "hg_lb": (512, 1), "hg_onorm_g": (1, 512), "w_out": (1024, 1024), "norm2_g": (1, 1024),
    "mem_norm_g": (1, 1024), "w_mq": (1024, 1024), "w_mkv": (1024, 2048), "mq_norm_g": (256, 1),
    "mk_norm_g": (256, 1), "w_mo": (1024, 1024), "norm3_g": (1, 1024), "w_ff1": (1024, 4096), "w_ff2": (4096, 1024),
}


def kernel(**inputs):
    import numpy as _np
    import concourse.bacc as _bacc
    from concourse import mybir as _mybir
    from concourse.bass_utils import run_bass_kernel_spmd as _run

    nc = _bacc.Bacc("TRN2", target_bir_lowering=False, num_devices=1)
    arrays, args = {}, []
    for name, shape in _SHAPES.items():
        a = _np.ascontiguousarray(inputs[name]).reshape(shape)
        arrays[f"in_{name}"] = a
        args.append(nc.dram_tensor(f"in_{name}", shape, _mybir.dt.from_np(a.dtype), kind="ExternalInput").ap())
    args.append(nc.dram_tensor("out_0", (2048, 1024), F32, kind="ExternalOutput").ap())
    decoder_layer(nc, *args)
    r = _run(nc, [arrays], core_ids=[0])
    return r.results[0]["out_0"].reshape(1, 2048, 1024)
```
